# Optimizing a Trainium2 kernel written in Bass

```python
import jax, jax.numpy as jnp
from jax import lax
import numpy as np

D_MODEL = 1024
BATCH = 1
SEQ = 256
DEPTH = 1

GRID_W = 64
CTX_LEN = 256
MLA_HEADS = 8
MLA_NOPE = 64
MLA_ROPE = 32
MLA_QK = MLA_NOPE + MLA_ROPE
MLA_V = 64
Q_LORA = 384
KV_LORA = 256
NA_HEADS = 8
NA_DIM = 64
NA_WIN_H = 8
NA_WIN_W = 16
MIX_WIDTH = MLA_HEADS * MLA_V + NA_HEADS * NA_DIM
Q_COLS = Q_LORA + NA_HEADS * NA_DIM
KV_COLS = KV_LORA + MLA_ROPE + 2 * NA_HEADS * NA_DIM
N_GROUPS = 4
EXPERTS_PER_GROUP = 4
N_EXPERTS = N_GROUPS * EXPERTS_PER_GROUP
TOP_K_IN_GROUP = 2
D_EXPERT = 512
Q_BLOCK = 128
ROPE_THETA = 10000.0
NORM_EPS = 1e-6
MASK_VALUE = -1e30


def rmsnorm(x, g):
    xf = x.astype(jnp.float32)
    y = xf * lax.rsqrt(jnp.mean(xf * xf, axis=-1, keepdims=True) + NORM_EPS)
    return (y * g.astype(jnp.float32)).astype(x.dtype)

def adaln(cond, w_mod, b_mod):
    return jnp.split(jax.nn.silu(cond) @ w_mod + b_mod, 6, axis=-1)

def modulate(h, shift, scale):
    return h * (1 + scale) + shift

def axial_rope_tables(row, col, dtype):
    half = MLA_ROPE // 2
    inv_freq = ROPE_THETA ** (-jnp.arange(0, half, 2, dtype=jnp.float32) / half)
    ang = jnp.concatenate([row.astype(jnp.float32)[:, None] * inv_freq,
                           col.astype(jnp.float32)[:, None] * inv_freq], axis=-1)
    return jnp.cos(ang).astype(dtype), jnp.sin(ang).astype(dtype)

def apply_rope(x, cos, sin):
    x1, x2 = jnp.split(x, 2, axis=-1)
    c, s = cos[:, None, :], sin[:, None, :]
    return jnp.concatenate([x1 * c - x2 * s, x1 * s + x2 * c], axis=-1)

def mixer_queries(pq, q_a_g, w_uq):
    B, L, _ = pq.shape
    q_lat, na_q = jnp.split(pq, [Q_LORA], axis=-1)
    q_mla = (rmsnorm(q_lat, q_a_g) @ w_uq).reshape(B, L, MLA_HEADS, MLA_QK)
    return q_mla, na_q.reshape(B, L, NA_HEADS, NA_DIM)

def mixer_keys_values(pkv, kv_a_g, w_ukv):
    B, L, _ = pkv.shape
    kv_lat, k_rope, na_k, na_v = jnp.split(
        pkv, [KV_LORA, KV_LORA + MLA_ROPE, KV_LORA + MLA_ROPE + NA_HEADS * NA_DIM], axis=-1)
    kv = (rmsnorm(kv_lat, kv_a_g) @ w_ukv).reshape(B, L, MLA_HEADS, MLA_NOPE + MLA_V)
    k_nope, v_mla = jnp.split(kv, [MLA_NOPE], axis=-1)
    return (k_nope, k_rope, v_mla,
            na_k.reshape(B, L, NA_HEADS, NA_DIM), na_v.reshape(B, L, NA_HEADS, NA_DIM))

def mla_keys(k_nope, k_rope_b):
    return jnp.concatenate([k_nope, jnp.broadcast_to(k_rope_b, k_nope.shape[:3] + (MLA_ROPE,))], axis=-1)

def dense_attention(q, k, v):
    s = jnp.einsum('bqhd,bkhd->bhqk', q, k).astype(jnp.float32) * (q.shape[-1] ** -0.5)
    p = jax.nn.softmax(s, axis=-1).astype(v.dtype)
    return jnp.einsum('bhqk,bkhd->bqhd', p, v)

def mla_latent_attention(q, k, v, k_ctx, v_ctx):
    B, N, H, Dq = q.shape
    k_all = jnp.concatenate([k_ctx, k], axis=1)
    v_all = jnp.concatenate([v_ctx, v], axis=1)
    q_blocks = jnp.moveaxis(q.reshape(B, N // Q_BLOCK, Q_BLOCK, H, Dq), 1, 0)
    out = lax.map(lambda qb: dense_attention(qb, k_all, v_all), q_blocks)
    return jnp.moveaxis(out, 0, 1).reshape(B, N, H, v.shape[-1])

def neighbourhood_attention(q, k, v, k_ctx, v_ctx, rel_bias):
    B, N, H, Dh = q.shape
    rows = N // GRID_W
    kh = min(NA_WIN_H, rows)
    kw = NA_WIN_W
    scale = Dh ** -0.5
    qg = jnp.moveaxis(q.reshape(B, rows, GRID_W, H, Dh), 1, 0)
    kg = k.reshape(B, rows, GRID_W, H, Dh)
    vg = v.reshape(B, rows, GRID_W, H, Dh)
    col = jnp.arange(GRID_W)
    col_start = jnp.clip(col - kw // 2, 0, GRID_W - kw)
    col_in = (col[None, :] >= col_start[:, None]) & (col[None, :] < col_start[:, None] + kw)
    bias_cols = rel_bias[:, :, col[None, :] - col[:, None] + (NA_WIN_W - 1)]

    def one_row(args):
        r, qr = args
        start = jnp.clip(r - kh // 2, 0, rows - kh)
        kr = lax.dynamic_slice_in_dim(kg, start, kh, axis=1)
        vr = lax.dynamic_slice_in_dim(vg, start, kh, axis=1)
        bias = bias_cols[:, start + jnp.arange(kh) - r + (NA_WIN_H - 1)]
        s = jnp.einsum('bqhd,bjkhd->bhqjk', qr, kr).astype(jnp.float32) * scale
        s = s + jnp.transpose(bias, (0, 2, 1, 3)).astype(jnp.float32)[None]
        s = jnp.where(col_in[None, None, :, None, :], s, MASK_VALUE).reshape(B, H, GRID_W, kh * GRID_W)
        s_ctx = jnp.einsum('bqhd,bchd->bhqc', qr, k_ctx).astype(jnp.float32) * scale
        p = jax.nn.softmax(jnp.concatenate([s, s_ctx], axis=-1), axis=-1).astype(v.dtype)
        p_win = p[..., :kh * GRID_W].reshape(B, H, GRID_W, kh, GRID_W)
        p_ctx = p[..., kh * GRID_W:]
        return (jnp.einsum('bhqjk,bjkhd->bqhd', p_win, vr)
                + jnp.einsum('bhqc,bchd->bqhd', p_ctx, v_ctx))

    out = lax.map(one_row, (jnp.arange(rows), qg))
    return jnp.moveaxis(out, 0, 1).reshape(B, N, H, Dh)

def hierarchical_moe(h, w_rg, b_rg, w_re, b_re, w_gate, w_up, w_down):
    B, L, D = h.shape
    t = h.reshape(B * L, D)
    T = t.shape[0]
    g_logits = (t @ w_rg + b_rg).astype(jnp.float32)
    g_prob = jax.nn.softmax(g_logits, axis=-1)
    g_sel = jnp.argmax(g_logits, axis=-1)
    g_w = jnp.take_along_axis(g_prob, g_sel[:, None], axis=-1)
    e_logits = (t @ w_re + b_re).astype(jnp.float32).reshape(T, N_GROUPS, EXPERTS_PER_GROUP)
    e_logits = jnp.take_along_axis(e_logits, g_sel[:, None, None], axis=1)[:, 0]
    top_p, top_i = lax.top_k(jax.nn.softmax(e_logits, axis=-1), TOP_K_IN_GROUP)
    top_p = top_p / jnp.sum(top_p, axis=-1, keepdims=True)
    within = jnp.sum(jax.nn.one_hot(top_i, EXPERTS_PER_GROUP, dtype=jnp.float32) * top_p[..., None], axis=1)
    combine = (jax.nn.one_hot(g_sel, N_GROUPS, dtype=jnp.float32)[:, :, None]
               * (g_w * within)[:, None, :]).astype(h.dtype)
    wg = w_gate.reshape(N_GROUPS, EXPERTS_PER_GROUP, D, D_EXPERT)
    wu = w_up.reshape(N_GROUPS, EXPERTS_PER_GROUP, D, D_EXPERT)
    wd = w_down.reshape(N_GROUPS, EXPERTS_PER_GROUP, D_EXPERT, D)

    def one_group(args):
        wg_g, wu_g, wd_g, comb_g = args
        hid = jax.nn.silu(jnp.einsum('td,edf->tef', t, wg_g)) * jnp.einsum('td,edf->tef', t, wu_g)
        return jnp.einsum('tef,efd->td', hid * comb_g[:, :, None], wd_g)

    y = jnp.sum(lax.map(one_group, (wg, wu, wd, jnp.moveaxis(combine, 1, 0))), axis=0)
    return y.reshape(B, L, D)

def first_inputs(seed: int = 0) -> dict:
    key = jax.random.key(seed)
    ks = jax.random.split(key, 24)
    D = D_MODEL

    def nrm(k, shape, scale):
        return jax.random.normal(k, shape, jnp.float32) * scale

    return {
        'x': nrm(ks[0], (BATCH, SEQ, D), 1.0),
        'c': nrm(ks[1], (BATCH, D), 1.0),
        'ctx': nrm(ks[2], (BATCH, CTX_LEN, D), 1.0),
        'c_ctx': nrm(ks[3], (D,), 1.0),
        'w_mod': nrm(ks[4], (DEPTH, D, 6 * D), 0.5 * D ** -0.5),
        'b_mod': nrm(ks[5], (DEPTH, 6 * D), 0.02),
        'norm_attn_g': 1.0 + nrm(ks[6], (DEPTH, D), 0.02),
        'norm_ffn_g': 1.0 + nrm(ks[7], (DEPTH, D), 0.02),
        'w_in': nrm(ks[8], (DEPTH, D, Q_COLS + KV_COLS), D ** -0.5),
        'q_a_norm_g': 1.0 + nrm(ks[9], (DEPTH, Q_LORA), 0.02),
        'kv_a_norm_g': 1.0 + nrm(ks[10], (DEPTH, KV_LORA), 0.02),
        'w_uq': nrm(ks[11], (DEPTH, Q_LORA, MLA_HEADS * MLA_QK), Q_LORA ** -0.5),
        'w_ukv': nrm(ks[12], (DEPTH, KV_LORA, MLA_HEADS * (MLA_NOPE + MLA_V)), KV_LORA ** -0.5),
        'na_rel_bias': nrm(ks[13], (DEPTH, NA_HEADS, 2 * NA_WIN_H - 1, 2 * NA_WIN_W - 1), 0.5),
        'w_out': nrm(ks[14], (DEPTH, MIX_WIDTH, D), MIX_WIDTH ** -0.5),
        'w_router_group': nrm(ks[15], (DEPTH, D, N_GROUPS), D ** -0.5),
        'b_router_group': nrm(ks[16], (DEPTH, N_GROUPS), 0.01),
        'w_router_expert': nrm(ks[17], (DEPTH, D, N_EXPERTS), D ** -0.5),
        'b_router_expert': nrm(ks[18], (DEPTH, N_EXPERTS), 0.01),
        'w_gate': nrm(ks[19], (DEPTH, N_EXPERTS, D, D_EXPERT), D ** -0.5),
        'w_up': nrm(ks[20], (DEPTH, N_EXPERTS, D, D_EXPERT), D ** -0.5),
        'w_down': nrm(ks[21], (DEPTH, N_EXPERTS, D_EXPERT, D), D_EXPERT ** -0.5),
        'final_norm_g': 1.0 + nrm(ks[22], (D,), 0.02),
    }

def first_block(x, c, ctx, c_ctx, w_mod, b_mod, norm_attn_g, norm_ffn_g, w_in, q_a_norm_g, kv_a_norm_g,
              w_uq, w_ukv, na_rel_bias, w_out, w_router_group, b_router_group, w_router_expert,
              b_router_expert, w_gate, w_up, w_down, final_norm_g):
    B, N, D = x.shape
    pos = jnp.arange(N)
    cos, sin = axial_rope_tables(pos // GRID_W, pos % GRID_W, x.dtype)
    for l in range(DEPTH):
        sh1, sc1, g1, sh2, sc2, g2 = [m[:, None, :] for m in adaln(c, w_mod[l], b_mod[l])]
        csh1, csc1, cg1, csh2, csc2, cg2 = adaln(c_ctx, w_mod[l], b_mod[l])
        hx = modulate(rmsnorm(x, norm_attn_g[l]), sh1, sc1)
        hc = modulate(rmsnorm(ctx, norm_attn_g[l]), csh1, csc1)

        kn_c, kr_c, v_c, nk_c, nv_c = mixer_keys_values(hc @ w_in[l][:, Q_COLS:], kv_a_norm_g[l], w_ukv[l])
        k_c = mla_keys(kn_c, kr_c[:, :, None, :])

        proj = hx @ w_in[l]
        q_m, nq = mixer_queries(proj[..., :Q_COLS], q_a_norm_g[l], w_uq[l])
        kn, kr, v_m, nk, nv = mixer_keys_values(proj[..., Q_COLS:], kv_a_norm_g[l], w_ukv[l])
        q_m = jnp.concatenate([q_m[..., :MLA_NOPE], apply_rope(q_m[..., MLA_NOPE:], cos, sin)], axis=-1)
        k_m = mla_keys(kn, apply_rope(kr[:, :, None, :], cos, sin))
        o_mla = mla_latent_attention(q_m, k_m, v_m, k_c, v_c)
        o_na = neighbourhood_attention(nq, nk, nv, nk_c, nv_c, na_rel_bias[l])
        mixed = jnp.concatenate([o_mla.reshape(B, N, -1), o_na.reshape(B, N, -1)], axis=-1) @ w_out[l]

        if l < DEPTH - 1:
            Bc, C = ctx.shape[:2]
            q_c, nq_c = mixer_queries(hc @ w_in[l][:, :Q_COLS], q_a_norm_g[l], w_uq[l])
            mixed_c = jnp.concatenate([dense_attention(q_c, k_c, v_c).reshape(Bc, C, -1),
                                       dense_attention(nq_c, nk_c, nv_c).reshape(Bc, C, -1)], axis=-1) @ w_out[l]
            ctx = ctx + cg1 * mixed_c
            hc2 = modulate(rmsnorm(ctx, norm_ffn_g[l]), csh2, csc2)
            ctx = ctx + cg2 * hierarchical_moe(hc2, w_router_group[l], b_router_group[l], w_router_expert[l],
                                               b_router_expert[l], w_gate[l], w_up[l], w_down[l])

        x = x + g1 * mixed
        hx2 = modulate(rmsnorm(x, norm_ffn_g[l]), sh2, sc2)
        x = x + g2 * hierarchical_moe(hx2, w_router_group[l], b_router_group[l], w_router_expert[l],
                                      b_router_expert[l], w_gate[l], w_up[l], w_down[l])
    return rmsnorm(x, final_norm_g)


CHUNK = 64
MEM_LEN = 256
CONV_DIM = D_MODEL
CONV_WIDTH = 3
SB_HEADS = 16
SB_HEAD_DIM = 64
SB_DIM = SB_HEADS * SB_HEAD_DIM
SB_BLOCK = 128
X_HEADS = 4
X_HEAD_DIM = 256
X_DIM = X_HEADS * X_HEAD_DIM
N_BRANCH = 3
D_FF = 4 * D_MODEL
EPS = 1e-6

IN_SPLITS = [CONV_DIM, CONV_DIM, CONV_DIM, SB_DIM, SB_DIM, SB_DIM, X_DIM, N_BRANCH * D_MODEL]
IN_COLS = int(sum(IN_SPLITS))


def rms_norm(x, g):
    xf = x.astype(jnp.float32)
    y = xf * lax.rsqrt(jnp.mean(xf * xf, axis=-1, keepdims=True) + EPS)
    return (y * g.astype(jnp.float32)).astype(x.dtype)

def causal_depthwise_conv(u, w):
    c = u.shape[-1]
    return lax.conv_general_dilated(
        u, w.astype(u.dtype)[:, None, :], window_strides=(1,),
        padding=[(CONV_WIDTH - 1, 0)],
        dimension_numbers=("NWC", "WIO", "NWC"),
        feature_group_count=c)

def stick_breaking_attention(q, k, v):
    seq = q.shape[2]
    scale = q.shape[-1] ** -0.5
    outs = []
    for start in range(0, seq, SB_BLOCK):
        end = start + SB_BLOCK
        qb = q[:, :, start:end]
        kb = k[:, :, :end]
        vb = v[:, :, :end]
        z = jnp.einsum("bhqd,bhkd->bhqk", qb, kb).astype(jnp.float32) * scale
        t_idx = start + jnp.arange(SB_BLOCK)[:, None]
        s_idx = jnp.arange(end)[None, :]
        past = s_idx < t_idx
        log_beta = jax.nn.log_sigmoid(z)
        log_1mb = jnp.where(past, jax.nn.log_sigmoid(-z), 0.0)
        between = lax.cumsum(log_1mb, axis=3, reverse=True) - log_1mb
        a = jnp.where(past, jnp.exp(log_beta + between), 0.0)
        outs.append(jnp.einsum("bhqk,bhkd->bhqd", a.astype(vb.dtype), vb))
    return jnp.concatenate(outs, axis=2)

def memory_cross_attention(xq, mem_n, w_mem_kv, q_norm_g, k_norm_g):
    b, s, _ = xq.shape
    m = mem_n.shape[1]
    q = xq.reshape(b, s, X_HEADS, X_HEAD_DIM)
    kv = mem_n @ w_mem_kv
    k, v = jnp.split(kv, 2, axis=-1)
    k = k.reshape(b, m, X_HEADS, X_HEAD_DIM)
    v = v.reshape(b, m, X_HEADS, X_HEAD_DIM)
    q = rms_norm(q, q_norm_g)
    k = rms_norm(k, k_norm_g)
    scores = jnp.einsum("bqhd,bkhd->bhqk", q, k).astype(jnp.float32) * (X_HEAD_DIM ** -0.5)
    p = jax.nn.softmax(scores, axis=-1).astype(v.dtype)
    o = jnp.einsum("bhqk,bkhd->bqhd", p, v)
    return o.reshape(b, s, X_DIM)

def second_inputs(seed: int = 0) -> dict:
    key = jax.random.key(seed)
    ks = jax.random.split(key, 20)
    f32 = jnp.float32

    def nrm(k, shape, fan_in):
        return jax.random.normal(k, shape, f32) * (fan_in ** -0.5)

    def gain(k, shape):
        return 1.0 + 0.02 * jax.random.normal(k, shape, f32)

    L = DEPTH
    return {
        "x": jax.random.normal(ks[0], (BATCH, SEQ, D_MODEL), f32),
        "mem": jax.random.normal(ks[1], (BATCH, MEM_LEN, D_MODEL), f32),
        "g_mix": gain(ks[2], (L, D_MODEL)),
        "g_mem": gain(ks[3], (L, D_MODEL)),
        "w_in": nrm(ks[4], (L, D_MODEL, IN_COLS), D_MODEL),
        "conv_w": nrm(ks[5], (L, CONV_WIDTH, CONV_DIM), CONV_WIDTH),
        "w_conv_out": nrm(ks[6], (L, CONV_DIM, D_MODEL), CONV_DIM),
        "w_sb_out": nrm(ks[7], (L, SB_DIM, D_MODEL), SB_DIM),
        "q_norm_g": gain(ks[8], (L, X_HEAD_DIM)),
        "k_norm_g": gain(ks[9], (L, X_HEAD_DIM)),
        "w_mem_kv": nrm(ks[10], (L, D_MODEL, 2 * X_DIM), D_MODEL),
        "w_x_out": nrm(ks[11], (L, X_DIM, D_MODEL), X_DIM),
        "w_out": nrm(ks[12], (L, D_MODEL, D_MODEL), D_MODEL),
        "g_mlp": gain(ks[13], (L, D_MODEL)),
        "w_up": nrm(ks[14], (L, D_MODEL, D_FF), D_MODEL),
        "w_down": nrm(ks[15], (L, D_FF, D_MODEL), D_FF),
    }

def second_block(x, mem, g_mix, g_mem, w_in, conv_w, w_conv_out, w_sb_out, q_norm_g,
              k_norm_g, w_mem_kv, w_x_out, w_out, g_mlp, w_up, w_down):
    b, s, d = x.shape
    split_idx = list(np.cumsum(IN_SPLITS)[:-1])
    for l in range(DEPTH):
        h = rms_norm(x, g_mix[l])
        proj = h @ w_in[l]
        c_h, c_b, c_c, sq, sk, sv, xq, gate_pre = jnp.split(proj, split_idx, axis=-1)

        y_conv = (c_b * causal_depthwise_conv(c_c * c_h, conv_w[l])) @ w_conv_out[l]

        to_heads = lambda t: t.reshape(b, s, SB_HEADS, SB_HEAD_DIM).transpose(0, 2, 1, 3)
        o_sb = stick_breaking_attention(to_heads(sq), to_heads(sk), to_heads(sv))
        y_sb = o_sb.transpose(0, 2, 1, 3).reshape(b, s, SB_DIM) @ w_sb_out[l]

        mem_n = rms_norm(mem, g_mem[l])
        y_x = memory_cross_attention(xq, mem_n, w_mem_kv[l], q_norm_g[l], k_norm_g[l]) @ w_x_out[l]

        gates = jax.nn.sigmoid(gate_pre.astype(jnp.float32)).astype(x.dtype)
        gates = gates.reshape(b, s, N_BRANCH, d)
        merged = gates[:, :, 0] * y_conv + gates[:, :, 1] * y_sb + gates[:, :, 2] * y_x
        x = x + merged @ w_out[l]

        h2 = rms_norm(x, g_mlp[l])
        x = x + jnp.square(jax.nn.relu(h2 @ w_up[l])) @ w_down[l]
    return x


def setup_inputs(seed=0):
    out = dict(first_inputs(seed))
    for name, value in second_inputs(seed + 1).items():
        if name != "x":
            out[name + "_2"] = value
    return out


def reference(
    x, c, ctx, c_ctx, w_mod, b_mod, norm_attn_g, norm_ffn_g, w_in, q_a_norm_g, kv_a_norm_g,
    w_uq, w_ukv, na_rel_bias, w_out, w_router_group, b_router_group, w_router_expert,
    b_router_expert, w_gate, w_up, w_down, final_norm_g, mem_2, g_mix_2, g_mem_2, w_in_2,
    conv_w_2, w_conv_out_2, w_sb_out_2, q_norm_g_2, k_norm_g_2, w_mem_kv_2, w_x_out_2, w_out_2,
    g_mlp_2, w_up_2, w_down_2,
):
    x = first_block(
        x, c, ctx, c_ctx, w_mod, b_mod, norm_attn_g, norm_ffn_g, w_in, q_a_norm_g, kv_a_norm_g,
        w_uq, w_ukv, na_rel_bias, w_out, w_router_group, b_router_group, w_router_expert,
        b_router_expert, w_gate, w_up, w_down, final_norm_g,
    )
    return second_block(
        x, mem_2, g_mix_2, g_mem_2, w_in_2, conv_w_2, w_conv_out_2, w_sb_out_2, q_norm_g_2,
        k_norm_g_2, w_mem_kv_2, w_x_out_2, w_out_2, g_mlp_2, w_up_2, w_down_2,
    )


_drawn_inputs = setup_inputs


def setup_inputs(seed=0):
    import zlib

    import numpy as np

    out = dict(_drawn_inputs(seed))
    spreads = {}
    factors = {'norm_attn_g': 8.0,
     'norm_ffn_g': 4.568,
     'q_a_norm_g': 8.0,
     'kv_a_norm_g': 8.0,
     'na_rel_bias': 4.199,
     'b_router_group': 7.813,
     'b_router_expert': 8.0,
     'g_mix_2': 2.999,
     'g_mem_2': 8.0,
     'q_norm_g_2': 8.0,
     'k_norm_g_2': 8.0,
     'g_mlp_2': 13.015}
    for name, (base, spread) in spreads.items():
        noise = np.random.default_rng([zlib.crc32(name.encode()), seed]).standard_normal(out[name].shape)
        drawn = base * np.exp(spread * noise) if base else spread * noise
        out[name] = __import__('jax').numpy.asarray(drawn.astype(out[name].dtype))
    for name, factor in factors.items():
        out[name] = (out[name] * factor).astype(out[name].dtype)
    return out
```

```python
import numpy as np
import concourse.bass as bass
from concourse import mybir
from contextlib import ExitStack

P = 128
D = 1024
KC = D // P
T = 256
TT = T // P
HEADS, NOPE, ROPE, VDIM = 8, 64, 32, 64
Q_LORA, KV_LORA = 384, 256
QC, KVC = Q_LORA // P, KV_LORA // P
NA_HEADS, NA_DIM = 8, 64
GRID_W, NA_WIN_H, NA_WIN_W = 64, 8, 16
EXPERTS, GROUPS, PER_GROUP, D_EXPERT = 16, 4, 4, 512
SB_HEADS, SB_DIM = 16, 64
X_HEADS, X_DIM = 4, 256
D_FF = 4096
SLABS = D_FF // D_EXPERT
EPS = 1e-6
MASKED = -1e30

UNIT = 2048
UNIT_COUNTS = [
    ("mod", 8),
    ("lat", 4),
    ("naq", 2), ("nak", 2), ("nav", 2),
    ("uq", 2),
    ("ukv", 1),
    ("mod2", 16),
    ("wout", 4),
    ("moe", 6 * EXPERTS),
    ("c_h", 4), ("c_c", 4), ("c_b", 4), ("conv_out", 4), ("gate0", 4),
    ("sq", 4), ("sk", 4), ("sv", 4), ("sb_out", 4), ("gate1", 4),
    ("mk", 4), ("mv", 4), ("xq", 4), ("x_out", 4), ("gate2", 4), ("out", 4),
    ("mlp", 4 * SLABS),
]
FIRST_UNIT, UNITS = {}, 0
for _name, _count in UNIT_COUNTS:
    FIRST_UNIT[_name] = UNITS
    UNITS += _count
RAW, SPLIT = 4, 2

COL = {}
N_COLS = 0
for _name, _count in [("attn_g", 8), ("ffn_g", 8), ("final_g", 8), ("mix_g", 8), ("mem_g", 8), ("mlp_g", 8),
                      ("q_a_g", 3), ("kv_a_g", 2), ("qn_g", 2), ("kn_g", 2), ("conv", 24), ("b_mod", 48),
                      ("c", 16), ("w_r", 160), ("b_r", 20)]:
    COL[_name] = slice(N_COLS, N_COLS + _count)
    N_COLS += _count
CONST = {}
N_CONST = 0
for _name, _count in [("ident", 128), ("ones", 128), ("tri", 128), ("zero", 1), ("cos", 512), ("sin", 512), ("sb_mask", 384),
                      ("win", 256), ("win_neg", 256), ("prio", 4), ("eps", 1)]:
    CONST[_name] = slice(N_CONST, N_CONST + _count)
    N_CONST += _count

ATT = 2 * (HEADS + NA_HEADS)
ATT_MLA = 2 * HEADS


def plan_blocks():
    r, q = [("ss", "ctx_x")], []
    r += [("mod", u) for u in range(8)]
    r += [("lat", j) for j in range(7)]
    r += [("naq", j) for j in range(4)] + [("nak", j) for j in range(4)]
    r += [("nav", u, t) for u in range(2) for t in range(4)]
    r += [("ss", "qa"), ("ss", "kva")]
    r += [("q", j) for j in range(8)] + [("kn", j) for j in range(4)] + [("v", t) for t in range(4)]
    q += [("S", a) for a in range(ATT)]
    for a in range(ATT + 2):
        if a < ATT:
            r += [("PT", a)]
            if a % 2 == 0:
                r += [("mod", 8 + a // 2)]
        if a % 4 == 3:
            r += [("O", a // 4)]
    r += [("wout", j) for j in range(8)]
    r += [("ss", "ffn"), ("logits",)] + [("comb", j) for j in range(EXPERTS // 2)]
    r += [("moe", j) for j in range(8 * EXPERTS)]
    r += [("ss", "final"), ("ss", "mix")]
    for part in ("c_h", "c_c", "c_b", "conv_out", "gate0", "sq", "sk"):
        r += [(part, j) for j in range(8)]
    r += [("sv", u, t) for u in range(4) for t in range(2)]
    q += [("z", h) for h in range(SB_HEADS)]
    for g in range(1, SB_HEADS + 2):
        if g <= SB_HEADS:
            r += [("rc", g - 1)]
        if g >= 2 and g % 2 == 0:
            r += [("sbo", (g - 2) // 2)]
    r += [("sb_out", j) for j in range(8)] + [("ss", "mem")] + [("gate1", j) for j in range(8)]
    r += [("mk", j) for j in range(8)] + [("mv", u, t) for u in range(4) for t in range(2)]
    r += [("ssk", h) for h in range(4)] + [("xq", j) for j in range(8)] + [("ssq", h) for h in range(4)]
    q += [("XS", h) for h in range(X_HEADS)]
    for g in range(X_HEADS + 1):
        if g < X_HEADS:
            r += [("XP", g)]
        if g >= 1:
            r += [("XO", g - 1)]
    for part in ("x_out", "gate2", "out"):
        r += [(part, j) for j in range(8)]
    r += [("ss", "mlp")]
    r += [("mlp", j) for j in range(4 * SLABS)]
    return {k: n for n, k in enumerate(r)}, {k: n for n, k in enumerate(q)}


R_AT, Q_AT = plan_blocks()


def unit_ends():
    out = [("mod", u) for u in range(8)] + [("lat", j) for j in (1, 3, 5, 6)]
    out += [(part, j) for part in ("naq", "nak") for j in (1, 3)] + [("nav", u, 3) for u in range(2)]
    out += [("q", 3), ("q", 7), ("v", 3)] + [("mod", 8 + u) for u in range(16)]
    out += [("wout", j) for j in (1, 3, 5, 7)]
    for e in range(EXPERTS):
        out += [("moe", 8 * e + j) for j in (1, 3, 5, 7)] + [None, None]
    for name, count in UNIT_COUNTS[-17:-1]:
        out += [(name, u, 1) if name in ("sv", "mv") else (name, 2 * u + 1) for u in range(count)]
    for s in range(SLABS):
        out += [("mlp", 4 * s + j) for j in (1, 3)] + [None, None]
    assert len(out) == UNITS
    return out


UNIT_END = unit_ends()
DOWNS_BEFORE = [sum(k is None for k in UNIT_END[:n + 1]) for n in range(UNITS)]

NORMS = {"ctx_x": (KC, 512, D), "qa": (QC, T, Q_LORA), "kva": (KVC, 512, KV_LORA), "ffn": (KC, T, D),
         "final": (KC, T, D), "mix": (KC, T, D), "mem": (KC, T, D), "mlp": (KC, T, D)}
CHUNK0, PART0 = {}, {}
_c = _s = 0
for _name, (_kc, _, _) in NORMS.items():
    CHUNK0[_name], PART0[_name] = _c, _s
    _c += _kc
    if _name != "final":
        _s += _kc
NORM_NAMES = list(NORMS)


def build_program(nc, weights, xcm_d, cols_d, const_d, bias_d, out_d):
    f32, f32r = mybir.dt.float32, mybir.dt.float32r
    ALU, ACT, AX = mybir.AluOpType, mybir.ActivationFunctionType, mybir.AxisListType
    with ExitStack() as ctx:
        def sb(name, shape, dt=f32):
            return ctx.enter_context(nc.sbuf_tensor(name, shape, dt))

        def sem(name):
            return ctx.enter_context(nc.semaphore(name))

        def chunks(ap, k):
            return ap.rearrange("p (k n) -> p k n", k=k)

        raw = sb("raw", [P, RAW, UNIT])
        w_hi = sb("w_hi", [P, SPLIT, UNIT], f32r)
        w_lo = sb("w_lo", [P, SPLIT, UNIT], f32r)
        consts = sb("consts", [P, N_CONST])
        cols = sb("cols", [P, N_COLS])
        x = sb("x", [P, KC, T])
        c2 = sb("c2", [P, KC, T])
        full = sb("full", [P, 4096])
        a_hi = sb("a_hi", [P, 4096], f32r)
        a_lo = sb("a_lo", [P, 4096], f32r)
        arena = sb("arena", [P, 12288])
        mod = sb("mod", [P, 6, KC, 2])
        gain = sb("gain", [P, 2, KC, 2])
        cond_s = sb("cond_s", [P, 16])
        cond_hi, cond_lo = sb("cond_hi", [P, 16], f32r), sb("cond_lo", [P, 16], f32r)
        wr_hi, wr_lo = sb("wr_hi", [P, 160], f32r), sb("wr_lo", [P, 160], f32r)
        rt = sb("rt", [P, 2, 512])
        stat = sb("stat", [P, 16])
        route = sb("route", [P, 2, 128])

        def const(name):
            return consts[:, CONST[name]]

        def col(name, k=None):
            s = COL[name]
            return cols[:, s] if k is None else cols[:, s.start + k:s.start + k + 1]

        ident, ones, tri, zero = const("ident"), const("ones"), const("tri"), const("zero")
        h_hi, h_lo = chunks(a_hi[:, :], KC), chunks(a_lo[:, :], KC)
        full_k = chunks(full[:, :], KC)
        qlat, kvlat = chunks(full[:, 0:768], QC), chunks(full[:, 768:1792], KVC)
        qa_f, kva_f = chunks(full[:, 1792:2560], QC), chunks(full[:, 2560:3584], KVC)
        qa_hi, qa_lo = chunks(a_hi[:, 0:768], QC), chunks(a_lo[:, 0:768], QC)
        kva_hi, kva_lo = chunks(a_hi[:, 768:1792], KVC), chunks(a_lo[:, 768:1792], KVC)
        naq, nak, nav = chunks(arena[:, 0:1024], 4), chunks(arena[:, 1024:3072], 4), chunks(arena[:, 3072:5120], 4)
        qn, qr, kr = chunks(arena[:, 5120:6144], 4), chunks(arena[:, 6144:6656], 2), arena[:, 6656:7168]
        vm = chunks(arena[:, 7168:9216], 4)
        na_bias = (chunks(arena[:, 9216:11264], NA_HEADS), chunks(full[:, 2048:4096], NA_HEADS))
        rot = arena[:, 11264:11776]
        kn = chunks(c2[:, :, :].rearrange("p k n -> p (k n)"), 4)
        probs = chunks(full[:, 0:1024], 2)
        probs_t = (chunks(full[:, 1024:2048], 4), chunks(arena[:, 11264:12288], 4))
        half_hi, half_lo = chunks(a_hi[:, 0:2048], KC), chunks(a_lo[:, 0:2048], KC)
        other_hi, other_lo = chunks(a_hi[:, 2048:4096], KC), chunks(a_lo[:, 2048:4096], KC)
        comb_all = chunks(arena[:, 0:4096], EXPERTS)
        gate_f, hid_f = chunks(arena[:, 4096:5120], 4), chunks(arena[:, 5120:6144], 4)
        hid_hi, hid_lo = chunks(a_hi[:, 2048:3072], 4), chunks(a_lo[:, 2048:3072], 4)
        merged, buf_a, buf_b, buf_c = (chunks(arena[:, n * 2048:(n + 1) * 2048], KC) for n in range(4))
        sb_v = chunks(arena[:, 6144:8192], TT)
        mem_x, x_v = chunks(arena[:, 8192:10240], KC), chunks(arena[:, 8192:10240], TT)
        zm, spl, lnb, att = (chunks(full[:, n * 768:(n + 1) * 768], 2) for n in range(4))
        x_sq = chunks(full[:, 0:2048], KC)
        x_rt = (chunks(full[:, 2048:3072], 4), chunks(full[:, 3072:4096], 4))
        x_p, x_pt = chunks(full[:, 0:1024], 2), chunks(full[:, 1024:2048], 2)

        R = [ctx.enter_context(nc.psum_tensor(f"r{i}", [P, 512], f32)) for i in range(4)]
        Q = [ctx.enter_context(nc.psum_tensor(f"q{i}", [P, 512], f32)) for i in range(4)]

        inputs_in, bias_in, mem_in = sem("inputs_in"), sem("bias_in"), sem("mem_in")
        raw_in = [sem(f"raw_in{i}") for i in range(RAW)]
        hi_done = sem("hi_done")
        lo_done = sem("lo_done")
        down_used = sem("down_used")
        r_full = [sem(f"r_full{i}") for i in range(4)]
        r_out = [sem(f"r_out{i}") for i in range(4)]
        q_full = [sem(f"q_full{i}") for i in range(4)]
        q_out = [sem(f"q_out{i}") for i in range(4)]
        cond_step, cond_ready = sem("cond_step"), sem("cond_ready")
        gain_ready = sem("gain_ready")
        squared, scaled = sem("squared"), sem("scaled")
        part_hi, part_lo = sem("part_hi"), sem("part_lo")
        dve_step = sem("dve_step")
        act_step = sem("act_step")
        pool_step = sem("pool_step")
        kr_ready, qr_ready = sem("kr_ready"), sem("qr_ready")
        biased = sem("biased")
        negmax_ready, na_exp, probs_ready = sem("negmax_ready"), sem("na_exp"), sem("probs_ready")
        first_head = sem("first_head")
        o_hi = sem("o_hi")
        exp_in, exp_out = sem("exp_in"), sem("exp_out")
        comb_ready = sem("comb_ready")
        gated = sem("gated")
        hid_hi_s, hid_lo_s = sem("hid_hi_s"), sem("hid_lo_s")
        y_full, y_out = sem("y_full"), sem("y_out")
        conv_done = sem("conv_done")
        cb_hi, cb_lo = sem("cb_hi"), sem("cb_lo")
        merge_done = sem("merge_done")
        z_abs, z_ln, z_sp, z_exp = sem("z_abs"), sem("z_ln"), sem("z_sp"), sem("z_exp")
        head_sq, head_scaled = sem("head_sq"), sem("head_scaled")
        x_negmax, x_probs, xo_hi = sem("x_negmax"), sem("x_probs"), sem("xo_hi")
        mg_hi, mg_lo = sem("mg_hi"), sem("mg_lo")
        stored = sem("stored")

        def r_bank(*key):
            return R[R_AT[key] % 4]

        def wait_full(e, *key):
            e.wait_ge(r_full[R_AT[key] % 4], R_AT[key] // 4 + 1)
            return R[R_AT[key] % 4]

        def wait_out(e, *key):
            e.wait_ge(r_out[R_AT[key] % 4], R_AT[key] // 4 + 1)

        def out_sem(*key):
            return r_out[R_AT[key] % 4]

        def wait_qfull(e, *key):
            e.wait_ge(q_full[Q_AT[key] % 4], Q_AT[key] // 4 + 1)
            return Q[Q_AT[key] % 4]

        def wait_qout(e, *key):
            e.wait_ge(q_out[Q_AT[key] % 4], Q_AT[key] // 4 + 1)

        def qout_sem(*key):
            return q_out[Q_AT[key] % 4]

        def norm_io(name):
            if name == "ctx_x":
                return full_k, h_hi, h_lo
            if name == "qa":
                return qa_f, qa_hi, qa_lo
            if name == "kva":
                return kva_f, kva_hi, kva_lo
            hi, lo = (other_hi, other_lo) if name == "mem" else (half_hi, half_lo)
            return chunks(full[:, 0:2048], KC), hi, lo

        U = FIRST_UNIT
        MOE_B, MLP_B = R_AT[("moe", 0)], R_AT[("mlp", 0)]
        block = ctx.enter_context(nc.Block())

        @block.sync
        def _(sp):
            sp.dma_start(cols[:, :], cols_d).then_inc(inputs_in, 16)
            sp.dma_start(x[:, :, :], xcm_d[0]).then_inc(inputs_in, 16)
            sp.dma_start(c2[:, :, :], xcm_d[1]).then_inc(inputs_in, 16)
            sp.dma_start(consts[:, :], const_d).then_inc(inputs_in, 16)
            for n in range(RAW):
                sp.dma_start(raw[:, n, :], weights[n]).then_inc(raw_in[n], 16)
            turns = UNITS // RAW - 1
            with sp.Fori(0, turns) as i:
                for j in range(RAW):
                    sp.wait_ge(lo_done, i * RAW + (j + 1))
                    sp.dma_start(raw[:, j, :], weights[i * RAW + (j + RAW)]).then_inc(raw_in[j], 16)
            for n in range(RAW * (turns + 1), UNITS):
                sp.wait_ge(lo_done, n - RAW + 1)
                sp.dma_start(raw[:, n % RAW, :], weights[n]).then_inc(raw_in[n % RAW], 16)
            for k in range(KC):
                sp.wait_ge(y_out, KC + k + 1)
                sp.dma_start(out_d[:, k, :], x[:, k, :]).then_inc(stored, 16)
            sp.wait_ge(stored, 16 * KC)

        @block.gpsimd
        def _(pool):
            step = [0]

            def link(ins):
                step[0] += 1
                ins.then_inc(pool_step, 1)
                pool.wait_ge(pool_step, step[0])

            for qrow in range(2):
                pool.dma_start(na_bias[0][64 * qrow:64 * qrow + 64, :, :], bias_d[qrow]).then_inc(bias_in, 16)
            pool.wait_ge(part_lo, PART0["kva"] + KVC)
            for qrow in range(2):
                pool.dma_start(na_bias[1][64 * qrow:64 * qrow + 64, :, :], bias_d[2 + qrow]).then_inc(bias_in, 16)
            pool.wait_ge(inputs_in, 64)
            pool.wait_ge(bias_in, 64)
            win = const("win").unsqueeze(1).to_broadcast([P, NA_HEADS, T])
            neg = const("win_neg").unsqueeze(1).to_broadcast([P, NA_HEADS, T])
            for t in range(2):
                link(nc.gpsimd.tensor_tensor(na_bias[t], na_bias[t], win, ALU.mult))
                nc.gpsimd.tensor_tensor(na_bias[t], na_bias[t], neg, ALU.add).then_inc(biased, 1)

            def gates(i, e):
                for f in range(4):
                    b = MOE_B + 8 * e + f
                    pool.wait_ge(inputs_in, 64)
                    pool.wait_ge(r_out[b % 4], i * 4 + (b // 4 + 1))
                    nc.gpsimd.tensor_tensor(gate_f[:, f, :], gate_f[:, f, :], comb_all[:, i * 2 + e, :], ALU.mult)\
                        .then_inc(gated, 1)

            with pool.Fori(0, EXPERTS // 2) as i:
                gates(i, 0)
                gates(i, 1)
            pool.dma_start(mem_x, xcm_d[2]).then_inc(mem_in, 16)

            def merge(branch, gate, first):
                for j in range(KC):
                    wait_out(pool, branch, j)
                    wait_out(pool, gate, j)
                    if first:
                        nc.gpsimd.tensor_tensor(merged[:, j, :], buf_a[:, j, :], buf_b[:, j, :], ALU.mult)\
                            .then_inc(merge_done, 1)
                    else:
                        link(nc.gpsimd.tensor_tensor(buf_a[:, j, :], buf_a[:, j, :], buf_b[:, j, :], ALU.mult))
                        nc.gpsimd.tensor_tensor(merged[:, j, :], merged[:, j, :], buf_a[:, j, :], ALU.add)\
                            .then_inc(merge_done, 1)

            merge("conv_out", "gate0", True)
            merge("sb_out", "gate1", False)
            merge("x_out", "gate2", False)

        @block.scalar
        def _(act):
            next_unit = [0]

            def split(n):
                act.wait_ge(raw_in[n % RAW], 16 * (n // RAW + 1))
                if n >= SPLIT and UNIT_END[n - SPLIT] is not None:
                    wait_full(act, *UNIT_END[n - SPLIT])
                elif n >= SPLIT:
                    act.wait_ge(down_used, DOWNS_BEFORE[n - SPLIT])
                nc.scalar.activation(w_hi[:, n % SPLIT, :], raw[:, n % RAW, :], ACT.Copy).then_inc(hi_done, 1)

            def ahead(n):
                while next_unit[0] <= min(n + 1, UNITS - 1):
                    split(next_unit[0])
                    next_unit[0] += 1

            def copy_out(dst, *key, w=T, func=ACT.Copy):
                b = wait_full(act, *key)
                nc.scalar.activation(dst, b[:, 0:w], func).then_inc(out_sem(*key), 1)

            def root(name):
                _, w, feats = NORMS[name]
                b = wait_full(act, "ss", name)
                nc.scalar.activation(rt[:, NORM_NAMES.index(name) % 2, 0:w], b[:, 0:w], ACT.Sqrt, bias=const("eps"),
                                     scale=1.0 / feats).then_inc(out_sem("ss", name), 1)

            def upper(name, shift=None):
                f, hi, _ = norm_io(name)
                for k in range(NORMS[name][0]):
                    act.wait_ge(scaled, CHUNK0[name] + k + 1)
                    if shift is None:
                        ins = nc.scalar.activation(hi[:, k, :], f[:, k, :], ACT.Copy)
                    elif name == "ctx_x":
                        for s in range(2):
                            ins = nc.scalar.activation(hi[:, k, T * s:T * s + T], f[:, k, T * s:T * s + T],
                                                       ACT.Identity, bias=mod[:, shift, k, s:s + 1])
                    else:
                        ins = nc.scalar.activation(hi[:, k, :], f[:, k, :], ACT.Identity, bias=mod[:, shift, k, 0:1])
                    ins.then_inc(part_hi, 1)

            def square(name, k, src):
                nc.scalar.activation(norm_io(name)[0][:, k, :], src, ACT.Square).then_inc(squared, 1)

            act.wait_ge(inputs_in, 64)
            nc.scalar.activation(cond_s[:, :], col("c"), ACT.Silu).then_inc(cond_step, 1)
            act.wait_ge(cond_step, 1)
            nc.scalar.activation(cond_hi[:, :], cond_s[:, :], ACT.Copy).then_inc(cond_step, 1)
            nc.scalar.activation(wr_hi[:, :], col("w_r"), ACT.Copy).then_inc(cond_step, 1)
            ahead(-1)
            for k in range(KC):
                nc.scalar.activation(full_k[:, k, 0:T], x[:, k, :], ACT.Square)
                nc.scalar.activation(full_k[:, k, T:512], c2[:, k, :], ACT.Square).then_inc(squared, 1)
            root("ctx_x")
            ahead(7)
            upper("ctx_x", 0)
            act.wait_ge(part_lo, PART0["ctx_x"] + KC)
            for j in range(5):
                ahead(U["lat"] + j // 2)
                dst, w = (qlat[:, j, :], T) if j < 3 else (kvlat[:, j - 3, :], 512)
                copy_out(dst, "lat", j, w=w)
            ahead(U["lat"] + 3)
            for j in range(5):
                wait_out(act, "lat", j)
                if j < 3:
                    square("qa", j, qlat[:, j, :])
                else:
                    square("kva", j - 3, kvlat[:, j - 3, :])
            for j in range(4):
                ahead(U["naq"] + j // 2)
                copy_out(naq[:, j, :], "naq", j)
            for j in range(4):
                ahead(U["nak"] + j // 2)
                copy_out(nak[:, j, :], "nak", j, w=512)
            for u in range(2):
                for t in range(4):
                    ahead(U["nav"] + u)
                    copy_out(nav[:, t, T * u:T * u + T], "nav", u, t)
            root("qa")
            root("kva")
            upper("qa")
            upper("kva")
            for j in range(4):
                ahead(U["uq"])
                copy_out(qn[:, j, :], "q", j)
            ahead(U["ukv"])
            for j in range(4):
                copy_out(kn[:, j, :], "kn", j, w=512)
            for t in range(4):
                copy_out(vm[:, t, :], "v", t, w=512)

            def exp_tile(a):
                act.wait_ge(negmax_ready, a + 1)
                if a < ATT_MLA:
                    if a >= 2:
                        wait_full(act, "PT", a - 2)
                    s = Q[Q_AT[("S", a)] % 4]
                    nc.scalar.activation(probs[:, a % 2, :], s[:, :], ACT.Exp, bias=stat[:, 2 + a % 2:3 + a % 2],
                                         scale=(NOPE + ROPE) ** -0.5, accum_out=stat[:, 4 + a % 2:5 + a % 2])\
                        .then_inc(qout_sem("S", a), 1)
                else:
                    nc.scalar.activation(probs[:, a % 2, :], probs[:, a % 2, :], ACT.Exp,
                                         bias=stat[:, 2 + a % 2:3 + a % 2], accum_out=stat[:, 4 + a % 2:5 + a % 2])\
                        .then_inc(na_exp, 1)

            def turn_tile(a):
                h, t = a // 2, a % 2
                b = wait_full(act, "PT", a)
                if h >= 2 and h % 2 == 0:
                    act.wait_ge(first_head, h // 2)
                elif h >= 2:
                    wait_full(act, "O", (h - 2) // 2)
                nc.scalar.activation(probs_t[h % 2][:, :, P * t:P * t + P], chunks(b[:, :], 4), ACT.Copy)\
                    .then_inc(out_sem("PT", a), 1)

            def o_upper(c):
                b = wait_full(act, "O", c)
                nc.scalar.activation(half_hi[:, c, :], b[:, 0:T], ACT.Copy).then_inc(o_hi, 1)

            for a in range(ATT + 3):
                if a < ATT:
                    if a % 2 == 0:
                        ahead(U["mod2"] + a // 2)
                    exp_tile(a)
                if 1 <= a <= ATT:
                    turn_tile(a - 1)
                if a % 4 == 2 and a >= 6:
                    o_upper((a - 6) // 4)
            ahead(U["wout"] + 3)
            for k in range(KC):
                wait_out(act, "wout", k)
                square("ffn", k, x[:, k, :])
            root("ffn")
            upper("ffn", 3)
            ahead(U["moe"] - 1)
            act.wait_ge(exp_in, 1)
            nc.scalar.activation(route[:, :, 32:40], route[:, :, 24:32], ACT.Exp).then_inc(exp_out, 1)
            for j in range(EXPERTS // 2):
                copy_out(comb_all[:, 2 * j:2 * j + 2, :].rearrange("p e n -> p (e n)"), "comb", j, w=512)

            def wait_unit(i, units, downs, blocks, n):
                first = U["moe"] if units == 12 else U["mlp"]
                if n < first:
                    act.wait_ge(down_used, i * downs + (0 if units == 12 else 2 * EXPERTS))
                elif UNIT_END[n] is None:
                    act.wait_ge(down_used, i * downs + DOWNS_BEFORE[n])
                else:
                    b = R_AT[UNIT_END[n]]
                    act.wait_ge(r_full[b % 4], i * (blocks // 4) + (b // 4 + 1))

            def expert(i, e):
                for u in range(6):
                    n = U["moe"] + 6 * e + u + 1
                    act.wait_ge(raw_in[n % RAW], i * 48 + 16 * (n // RAW + 1))
                    wait_unit(i, 12, 4, 16, n - SPLIT)
                    nc.scalar.activation(w_hi[:, n % SPLIT, :], raw[:, n % RAW, :], ACT.Copy).then_inc(hi_done, 1)
                    for s in range(2):
                        f = 2 * (u % 2) + s
                        b = MOE_B + 8 * e + 2 * u + s
                        if u < 2:
                            act.wait_ge(r_full[b % 4], i * 4 + (b // 4 + 1))
                            nc.scalar.activation(gate_f[:, f, :], R[b % 4][:, 0:T], ACT.Silu).then_inc(r_out[b % 4], 1)
                        elif u < 4:
                            act.wait_ge(r_out[b % 4], i * 4 + (b // 4 + 1))
                            nc.scalar.activation(hid_hi[:, f, :], hid_f[:, f, :], ACT.Copy).then_inc(hid_hi_s, 1)

            ahead(U["moe"] - 1)
            with act.Fori(0, EXPERTS // 2) as i:
                expert(i, 0)
                expert(i, 1)
            next_unit[0] = U["moe"] + 6 * EXPERTS + 1
            for k in range(KC):
                act.wait_ge(y_out, k + 1)
                square("final", k, x[:, k, :])
            root("final")
            for k in range(KC):
                act.wait_ge(scaled, CHUNK0["final"] + k + 1)
                square("mix", k, x[:, k, :])
            root("mix")
            upper("mix")

            def part_out(part, dst, func=ACT.Copy, merged_before=None):
                for j in range(KC):
                    ahead(U[part] + j // 2)
                    if merged_before is not None:
                        act.wait_ge(merge_done, merged_before + j + 1)
                    copy_out(dst[:, j, :], part, j, func=func)

            part_out("c_h", buf_a)
            ahead(U["c_c"] + 3)
            for j in range(KC):
                ahead(U["c_b"] + j // 2)
                wait_out(act, "c_b", j)
                nc.scalar.activation(other_hi[:, j, :], buf_c[:, j, :], ACT.Copy).then_inc(cb_hi, 1)
            part_out("conv_out", buf_a)
            part_out("gate0", buf_b, ACT.Sigmoid)
            part_out("sq", buf_a, merged_before=0)
            part_out("sk", buf_b)
            for u in range(4):
                for t in range(TT):
                    ahead(U["sv"] + u)
                    copy_out(sb_v[:, t, T * u:T * u + T], "sv", u, t)
            act.preload_act_table_set("natural_log_exp_and_others")
            for g in range(SB_HEADS + 2):
                if g >= 2:
                    h = g - 2
                    wait_out(act, "rc", h)
                    nc.scalar.activation(att[:, h % 2, :], att[:, h % 2, :], ACT.Exp).then_inc(z_exp, 1)
                if g < SB_HEADS:
                    h = g
                    act.wait_ge(z_abs, h + 1)
                    nc.scalar.activation(lnb[:, h % 2, :], lnb[:, h % 2, :], ACT.Exp, scale=-1.0).then_inc(act_step, 1)
                    act.wait_ge(act_step, h + 1)
                    nc.scalar.activation(lnb[:, h % 2, :], lnb[:, h % 2, :], ACT.Ln, bias=ones[:, 0:1]).then_inc(z_ln, 1)
                if g % 2 == 0 and g >= 4:
                    c = g // 2 - 2
                    b = wait_full(act, "sbo", c)
                    nc.scalar.activation(other_hi[:, c, :], b[:, 0:T], ACT.Copy).then_inc(o_hi, 1)
            b = wait_full(act, "sbo", 7)
            nc.scalar.activation(other_hi[:, 7, :], b[:, 0:T], ACT.Copy).then_inc(o_hi, 1)
            part_out("sb_out", buf_a)
            act.wait_ge(mem_in, 16)
            for k in range(KC):
                square("mem", k, mem_x[:, k, :])
            root("mem")
            ahead(U["gate1"])
            upper("mem")
            part_out("gate1", buf_b, ACT.Sigmoid)
            part_out("mk", buf_c)
            for u in range(4):
                for t in range(TT):
                    ahead(U["mv"] + u)
                    copy_out(x_v[:, t, T * u:T * u + T], "mv", u, t)

            def head_roots(key, src, which):
                for j in range(KC):
                    wait_out(act, *((("mk", j)) if key == "ssk" else ("xq", j)))
                    nc.scalar.activation(x_sq[:, j, :], src[:, j, :], ACT.Square).then_inc(head_sq, 1)
                for h in range(X_HEADS):
                    b = wait_full(act, key, h)
                    nc.scalar.activation(x_rt[which][:, h, :], b[:, 0:T], ACT.Sqrt, bias=const("eps"),
                                         scale=1.0 / X_DIM).then_inc(out_sem(key, h), 1)

            head_roots("ssk", buf_c, 0)
            part_out("xq", buf_a, merged_before=KC)
            head_roots("ssq", buf_a, 1)
            for h in range(X_HEADS):
                act.wait_ge(x_negmax, h + 1)
                s = Q[Q_AT[("XS", h)] % 4]
                for t in range(TT):
                    if h >= 2 and t == 0:
                        wait_full(act, "XP", h - 2)
                    ins = nc.scalar.activation(x_p[:, h % 2, T * t:T * t + T], s[:, T * t:T * t + T], ACT.Exp,
                                               bias=stat[:, 10 + t:11 + t], scale=X_DIM ** -0.5,
                                               accum_out=stat[:, 12 + t:13 + t])
                ins.then_inc(qout_sem("XS", h), 1)
                b = wait_full(act, "XP", h)
                if h >= 2:
                    wait_full(act, "XO", h - 2)
                nc.scalar.activation(x_pt[:, h % 2, :], b[:, :], ACT.Copy).then_inc(out_sem("XP", h), 1)
                if h >= 1:
                    b = wait_full(act, "XO", h - 1)
                    nc.scalar.activation(other_hi[:, 2 * h - 2:2 * h, :], chunks(b[:, :], 2), ACT.Copy).then_inc(xo_hi, 1)
            b = wait_full(act, "XO", 3)
            nc.scalar.activation(other_hi[:, 6:8, :], chunks(b[:, :], 2), ACT.Copy).then_inc(xo_hi, 1)
            part_out("x_out", buf_a)
            part_out("gate2", buf_b, ACT.Sigmoid)
            ahead(U["out"])
            for j in range(KC):
                act.wait_ge(merge_done, 2 * KC + j + 1)
                nc.scalar.activation(other_hi[:, j, :], merged[:, j, :], ACT.Copy).then_inc(mg_hi, 1)
            ahead(U["out"] + 3)
            for k in range(KC):
                wait_out(act, "out", k)
                square("mlp", k, x[:, k, :])
            root("mlp")
            upper("mlp")

            def slab(i, last=False):
                for u in range(4):
                    n = U["mlp"] + u + 1
                    if not (last and u == 3):
                        act.wait_ge(raw_in[n % RAW], i * 16 + 16 * (n // RAW + 1))
                        wait_unit(i, 4, 2, 4, n - SPLIT)
                        nc.scalar.activation(w_hi[:, n % SPLIT, :], raw[:, n % RAW, :], ACT.Copy).then_inc(hi_done, 1)
                    for s in range(2):
                        f = 2 * u + s
                        if u < 2:
                            b = MLP_B + f
                            act.wait_ge(r_full[b % 4], i + (b // 4 + 1))
                            nc.scalar.activation(gate_f[:, f, :], R[b % 4][:, 0:T], ACT.Relu).then_inc(gated, 1)
                            act.wait_ge(r_out[b % 4], i + (b // 4 + 1))
                            nc.scalar.activation(hid_hi[:, f, :], hid_f[:, f, :], ACT.Copy).then_inc(hid_hi_s, 1)

            ahead(U["mlp"] - 1)
            with act.Fori(0, SLABS - 1) as i:
                slab(i)
            slab(SLABS - 1, last=True)

        @block.vector
        def _(dve):
            next_unit, step = [0], [0]

            def link(ins):
                step[0] += 1
                ins.then_inc(dve_step, 1)
                dve.wait_ge(dve_step, step[0])

            def split(n):
                dve.wait_ge(hi_done, n + 1)
                nc.vector.tensor_tensor(w_lo[:, n % SPLIT, :], raw[:, n % RAW, :], w_hi[:, n % SPLIT, :].bitcast(f32),
                                        ALU.subtract).then_inc(lo_done, 1)

            def ahead(n):
                while next_unit[0] <= min(n + 1, UNITS - 1):
                    split(next_unit[0])
                    next_unit[0] += 1

            def lower(dst, src, hi):
                return nc.vector.tensor_tensor(dst, src, hi.bitcast(f32), ALU.subtract)

            def scale_and_split(name, src, gain_of, shift=None):
                kc, w, _ = NORMS[name]
                f, hi, lo = norm_io(name)
                r = rt[:, NORM_NAMES.index(name) % 2, 0:w]
                wait_out(dve, "ss", name)
                link(nc.vector.reciprocal(r, r))
                for k in range(kc + 1):
                    if k < kc and name == "ctx_x":
                        for s in range(2):
                            ins = nc.vector.scalar_tensor_tensor(
                                out=f[:, k, T * s:T * s + T], in0=(x, c2)[s][:, k, :], scalar=gain[:, 0, k, s:s + 1],
                                in1=r[:, T * s:T * s + T], op0=ALU.mult, op1=ALU.mult)
                        ins.then_inc(scaled, 1)
                    elif k < kc:
                        dst = x[:, k, :] if name == "final" else f[:, k, :]
                        nc.vector.scalar_tensor_tensor(out=dst, in0=src[:, k, :], scalar=gain_of(k), in1=r,
                                                       op0=ALU.mult, op1=ALU.mult).then_inc(scaled, 1)
                    if k >= 1 and name != "final":
                        j = k - 1
                        dve.wait_ge(part_hi, PART0[name] + j + 1)
                        if shift is None:
                            ins = lower(lo[:, j, :], f[:, j, :], hi[:, j, :])
                        elif name == "ctx_x":
                            for s in range(2):
                                c = slice(T * s, T * s + T)
                                ins = nc.vector.scalar_tensor_tensor(
                                    out=lo[:, j, c], in0=f[:, j, c], scalar=mod[:, shift, j, s:s + 1],
                                    in1=hi[:, j, c].bitcast(f32), op0=ALU.add, op1=ALU.subtract)
                        else:
                            ins = nc.vector.scalar_tensor_tensor(
                                out=lo[:, j, :], in0=f[:, j, :], scalar=mod[:, shift, j, 0:1],
                                in1=hi[:, j, :].bitcast(f32), op0=ALU.add, op1=ALU.subtract)
                        ins.then_inc(part_lo, 1)

            def mod_out(u):
                g, k = u // 4, 2 * (u % 4)
                b = wait_full(dve, "mod", u)
                bias = col("b_mod")[:, 2 * u:2 * u + 2].unsqueeze(2).to_broadcast([P, 2, 2])
                nc.vector.tensor_tensor(mod[:, g, k:k + 2, :], chunks(b[:, 0:4], 2), bias, ALU.add)\
                    .then_inc(out_sem("mod", u), 1)

            def gains(which, g, name):
                for u in range(4 * g, 4 * g + 4):
                    wait_out(dve, "mod", u)
                gb = col(name).unsqueeze(2).to_broadcast([P, KC, 2])
                link(nc.vector.scalar_tensor_tensor(out=gain[:, which, :, :], in0=mod[:, g, :, :], scalar=1.0, in1=gb,
                                                    op0=ALU.add, op1=ALU.mult))

            dve.wait_ge(cond_step, 2)
            lower(cond_lo[:, :], cond_s[:, :], cond_hi[:, :]).then_inc(cond_ready, 1)
            dve.wait_ge(cond_step, 3)
            lower(wr_lo[:, :], col("w_r"), wr_hi[:, :]).then_inc(cond_ready, 1)
            for u in range(8):
                ahead(U["mod"] + u)
                mod_out(u)
            gains(0, 1, "attn_g")
            scale_and_split("ctx_x", None, None, 0)

            ahead(U["lat"] + 3)
            b = wait_full(dve, "lat", 5)
            nc.vector.tensor_tensor(kr, b[:, :], const("cos"), ALU.mult).then_inc(out_sem("lat", 5), 1)
            b = wait_full(dve, "lat", 6)
            nc.vector.tensor_tensor(rot, b[:, :], const("sin"), ALU.mult).then_inc(out_sem("lat", 6), 1)
            wait_out(dve, "lat", 5)
            wait_out(dve, "lat", 6)
            nc.vector.tensor_tensor(kr, kr, rot, ALU.add).then_inc(kr_ready, 1)
            for part in ("naq", "nak", "nav"):
                ahead(U[part] + 1)
            scale_and_split("qa", qlat, lambda k: col("q_a_g", k))
            scale_and_split("kva", kvlat, lambda k: col("kv_a_g", k))
            ahead(U["uq"] + 1)
            for j in range(2):
                b = wait_full(dve, "q", 4 + j)
                nc.vector.tensor_tensor(qr[:, j, :], b[:, 0:T], const("cos")[:, 0:T], ALU.mult)\
                    .then_inc(out_sem("q", 4 + j), 1)
            for j in range(2):
                b = wait_full(dve, "q", 6 + j)
                nc.vector.tensor_tensor(rot[:, T * j:T * j + T], b[:, 0:T], const("sin")[:, 0:T], ALU.mult)\
                    .then_inc(out_sem("q", 6 + j), 1)
            for j in range(2):
                wait_out(dve, "q", 4 + j)
                wait_out(dve, "q", 6 + j)
                nc.vector.tensor_tensor(qr[:, j, :], qr[:, j, :], rot[:, T * j:T * j + T], ALU.add)\
                    .then_inc(qr_ready, 1)
            ahead(U["ukv"])

            def tile_max(a):
                b = wait_qfull(dve, "S", a)
                mx, nm = stat[:, a % 2:a % 2 + 1], stat[:, 2 + a % 2:3 + a % 2]
                if a < ATT_MLA:
                    link(nc.vector.reduce_max(mx, b[:, :], AX.X))
                    nc.vector.tensor_scalar(nm, mx, -(NOPE + ROPE) ** -0.5, None, ALU.mult).then_inc(negmax_ready, 1)
                else:
                    if a == ATT_MLA:
                        dve.wait_ge(biased, 2)
                    p = probs[:, a % 2, :]
                    wait_full(dve, "PT", a - 2)
                    nc.vector.scalar_tensor_tensor(out=p[:, 0:T], in0=b[:, 0:T], scalar=NA_DIM ** -0.5,
                                                   in1=na_bias[a % 2][:, a // 2 - HEADS, :], op0=ALU.mult, op1=ALU.add)
                    nc.vector.tensor_scalar(p[:, T:512], b[:, T:512], NA_DIM ** -0.5, None, ALU.mult)\
                        .then_inc(qout_sem("S", a), 1)
                    wait_qout(dve, "S", a)
                    link(nc.vector.reduce_max(mx, p, AX.X))
                    nc.vector.tensor_scalar(nm, mx, -1.0, None, ALU.mult).then_inc(negmax_ready, 1)

            def tile_scale(a):
                if a < ATT_MLA:
                    wait_qout(dve, "S", a)
                else:
                    dve.wait_ge(na_exp, a - ATT_MLA + 1)
                s, p = stat[:, 4 + a % 2:5 + a % 2], probs[:, a % 2, :]
                link(nc.vector.reciprocal(s, s))
                nc.vector.tensor_scalar(p, p, s, None, ALU.mult).then_inc(probs_ready, 1)

            for a in range(ATT + 3):
                if a < ATT:
                    if a % 2 == 0:
                        ahead(U["mod2"] + a // 2)
                    tile_max(a)
                    if a % 2 == 0 and a >= 2:
                        mod_out(8 + a // 2 - 1)
                if 1 <= a <= ATT:
                    tile_scale(a - 1)
                if a % 4 == 2 and a >= 6:
                    c = (a - 6) // 4
                    dve.wait_ge(o_hi, c + 1)
                    b = wait_full(dve, "O", c)
                    lower(half_lo[:, c, :], b[:, 0:T], half_hi[:, c, :]).then_inc(out_sem("O", c), 1)
            mod_out(23)
            gains(1, 4, "ffn_g")
            for j in range(KC):
                ahead(U["wout"] + j // 2)
                b = wait_full(dve, "wout", j)
                nc.vector.scalar_tensor_tensor(out=x[:, j, :], in0=b[:, 0:T], scalar=mod[:, 2, j, 0:1], in1=x[:, j, :],
                                               op0=ALU.mult, op1=ALU.add).then_inc(out_sem("wout", j), 1)
            for j in range(KC):
                wait_out(dve, "wout", j)
            scale_and_split("ffn", x, lambda k: gain[:, 1, k, 0:1], 3)
            ahead(U["moe"] - 1)

            def rv(lo, w):
                return route[:, :, lo:lo + w]

            def wide(ap, w):
                return ap.to_broadcast([P, TT, w])

            prio = const("prio").unsqueeze(1).to_broadcast([P, TT, 4])

            def largest(val, mx, eq, one):
                link(nc.vector.reduce_max(mx, val, AX.X))
                link(nc.vector.tensor_tensor(eq, val, wide(mx, 4), ALU.is_equal))
                link(nc.vector.tensor_tensor(eq, eq, prio, ALU.mult))
                link(nc.vector.reduce_max(rv(120, 1), eq, AX.X))
                link(nc.vector.tensor_tensor(one, eq, wide(rv(120, 1), 4), ALU.is_equal))

            logits, g_hot, g_max = rv(0, 20), rv(48, 4), rv(121, 1)
            e_sel, e_max, hot1, hot2, top1, top2 = rv(52, 4), rv(122, 1), rv(56, 4), rv(60, 4), rv(123, 1), rv(124, 1)
            scr, comb = rv(64, 16), rv(80, 16)
            b = wait_full(dve, "logits")
            nc.vector.tensor_tensor(logits, chunks(b[:, 0:40], TT), col("b_r").unsqueeze(1).to_broadcast([P, TT, 20]),
                                    ALU.add).then_inc(out_sem("logits"), 1)
            wait_out(dve, "logits")
            largest(rv(0, 4), g_max, rv(100, 4), g_hot)
            for g in range(GROUPS):
                link(nc.vector.tensor_tensor(scr[:, :, 4 * g:4 * g + 4], rv(4 + 4 * g, 4), wide(g_hot[:, :, g:g + 1], 4),
                                             ALU.mult))
            link(nc.vector.reduce_sum(e_sel, scr.rearrange("p t (g e) -> p t e g", g=GROUPS), AX.X))
            link(nc.vector.reduce_max(e_max, e_sel, AX.X))
            link(nc.vector.tensor_tensor(rv(24, 4), rv(0, 4), wide(g_max, 4), ALU.subtract))
            nc.vector.tensor_tensor(rv(28, 4), e_sel, wide(e_max, 4), ALU.subtract).then_inc(exp_in, 1)
            dve.wait_ge(exp_out, 1)
            sums = rv(40, 2)
            link(nc.vector.reduce_sum(sums, rv(32, 8).rearrange("p t (s e) -> p t s e", s=2), AX.X))
            link(nc.vector.reciprocal(sums, sums))
            prob, prob2 = rv(104, 4), rv(108, 4)
            link(nc.vector.tensor_tensor(prob, rv(36, 4), wide(rv(41, 1), 4), ALU.mult))
            largest(prob, top1, rv(100, 4), hot1)
            link(nc.vector.scalar_tensor_tensor(out=prob2, in0=hot1, scalar=-2.0, in1=prob, op0=ALU.mult, op1=ALU.add))
            largest(prob2, top2, rv(100, 4), hot2)
            link(nc.vector.tensor_tensor(hot1, hot1, wide(top1, 4), ALU.mult))
            link(nc.vector.tensor_tensor(hot2, hot2, wide(top2, 4), ALU.mult))
            link(nc.vector.tensor_tensor(hot1, hot1, hot2, ALU.add))
            link(nc.vector.tensor_tensor(top1, top1, top2, ALU.add))
            link(nc.vector.reciprocal(top1, top1))
            link(nc.vector.tensor_tensor(hot1, hot1, wide(top1, 4), ALU.mult))
            link(nc.vector.tensor_tensor(hot1, hot1, wide(rv(40, 1), 4), ALU.mult))
            for g in range(GROUPS):
                ins = nc.vector.tensor_tensor(comb[:, :, 4 * g:4 * g + 4], hot1, wide(g_hot[:, :, g:g + 1], 4), ALU.mult)
            ins.then_inc(comb_ready, 1)

            def expert(i, e):
                for u in range(6):
                    n = U["moe"] + 6 * e + u + 1
                    dve.wait_ge(hi_done, i * 12 + (n + 1))
                    nc.vector.tensor_tensor(w_lo[:, n % SPLIT, :], raw[:, n % RAW, :],
                                            w_hi[:, n % SPLIT, :].bitcast(f32), ALU.subtract).then_inc(lo_done, 1)
                    for s in range(2):
                        f = 2 * (u % 2) + s
                        b = MOE_B + 8 * e + 2 * u + s
                        if 2 <= u < 4:
                            dve.wait_ge(gated, i * 8 + (4 * e + f + 1))
                            dve.wait_ge(r_full[b % 4], i * 4 + (b // 4 + 1))
                            nc.vector.tensor_tensor(hid_f[:, f, :], R[b % 4][:, 0:T], gate_f[:, f, :], ALU.mult)\
                                .then_inc(r_out[b % 4], 1)
                            dve.wait_ge(hid_hi_s, i * 8 + (4 * e + f + 1))
                            lower(hid_lo[:, f, :], hid_f[:, f, :], hid_hi[:, f, :]).then_inc(hid_lo_s, 1)

            with dve.Fori(0, EXPERTS // 2) as i:
                expert(i, 0)
                expert(i, 1)
            next_unit[0] = U["moe"] + 6 * EXPERTS + 1
            for m in range(KC):
                dve.wait_ge(y_full, m // 2 + 1)
                nc.vector.scalar_tensor_tensor(out=x[:, m, :], in0=Q[m // 2][:, T * (m % 2):T * (m % 2) + T],
                                               scalar=mod[:, 5, m, 0:1], in1=x[:, m, :], op0=ALU.mult, op1=ALU.add)\
                    .then_inc(y_out, 1)
            scale_and_split("final", x, lambda k: col("final_g", k))
            scale_and_split("mix", x, lambda k: col("mix_g", k))
            ahead(U["c_h"] + 3)
            for j in range(KC):
                ahead(U["c_c"] + j // 2)
                wait_out(dve, "c_h", j)
                b = wait_full(dve, "c_c", j)
                nc.vector.tensor_tensor(buf_b[:, j, :], b[:, 0:T], buf_a[:, j, :], ALU.mult)\
                    .then_inc(out_sem("c_c", j), 1)
            for j in range(KC):
                wait_out(dve, "c_c", j)
                link(nc.vector.tensor_scalar(buf_c[:, j, :], buf_b[:, j, :], col("conv", 16 + j), None, ALU.mult))
                for lag in (1, 2):
                    link(nc.vector.scalar_tensor_tensor(
                        out=buf_c[:, j, lag:T], in0=buf_b[:, j, 0:T - lag], scalar=col("conv", 8 * (2 - lag) + j),
                        in1=buf_c[:, j, lag:T], op0=ALU.mult, op1=ALU.add))
            for j in range(KC):
                ahead(U["c_b"] + j // 2)
                b = wait_full(dve, "c_b", j)
                nc.vector.tensor_tensor(buf_c[:, j, :], b[:, 0:T], buf_c[:, j, :], ALU.mult)\
                    .then_inc(out_sem("c_b", j), 1)
                dve.wait_ge(cb_hi, j + 1)
                lower(other_lo[:, j, :], buf_c[:, j, :], other_hi[:, j, :]).then_inc(cb_lo, 1)
            for part in ("conv_out", "gate0", "sq", "sk", "sv"):
                ahead(U[part] + 3)
            for g in range(SB_HEADS + 2):
                if 2 <= g < SB_HEADS + 2:
                    h = g - 2
                    b = wait_full(dve, "rc", h)
                    if h >= 2 and h % 2 == 0:
                        dve.wait_ge(first_head, HEADS + h // 2)
                    elif h >= 2:
                        wait_full(dve, "sbo", (h - 2) // 2)
                    nc.vector.tensor_tensor(att[:, h % 2, :], zm[:, h % 2, :], b[:, 0:384], ALU.subtract)\
                        .then_inc(out_sem("rc", h), 1)
                if g < SB_HEADS:
                    h = g
                    if h >= 2:
                        wait_out(dve, "rc", h - 2)
                    b = wait_qfull(dve, "z", h)
                    nc.vector.scalar_tensor_tensor(out=zm[:, h % 2, :], in0=b[:, 0:384], scalar=SB_DIM ** -0.5,
                                                   in1=const("sb_mask"), op0=ALU.mult, op1=ALU.add)\
                        .then_inc(qout_sem("z", h), 1)
                    wait_qout(dve, "z", h)
                    nc.vector.scalar_tensor_tensor(out=lnb[:, h % 2, :], in0=zm[:, h % 2, :], scalar=-1.0,
                                                   in1=zm[:, h % 2, :], op0=ALU.mult, op1=ALU.max).then_inc(z_abs, 1)
                if 1 <= g <= SB_HEADS:
                    h = g - 1
                    dve.wait_ge(z_ln, h + 1)
                    nc.vector.scalar_tensor_tensor(out=spl[:, h % 2, :], in0=zm[:, h % 2, :], scalar=0.0,
                                                   in1=lnb[:, h % 2, :], op0=ALU.max, op1=ALU.add).then_inc(z_sp, 1)
                if g % 2 == 0 and g >= 4:
                    c = g // 2 - 2
                    dve.wait_ge(o_hi, HEADS + c + 1)
                    b = wait_full(dve, "sbo", c)
                    lower(other_lo[:, c, :], b[:, 0:T], other_hi[:, c, :]).then_inc(out_sem("sbo", c), 1)
            ahead(U["sb_out"])
            dve.wait_ge(o_hi, HEADS + 8)
            b = wait_full(dve, "sbo", 7)
            lower(other_lo[:, 7, :], b[:, 0:T], other_hi[:, 7, :]).then_inc(out_sem("sbo", 7), 1)
            ahead(U["gate1"])
            scale_and_split("mem", mem_x, lambda k: col("mem_g", k))
            for part in ("gate1", "mk", "mv"):
                ahead(U[part] + 3)

            def head_scale(key, dst, which, g):
                for h in range(X_HEADS):
                    wait_out(dve, key, h)
                    link(nc.vector.reciprocal(x_rt[which][:, h, :], x_rt[which][:, h, :]))
                    for c in range(2):
                        nc.vector.scalar_tensor_tensor(out=dst[:, 2 * h + c, :], in0=dst[:, 2 * h + c, :],
                                                       scalar=col(g, c), in1=x_rt[which][:, h, :],
                                                       op0=ALU.mult, op1=ALU.mult).then_inc(head_scaled, 1)

            head_scale("ssk", buf_c, 0, "kn_g")
            ahead(U["xq"] + 3)
            head_scale("ssq", buf_a, 1, "qn_g")

            def x_scale(h):
                wait_qout(dve, "XS", h)
                link(nc.vector.reciprocal(stat[:, 12:14], stat[:, 12:14]))
                for t in range(TT):
                    p = x_p[:, h % 2, T * t:T * t + T]
                    ins = nc.vector.tensor_scalar(p, p, stat[:, 12 + t:13 + t], None, ALU.mult)
                ins.then_inc(x_probs, 1)

            def x_lower(h):
                dve.wait_ge(xo_hi, h + 1)
                b = wait_full(dve, "XO", h)
                lower(other_lo[:, 2 * h:2 * h + 2, :], chunks(b[:, :], 2), other_hi[:, 2 * h:2 * h + 2, :])\
                    .then_inc(out_sem("XO", h), 1)

            for h in range(X_HEADS):
                b = wait_qfull(dve, "XS", h)
                link(nc.vector.reduce_max(stat[:, 8:10], chunks(b[:, :], 2), AX.X))
                nc.vector.tensor_scalar(stat[:, 10:12], stat[:, 8:10], -X_DIM ** -0.5, None, ALU.mult)\
                    .then_inc(x_negmax, 1)
                x_scale(h)
                if h >= 1:
                    x_lower(h - 1)
            x_lower(X_HEADS - 1)
            ahead(U["x_out"] + 3)
            ahead(U["gate2"] + 3)
            for j in range(KC):
                dve.wait_ge(mg_hi, j + 1)
                lower(other_lo[:, j, :], merged[:, j, :], other_hi[:, j, :]).then_inc(mg_lo, 1)
            for j in range(KC):
                ahead(U["out"] + j // 2)
                b = wait_full(dve, "out", j)
                nc.vector.tensor_tensor(x[:, j, :], b[:, 0:T], x[:, j, :], ALU.add).then_inc(out_sem("out", j), 1)
            for j in range(KC):
                wait_out(dve, "out", j)
            scale_and_split("mlp", x, lambda k: col("mlp_g", k))

            def slab(i, last=False):
                for u in range(4):
                    n = U["mlp"] + u + 1
                    if not (last and u == 3):
                        dve.wait_ge(hi_done, i * 4 + (n + 1))
                        nc.vector.tensor_tensor(w_lo[:, n % SPLIT, :], raw[:, n % RAW, :],
                                                w_hi[:, n % SPLIT, :].bitcast(f32), ALU.subtract).then_inc(lo_done, 1)
                    for s in range(2):
                        f = 2 * u + s
                        if u < 2:
                            b = MLP_B + f
                            dve.wait_ge(r_full[b % 4], i + (b // 4 + 1))
                            dve.wait_ge(gated, i * 4 + (4 * EXPERTS + f + 1))
                            nc.vector.tensor_tensor(hid_f[:, f, :], R[b % 4][:, 0:T], gate_f[:, f, :], ALU.mult)\
                                .then_inc(r_out[b % 4], 1)
                            dve.wait_ge(hid_hi_s, i * 4 + (4 * EXPERTS + f + 1))
                            lower(hid_lo[:, f, :], hid_f[:, f, :], hid_hi[:, f, :]).then_inc(hid_lo_s, 1)

            ahead(U["mlp"] - 1)
            with dve.Fori(0, SLABS - 1) as i:
                slab(i)
            slab(SLABS - 1, last=True)
            for m in range(KC):
                dve.wait_ge(y_full, 4 + m // 2 + 1)
                nc.vector.tensor_tensor(x[:, m, :], Q[m // 2][:, T * (m % 2):T * (m % 2) + T], x[:, m, :], ALU.add)\
                    .then_inc(y_out, 1)

        @block.tensor
        def _(pe):
            mm = nc.tensor.matmul
            filled, q_filled = [0], [0]

            def open_block(*key):
                n = filled[0]
                assert R_AT[key] == n, (key, n)
                filled[0] += 1
                if n >= 4:
                    pe.wait_ge(r_out[n % 4], n // 4)
                return R[n % 4]

            def full_sem(*key):
                return r_full[R_AT[key] % 4]

            def open_q(*key):
                n = q_filled[0]
                assert Q_AT[key] == n, (key, n)
                q_filled[0] += 1
                if n >= 4:
                    pe.wait_ge(q_out[n % 4], n // 4)
                return Q[n % 4]

            def w_part(n, at, w=P):
                return w_hi[:, n % SPLIT, at:at + w], w_lo[:, n % SPLIT, at:at + w]

            def three(out, left, right, start, stop, group=True):
                (lh, ll), (rh, rl) = left, right
                mm(out, lh, rh, start=start, stop=False, skip_group_check=not group)
                mm(out, lh, rl, start=False, stop=False, skip_group_check=not group)
                return mm(out, ll, rh, start=False, stop=stop, skip_group_check=not group)

            def t_block(key, n, at, kc, hi, lo, w=T, ready=None):
                b = open_block(*key)
                for k in range(kc):
                    if ready is not None:
                        ready(k)
                    ins = three(b[:, 0:w], w_part(n, at + k * P), (hi[:, k, 0:w], lo[:, k, 0:w]), k == 0, k == kc - 1)
                ins.then_inc(full_sem(*key), 1)

            def after_norm(name):
                return lambda k: pe.wait_ge(part_lo, PART0[name] + k + 1)

            def product(part, hi, lo, w=T, ready=None, blocks=KC):
                for j in range(blocks):
                    n = U[part] + j // 2
                    if j % 2 == 0:
                        pe.wait_ge(lo_done, n + 1)
                    t_block((part, j), n, (j % 2) * KC * P, KC, hi, lo, w, ready if j == 0 else None)

            def rows(part, hi, lo, units, tiles, ready=None):
                for u in range(units):
                    n = U[part] + u
                    pe.wait_ge(lo_done, n + 1)
                    for t in range(tiles):
                        b = open_block(part, u, t)
                        for k in range(KC):
                            c = slice(P * t, P * t + P)
                            ins = three(b[:, 0:T], (hi[:, k, c], lo[:, k, c]), w_part(n, k * T, T), k == 0, k == KC - 1)
                        ins.then_inc(full_sem(part, u, t), 1)

            def sum_squares(name):
                kc, w, _ = NORMS[name]
                b = open_block("ss", name)
                for k in range(kc):
                    pe.wait_ge(squared, CHUNK0[name] + k + 1)
                    ins = mm(b[:, 0:w], ones, norm_io(name)[0][:, k, :], start=(k == 0), stop=(k == kc - 1))
                ins.then_inc(full_sem("ss", name), 1)

            def mod_unit(u):
                n = U["mod"] + u if u < 8 else U["mod2"] + u - 8
                pe.wait_ge(lo_done, n + 1)
                b = open_block("mod", u)
                for m in range(2):
                    for k in range(KC):
                        ins = three(b[:, 2 * m:2 * m + 2], w_part(n, (m * KC + k) * P),
                                    (cond_hi[:, 2 * k:2 * k + 2], cond_lo[:, 2 * k:2 * k + 2]), k == 0, k == KC - 1)
                ins.then_inc(full_sem("mod", u), 1)

            pe.wait_ge(inputs_in, 64)
            sum_squares("ctx_x")
            pe.wait_ge(cond_ready, 2)
            for u in range(8):
                mod_unit(u)
            for j in range(7):
                n = U["lat"] + j // 2
                if j % 2 == 0:
                    pe.wait_ge(lo_done, n + 1)
                t_block(("lat", j), n, (j % 2) * KC * P, KC, h_hi, h_lo, T if j < 3 else 512,
                        after_norm("ctx_x") if j == 0 else None)
            product("naq", h_hi, h_lo, blocks=4)
            product("nak", h_hi, h_lo, w=512, blocks=4)
            rows("nav", h_hi, h_lo, 2, 4)
            sum_squares("qa")
            sum_squares("kva")
            for j in range(8):
                n = U["uq"] + j // 4
                if j % 4 == 0:
                    pe.wait_ge(lo_done, n + 1)
                t_block(("q", j), n, (j % 4) * QC * P, QC, qa_hi, qa_lo, ready=after_norm("qa") if j == 0 else None)
            n = U["ukv"]
            pe.wait_ge(lo_done, n + 1)
            for j in range(4):
                t_block(("kn", j), n, j * KVC * P, KVC, kva_hi, kva_lo, 512, after_norm("kva") if j == 0 else None)
            for t in range(4):
                b = open_block("v", t)
                for k in range(KVC):
                    c = slice(P * t, P * t + P)
                    ins = three(b[:, :], (kva_hi[:, k, c], kva_lo[:, k, c]), w_part(n, 1024 + 512 * k, 512),
                                k == 0, k == KVC - 1)
                ins.then_inc(full_sem("v", t), 1)

            def scores(a):
                h, q = a // 2, slice(P * (a % 2), P * (a % 2) + P)
                b = open_q("S", a)
                if a < ATT_MLA:
                    n_, r_ = slice(64 * (h % 2), 64 * (h % 2) + 64), slice(32 * (h % 4), 32 * (h % 4) + 32)
                    mm(b[:, :], qn[n_, h // 2, q], kn[n_, h // 2, :], start=True, stop=False)
                    ins = mm(b[:, :], qr[r_, h // 4, q], kr[r_, :], start=False, stop=True)
                else:
                    h -= HEADS
                    n_ = slice(64 * (h % 2), 64 * (h % 2) + 64)
                    ins = mm(b[:, :], naq[n_, h // 2, q], nak[n_, h // 2, :], start=True, stop=True)
                ins.then_inc(q_full[Q_AT[("S", a)] % 4], 1)

            def weigh_values(h):
                v = vm if h < HEADS else nav
                b = open_block("O", h // 2) if h % 2 == 0 else r_bank("O", h // 2)
                wait_out(pe, "PT", 2 * h)
                wait_out(pe, "PT", 2 * h + 1)
                hv, ph = (h % HEADS) * VDIM, 64 * (h % 2)
                for kt in range(4):
                    ins = mm(b[ph:ph + 64, 0:T], v[:, kt, hv:hv + VDIM], probs_t[h % 2][:, kt, :],
                             start=(kt == 0), stop=(kt == 3))
                ins.then_inc(first_head if h % 2 == 0 else full_sem("O", h // 2), 1)

            for j in range(4):
                wait_out(pe, "q", j)
                wait_out(pe, "kn", j)
            for t in range(4):
                wait_out(pe, "v", t)
            pe.wait_ge(kr_ready, 1)
            pe.wait_ge(qr_ready, 2)
            scores(0)
            scores(1)
            for a in range(ATT + 2):
                if a + 2 < ATT:
                    scores(a + 2)
                if a < ATT:
                    pe.wait_ge(probs_ready, a + 1)
                    b = open_block("PT", a)
                    for kt in range(4):
                        ins = nc.tensor.transpose(b[:, P * kt:P * kt + P], probs[:, a % 2, P * kt:P * kt + P], ident)
                    ins.then_inc(full_sem("PT", a), 1)
                    if a % 2 == 0:
                        mod_unit(8 + a // 2)
                if a % 2 == 1 and a >= 3:
                    weigh_values((a - 3) // 2)

            def after_heads(k):
                wait_out(pe, "O", k)

            product("wout", half_hi, half_lo, ready=after_heads)
            sum_squares("ffn")
            b = open_block("logits")
            for t in range(TT):
                for k in range(KC):
                    if t == 0:
                        after_norm("ffn")(k)
                    c = slice(P * t, P * t + P)
                    ins = three(b[:, 20 * t:20 * t + 20], (half_hi[:, k, c], half_lo[:, k, c]),
                                (wr_hi[:, 20 * k:20 * k + 20], wr_lo[:, 20 * k:20 * k + 20]), k == 0, k == KC - 1)
            ins.then_inc(full_sem("logits"), 1)
            pe.wait_ge(comb_ready, 1)
            for j in range(EXPERTS // 2):
                b = open_block("comb", j)
                for e in range(2):
                    for t in range(TT):
                        weight = route[:, t, 80 + 2 * j + e:81 + 2 * j + e].to_broadcast([P, P])
                        ins = mm(b[:, T * e + P * t:T * e + P * t + P], weight, ident, start=True, stop=True)
                ins.then_inc(full_sem("comb", j), 1)

            def clear_y():
                for m in range(4):
                    mm(Q[m][:, :], ident, zero.to_broadcast([P, 512]), start=True, stop=False, skip_group_check=True)

            def close_y():
                for m in range(4):
                    mm(Q[m][:, :], ident, zero.to_broadcast([P, 512]), start=False, stop=True, skip_group_check=True)\
                        .then_inc(y_full, 1)

            def hidden_unit(n, u, i, units, blocks, b0):
                pe.wait_ge(lo_done, i * units + (n + 1))
                for s in range(2):
                    b = b0 + s
                    pe.wait_ge(r_out[b % 4], i * (blocks // 4) + b // 4)
                    for k in range(KC):
                        ins = three(R[b % 4][:, 0:T], w_part(n, (s * KC + k) * P), (half_hi[:, k, :], half_lo[:, k, :]),
                                    k == 0, k == KC - 1)
                    ins.then_inc(r_full[b % 4], 1)

            def down_unit(n, u, i, units, hid, h0):
                pe.wait_ge(lo_done, i * units + (n + 1))
                for c in range(2):
                    f = 2 * u + c
                    pe.wait_ge(hid_lo_s, i * hid + (h0 + f + 1))
                    for m in range(KC):
                        ins = three(Q[m // 2][:, T * (m % 2):T * (m % 2) + T], w_part(n, (c * KC + m) * P),
                                    (hid_hi[:, f, :], hid_lo[:, f, :]), False, False, group=False)
                ins.then_inc(down_used, 1)

            clear_y()
            with pe.Fori(0, EXPERTS // 2) as i:
                for e in range(2):
                    n = U["moe"] + 6 * e
                    for u in range(4):
                        hidden_unit(n + u, u, i, 12, 16, MOE_B + 8 * e + 2 * u)
                    for u in range(2):
                        down_unit(n + 4 + u, u, i, 12, 8, 4 * e)
            filled[0] += 8 * EXPERTS
            close_y()
            sum_squares("final")
            sum_squares("mix")
            product("c_h", half_hi, half_lo, ready=after_norm("mix"))
            product("c_c", half_hi, half_lo)
            product("c_b", half_hi, half_lo)
            product("conv_out", other_hi, other_lo, ready=lambda k: pe.wait_ge(cb_lo, k + 1))
            for part in ("gate0", "sq", "sk"):
                product(part, half_hi, half_lo)
            rows("sv", half_hi, half_lo, 4, TT)

            def z_scores(h):
                ph, c = slice(64 * (h % 2), 64 * (h % 2) + 64), h // 2
                b = open_q("z", h)
                mm(b[:, 0:256], buf_b[ph, c, 0:P], buf_a[ph, c, :], start=True, stop=True)
                mm(b[:, 256:384], buf_b[ph, c, P:T], buf_a[ph, c, P:T], start=True, stop=True)\
                    .then_inc(q_full[Q_AT[("z", h)] % 4], 1)

            def later_keys(h):
                pe.wait_ge(z_sp, h + 1)
                b, s = open_block("rc", h), spl[:, h % 2, :]
                mm(b[:, 0:128], tri, s[:, 0:128], start=True, stop=True)
                mm(b[:, 128:256], tri, s[:, 128:256], start=True, stop=False)
                mm(b[:, 128:256], ones, s[:, 256:384], start=False, stop=True)
                mm(b[:, 256:384], tri, s[:, 256:384], start=True, stop=True)\
                    .then_inc(full_sem("rc", h), 1)

            def sb_values(h):
                pe.wait_ge(z_exp, h + 1)
                b = open_block("sbo", h // 2) if h % 2 == 0 else r_bank("sbo", h // 2)
                ph, hv = slice(64 * (h % 2), 64 * (h % 2) + 64), slice(SB_DIM * h, SB_DIM * h + SB_DIM)
                mm(b[ph, 0:128], sb_v[:, 0, hv], att[:, h % 2, 0:128], start=True, stop=True)
                mm(b[ph, 128:256], sb_v[:, 0, hv], att[:, h % 2, 128:256], start=True, stop=False)
                mm(b[ph, 128:256], sb_v[:, 1, hv], att[:, h % 2, 256:384], start=False, stop=True)\
                    .then_inc(first_head if h % 2 == 0 else full_sem("sbo", h // 2), 1)

            for j in range(KC):
                wait_out(pe, "sq", j)
                wait_out(pe, "sk", j)
                wait_out(pe, "sv", j // 2, j % 2)
            z_scores(0)
            for g in range(SB_HEADS + 2):
                if g + 1 < SB_HEADS:
                    z_scores(g + 1)
                if 1 <= g <= SB_HEADS:
                    later_keys(g - 1)
                if g >= 2:
                    sb_values(g - 2)
            product("sb_out", other_hi, other_lo, ready=lambda k: wait_out(pe, "sbo", k))
            sum_squares("mem")
            product("gate1", half_hi, half_lo)
            product("mk", other_hi, other_lo, ready=after_norm("mem"))
            rows("mv", other_hi, other_lo, 4, TT)

            def head_squares(key, before):
                for h in range(X_HEADS):
                    pe.wait_ge(head_sq, before + 2 * h + 2)
                    b = open_block(key, h)
                    for c in range(2):
                        ins = mm(b[:, 0:T], ones, x_sq[:, 2 * h + c, :], start=(c == 0), stop=(c == 1))
                    ins.then_inc(full_sem(key, h), 1)

            def x_scores(h):
                b = open_q("XS", h)
                for t in range(TT):
                    for c in range(2):
                        ins = mm(b[:, T * t:T * t + T], buf_a[:, 2 * h + c, P * t:P * t + P], buf_c[:, 2 * h + c, :],
                                 start=(c == 0), stop=(c == 1))
                ins.then_inc(q_full[Q_AT[("XS", h)] % 4], 1)

            head_squares("ssk", 0)
            product("xq", half_hi, half_lo)
            head_squares("ssq", KC)
            for u in range(4):
                for t in range(TT):
                    wait_out(pe, "mv", u, t)
            pe.wait_ge(head_scaled, 2 * KC)
            x_scores(0)
            x_scores(1)
            for g in range(X_HEADS + 1):
                if g < X_HEADS:
                    pe.wait_ge(x_probs, g + 1)
                    b = open_block("XP", g)
                    for kt in range(TT):
                        for t in range(TT):
                            ins = nc.tensor.transpose(b[:, T * kt + P * t:T * kt + P * t + P],
                                                      x_p[:, g % 2, T * t + P * kt:T * t + P * kt + P], ident)
                    ins.then_inc(full_sem("XP", g), 1)
                if g + 2 < X_HEADS:
                    x_scores(g + 2)
                if g >= 1:
                    h = g - 1
                    wait_out(pe, "XP", h)
                    b = open_block("XO", h)
                    for c in range(2):
                        for kt in range(TT):
                            at = X_DIM * h + P * c
                            ins = mm(b[:, T * c:T * c + T], x_v[:, kt, at:at + P], x_pt[:, h % 2, T * kt:T * kt + T],
                                     start=(kt == 0), stop=(kt == 1))
                    ins.then_inc(full_sem("XO", h), 1)
            product("x_out", other_hi, other_lo, ready=lambda k: wait_out(pe, "XO", k // 2))
            product("gate2", half_hi, half_lo)
            product("out", other_hi, other_lo, ready=lambda k: pe.wait_ge(mg_lo, k + 1))
            sum_squares("mlp")
            clear_y()
            for k in range(KC):
                after_norm("mlp")(k)
            with pe.Fori(0, SLABS) as i:
                for u in range(2):
                    hidden_unit(U["mlp"] + u, u, i, 4, 4, MLP_B + 2 * u)
                for u in range(2):
                    down_unit(U["mlp"] + 2 + u, u, i, 4, 4, 4 * EXPERTS)
            close_y()


def constants():
    out = np.zeros((P, N_CONST), np.float32)
    out[:, CONST["ident"]] = np.eye(P, dtype=np.float32)
    out[:, CONST["ones"]] = 1.0
    i = np.arange(P)
    out[:, CONST["tri"]] = i[:, None] >= i[None, :]
    pos = np.arange(T)
    half = ROPE // 2
    inv = (np.float32(10000.0) ** (-np.arange(0, half, 2, dtype=np.float32) / np.float32(half))).astype(np.float32)
    ang = np.concatenate([(pos // GRID_W).astype(np.float32)[:, None] * inv,
                          (pos % GRID_W).astype(np.float32)[:, None] * inv], axis=1)
    at = i % half
    sign = np.where(i % ROPE < half, -1.0, 1.0).astype(np.float32)
    cos, sin = np.ones((P, 512), np.float32), np.zeros((P, 512), np.float32)
    cos[:, 0:T] = np.cos(ang).astype(np.float32).T[at]
    sin[:, 0:T] = sign[:, None] * np.sin(ang).astype(np.float32).T[at]
    out[:, CONST["cos"]], out[:, CONST["sin"]] = cos, sin
    diag = np.where(i[:, None] < i[None, :], 0.0, MASKED)
    out[:, CONST["sb_mask"]] = np.concatenate([diag, np.zeros((P, P)), diag], axis=1)
    c = np.arange(GRID_W)
    start = np.clip(c - NA_WIN_W // 2, 0, GRID_W - NA_WIN_W)
    inside = (c[None, :] >= start[:, None]) & (c[None, :] < start[:, None] + NA_WIN_W)
    inside = np.tile(inside, (2, 4)).astype(np.float32)
    out[:, CONST["win"]] = inside
    out[:, CONST["win_neg"]] = np.where(inside > 0, 0.0, MASKED)
    out[:, CONST["prio"]] = np.arange(4, 0, -1)
    out[:, CONST["eps"]] = EPS
    return out


def in_blocks(w, per_unit=2):
    k, n = w.shape
    b = w.reshape(k // P, P, n // P, P).transpose(2, 1, 0, 3).reshape(n // P, P, k)
    units = -(-len(b) // per_unit)
    out = np.zeros((units, P, UNIT), w.dtype)
    for j in range(len(b)):
        u, s = divmod(j, per_unit)
        out[u, :, s * k:(s + 1) * k] = b[j]
    return out


def in_rows(w):
    k, n = w.shape
    return w.reshape(k // P, P, n // T, T).transpose(2, 1, 0, 3).reshape(n // T, P, UNIT)


def in_down(w):
    k, n = w.shape
    return w.reshape(k // (2 * P), 2, P, n).transpose(0, 2, 1, 3).reshape(k // (2 * P), P, UNIT)


def by_feature(v):
    return v.reshape(-1, P).T


def kernel(**inputs):
    import concourse.bacc as bacc
    from concourse.bass_utils import run_bass_kernel_spmd

    a = {k: np.asarray(v) for k, v in inputs.items()}
    f32 = a["x"].dtype
    w_in, w2, w_uq, w_ukv = a["w_in"][0], a["w_in_2"][0], a["w_uq"][0], a["w_ukv"][0]
    half = ROPE // 2
    swapped = np.concatenate([np.arange(half, ROPE), np.arange(half)])
    q_cols = Q_LORA + NA_HEADS * NA_DIM
    k_rope = w_in[:, q_cols + KV_LORA:q_cols + KV_LORA + ROPE]
    na_k0 = q_cols + KV_LORA + ROPE
    na_w = NA_HEADS * NA_DIM
    uq = w_uq.reshape(Q_LORA, HEADS, NOPE + ROPE)
    ukv = w_ukv.reshape(KV_LORA, HEADS, NOPE + VDIM)
    wm = in_blocks(a["w_mod"][0])

    def cut(n):
        return w2[:, n * D:(n + 1) * D]

    kn_v = np.concatenate([
        in_blocks(ukv[:, :, :NOPE].reshape(KV_LORA, -1), 4)[0][:, 0:1024],
        ukv[:, :, NOPE:].reshape(KVC, P, HEADS * VDIM).transpose(1, 0, 2).reshape(P, 1024)], axis=1)[None]
    experts = []
    for e in range(EXPERTS):
        experts += [in_blocks(a["w_gate"][0, e]), in_blocks(a["w_up"][0, e]), in_down(a["w_down"][0, e])]
    slabs = []
    for s in range(SLABS):
        c = slice(s * D_EXPERT, (s + 1) * D_EXPERT)
        slabs += [in_blocks(a["w_up_2"][0][:, c]), in_down(a["w_down_2"][0][c, :])]
    weights = np.concatenate([
        wm[:8],
        in_blocks(np.concatenate([w_in[:, :Q_LORA], w_in[:, q_cols:q_cols + KV_LORA], np.tile(k_rope, (1, 4)),
                                  np.tile(k_rope[:, swapped], (1, 4))], axis=1)),
        in_blocks(w_in[:, Q_LORA:q_cols]), in_blocks(w_in[:, na_k0:na_k0 + na_w]), in_rows(w_in[:, na_k0 + na_w:]),
        in_blocks(np.concatenate([uq[:, :, :NOPE].reshape(Q_LORA, -1), uq[:, :, NOPE:].reshape(Q_LORA, -1),
                                  uq[:, :, NOPE:][:, :, swapped].reshape(Q_LORA, -1)], axis=1), 4),
        kn_v, wm[8:], in_blocks(a["w_out"][0]), *experts,
        in_blocks(cut(0)), in_blocks(cut(2)), in_blocks(cut(1)), in_blocks(a["w_conv_out_2"][0]), in_blocks(cut(7)),
        in_blocks(cut(3)), in_blocks(cut(4)), in_rows(cut(5)), in_blocks(a["w_sb_out_2"][0]), in_blocks(cut(8)),
        in_blocks(a["w_mem_kv_2"][0][:, :D]), in_rows(a["w_mem_kv_2"][0][:, D:]), in_blocks(cut(6)),
        in_blocks(a["w_x_out_2"][0]), in_blocks(cut(9)), in_blocks(a["w_out_2"][0]), *slabs])
    assert weights.shape == (UNITS, P, UNIT)
    tokens = np.stack([v[0].T.reshape(KC, P, T).transpose(1, 0, 2) for v in (a["x"], a["ctx"], a["mem_2"])])
    cond = np.stack([by_feature(a["c"][0]), by_feature(a["c_ctx"])], axis=2).reshape(P, 16)
    router = np.concatenate([a["w_router_group"][0], a["w_router_expert"][0]], axis=1)
    b_router = np.concatenate([a["b_router_group"][0], a["b_router_expert"][0]])
    cols = np.concatenate(
        [by_feature(a[n].reshape(-1)) for n in ("norm_attn_g", "norm_ffn_g", "final_norm_g", "g_mix_2", "g_mem_2",
                                                "g_mlp_2", "q_a_norm_g", "kv_a_norm_g", "q_norm_g_2", "k_norm_g_2")]
        + [by_feature(a["conv_w_2"][0, tap]) for tap in range(3)]
        + [by_feature(a["b_mod"][0]), cond, router.reshape(KC, P, 20).transpose(1, 0, 2).reshape(P, 160),
           np.tile(b_router, (P, 1))], axis=1)
    c = np.arange(GRID_W)
    across = np.clip(c[None, :] - c[:, None] + NA_WIN_W - 1, 0, 2 * NA_WIN_W - 2)
    rows = T // GRID_W
    down = np.arange(rows)[None, :] - np.arange(rows)[:, None] + NA_WIN_H - 1
    bias = a["na_rel_bias"][0][:, down[:, None, :, None], across[None, :, None, :]]
    bias = bias.transpose(1, 2, 0, 3, 4).reshape(rows, GRID_W, NA_HEADS, T)
    arrays = {"weights": weights, "tokens": tokens, "cols": cols, "constants": constants(), "bias": bias}
    arrays = {f"in_{n}": np.ascontiguousarray(v) for n, v in arrays.items()}
    nc = bacc.Bacc("TRN2", target_bir_lowering=False, num_devices=1)
    args = [nc.dram_tensor(n, v.shape, mybir.dt.from_np(v.dtype), kind="ExternalInput").ap() for n, v in arrays.items()]
    out = nc.dram_tensor("out_features", (P, KC, T), mybir.dt.float32, kind="ExternalOutput").ap()
    build_program(nc, *args, out)
    r = run_bass_kernel_spmd(nc, [arrays], core_ids=[0])
    y = r.results[0]["out_features"]
    return y.transpose(1, 0, 2).reshape(D, T).T[None]
```

```python
import numpy as np
import concourse.bass as bass
from concourse import mybir
from contextlib import ExitStack

P = 128
D = 1024
KC = D // P
T = 256
TT = T // P
HEADS, NOPE, ROPE, VDIM = 8, 64, 32, 64
Q_LORA, KV_LORA = 384, 256
QC, KVC = Q_LORA // P, KV_LORA // P
NA_HEADS, NA_DIM = 8, 64
GRID_W, NA_WIN_H, NA_WIN_W = 64, 8, 16
EXPERTS, GROUPS, PER_GROUP, D_EXPERT = 16, 4, 4, 512
SB_HEADS, SB_DIM = 16, 64
X_HEADS, X_DIM = 4, 256
D_FF = 4096
SLABS = D_FF // D_EXPERT
EPS = 1e-6
MASKED = -1e30

UNIT = 2048
UNIT_COUNTS = [
    ("mod", 8),
    ("lat", 4),
    ("naq", 2), ("nak", 2), ("nav", 2),
    ("uq", 2),
    ("ukv", 1),
    ("mod2", 16),
    ("wout", 4), ("mk", 4),
    ("moe", 6 * EXPERTS), ("mv", 4),
    ("c_h", 4), ("c_c", 4), ("c_b", 4), ("gate0", 4), ("conv_out", 4),
    ("sq", 4), ("sk", 4), ("sv", 4), ("xq", 4), ("sb_out", 4), ("gate1", 4),
    ("gate2", 4), ("x_out", 4), ("out", 4),
    ("mlp", 4 * SLABS),
]
FIRST_UNIT, UNITS = {}, 0
for _name, _count in UNIT_COUNTS:
    FIRST_UNIT[_name] = UNITS
    UNITS += _count
RAW, SPLIT = 4, 2

COL = {}
N_COLS = 0
for _name, _count in [("attn_g", 8), ("ffn_g", 8), ("final_g", 8), ("mix_g", 8), ("mem_g", 8), ("mlp_g", 8),
                      ("q_a_g", 3), ("kv_a_g", 2), ("qn_g", 2), ("kn_g", 2), ("conv", 24), ("b_mod", 48),
                      ("c", 16), ("w_r", 160), ("b_r", 20)]:
    COL[_name] = slice(N_COLS, N_COLS + _count)
    N_COLS += _count
CONST = {}
N_CONST = 0
for _name, _count in [("ident", 128), ("ones", 128), ("tri", 128), ("zero", 1), ("cos", 512), ("sin", 512), ("sb_mask", 384),
                      ("win", 256), ("win_neg", 256), ("prio", 4), ("eps", 1)]:
    CONST[_name] = slice(N_CONST, N_CONST + _count)
    N_CONST += _count

ATT = 2 * (HEADS + NA_HEADS)
ATT_MLA = 2 * HEADS
LEAD = 3


XQ_AT = {g: (g - 1) // 2 for g in range(1, 2 * KC, 2)}


def plan_blocks():
    r, q = [], []
    for u in range(9):
        if u == 4:
            r += [("ss", "ctx_x")]
        if u < 8:
            r += [("mod", u)]
    r += [("lat", j) for j in range(7)]
    r += [("naq", j) for j in range(4)] + [("ss", "qa"), ("ss", "kva")] + [("nak", j) for j in range(4)]
    r += [("nav", u, t) for u in range(2) for t in range(4)]
    r += [("q", j) for j in range(8)] + [("kn", j) for j in range(4)] + [("v", t) for t in range(4)]
    q += [("S", a) for a in range(ATT)]
    for a in range(ATT + 2):
        if a < ATT:
            r += [("PT", a)]
            if a % 2 == 0:
                r += [("mod", 8 + a // 2)]
        if a % 4 == 3:
            r += [("O", a // 4)]
    for j in range(8):
        r += [("wout", j)] + ([("ss", "mem")] if j == 3 else [])
    r += [("mk", j) for j in range(2)] + [("ss", "ffn")] + [("mk", j) for j in range(2, 4)] + [("logits",)]
    r += [("mk", j) for j in range(4, 7)] + [("comb", j) for j in range(EXPERTS // 2)]
    q += [("mk", 7)]
    r += [("moe", j) for j in range(8 * EXPERTS)]
    for u in range(4):
        r += [("mv", u, t) for t in range(2)] + ([("ss", "final")] if u == 1 else [])
    r += [("ss", "mix")]
    for part in ("c_h", "c_c", "c_b", "gate0", "conv_out", "sq", "sk"):
        r += [(part, j) for j in range(8)]
    r += [("sv", u, t) for u in range(4) for t in range(2)]
    q += [("z", 0)]
    for g in range(SB_HEADS + 3):
        if g + 1 < SB_HEADS:
            q += [("z", g + 1)]
        if g in XQ_AT:
            q += [("xq", XQ_AT[g])]
        if 1 <= g <= SB_HEADS:
            r += [("rc", g - 1)]
        if g >= 3 and g % 2 == 1:
            r += [("sbo", (g - 3) // 2)]
    for j in range(8):
        r += [("sb_out", j)] + ([("ssk", j - 4)] if j >= 4 else [])
    for j in range(8):
        r += [("gate1", j)]
    r += [("ssq", h) for h in range(X_HEADS)] + [("gate2", j) for j in range(4)]
    q += [("XS", h) for h in range(X_HEADS)]
    for g in range(X_HEADS + 1):
        if g < X_HEADS:
            r += [("gate2", 4 + g), ("XP", g)]
        if g >= 1:
            r += [("XO", g - 1)]
    for part in ("x_out", "out"):
        r += [(part, j) for j in range(8)]
    r += [("ss", "mlp")]
    r += [("mlp", j) for j in range(4 * SLABS)]
    return {k: n for n, k in enumerate(r)}, {k: n for n, k in enumerate(q)}


R_AT, Q_AT = plan_blocks()


def unit_ends():
    out = [("mod", u) for u in range(8)] + [("lat", j) for j in (1, 3, 5, 6)]
    out += [(part, j) for part in ("naq", "nak") for j in (1, 3)] + [("nav", u, 3) for u in range(2)]
    out += [("q", 3), ("q", 7), ("v", 3)] + [("mod", 8 + u) for u in range(16)]
    out += [(part, j) for part in ("wout", "mk") for j in (1, 3, 5, 7)]
    for e in range(EXPERTS):
        out += [("moe", 8 * e + j) for j in (1, 3, 5, 7)] + [None, None]
    for name, count in UNIT_COUNTS[UNIT_COUNTS.index(("mv", 4)):-1]:
        out += [(name, u, 1) if name in ("sv", "mv") else (name, 2 * u + 1) for u in range(count)]
    for s in range(SLABS):
        out += [("mlp", 4 * s + j) for j in (1, 3)] + [None, None]
    assert len(out) == UNITS
    return out


assert R_AT[("moe", 0)] % 4 == 0
UNIT_END = unit_ends()
DOWNS_BEFORE = [sum(k is None for k in UNIT_END[:n + 1]) for n in range(UNITS)]

NORMS = {"ctx_x": (KC, 512, D), "qa": (QC, T, Q_LORA), "kva": (KVC, 512, KV_LORA), "mem": (KC, T, D),
         "ffn": (KC, T, D), "final": (KC, T, D), "mix": (KC, T, D), "mlp": (KC, T, D)}
CHUNK0, PART0 = {}, {}
_c = _s = 0
for _name, (_kc, _, _) in NORMS.items():
    CHUNK0[_name], PART0[_name] = _c, _s
    _c += _kc
    if _name != "final":
        _s += _kc
NORM_NAMES = list(NORMS)


def build_program(nc, weights, xcm_d, cols_d, const_d, bias_d, out_d):
    f32, f32r = mybir.dt.float32, mybir.dt.float32r
    ALU, ACT, AX = mybir.AluOpType, mybir.ActivationFunctionType, mybir.AxisListType
    with ExitStack() as ctx:
        def sb(name, shape, dt=f32):
            return ctx.enter_context(nc.sbuf_tensor(name, shape, dt))

        def sem(name):
            return ctx.enter_context(nc.semaphore(name))

        def chunks(ap, k):
            return ap.rearrange("p (k n) -> p k n", k=k)

        raw = sb("raw", [P, RAW, UNIT])
        w_hi = sb("w_hi", [P, SPLIT, UNIT], f32r)
        w_lo = sb("w_lo", [P, SPLIT, UNIT], f32r)
        consts = sb("consts", [P, N_CONST])
        cols = sb("cols", [P, N_COLS])
        x = sb("x", [P, KC, T])
        c2 = sb("c2", [P, KC, T])
        full = sb("full", [P, 4096])
        a_hi = sb("a_hi", [P, 5120], f32r)
        a_lo = sb("a_lo", [P, 5120], f32r)
        arena = sb("arena", [P, 12288])
        mod = sb("mod", [P, 6, KC, 2])
        gain = sb("gain", [P, 2, KC, 2])
        cond_s = sb("cond_s", [P, 16])
        cond_hi, cond_lo = chunks(a_hi[:, 4096:5120], KC), chunks(a_lo[:, 4096:5120], KC)
        mod_rows = sb("mod_rows", [P, 2, T])
        wr_hi, wr_lo = sb("wr_hi", [P, 160], f32r), sb("wr_lo", [P, 160], f32r)
        rt = sb("rt", [P, 2, 512])
        stat = sb("stat", [P, 16])
        route = sb("route", [P, 2, 128])

        def const(name):
            return consts[:, CONST[name]]

        def col(name, k=None):
            s = COL[name]
            return cols[:, s] if k is None else cols[:, s.start + k:s.start + k + 1]

        ident, ones, tri, zero = const("ident"), const("ones"), const("tri"), const("zero")
        h_hi, h_lo = chunks(a_hi[:, 0:4096], KC), chunks(a_lo[:, 0:4096], KC)
        full_k = chunks(full[:, :], KC)
        qlat, kvlat = chunks(full[:, 0:768], QC), chunks(full[:, 768:1792], KVC)
        qa_f, kva_f = chunks(full[:, 1792:2560], QC), chunks(full[:, 2560:3584], KVC)
        qa_hi, qa_lo = chunks(a_hi[:, 0:768], QC), chunks(a_lo[:, 0:768], QC)
        kva_hi, kva_lo = chunks(a_hi[:, 768:1792], KVC), chunks(a_lo[:, 768:1792], KVC)
        naq, nak, nav = chunks(arena[:, 0:1024], 4), chunks(arena[:, 1024:3072], 4), chunks(arena[:, 3072:5120], 4)
        qn, qr, kr = chunks(arena[:, 5120:6144], 4), chunks(arena[:, 6144:6656], 2), arena[:, 6656:7168]
        vm = chunks(arena[:, 7168:9216], 4)
        na_bias = (chunks(arena[:, 9216:11264], NA_HEADS), chunks(full[:, 2048:4096], NA_HEADS))
        rot = arena[:, 11264:11776]
        kn = chunks(c2[:, :, :].rearrange("p k n -> p (k n)"), 4)
        mla_probs = chunks(full[:, 0:1024], 2)
        na_probs = chunks(c2[:, :, :].rearrange("p k n -> p (k n)"), 4)
        probs_t = (chunks(full[:, 1024:2048], 4), chunks(arena[:, 11264:12288], 4))
        half_hi, half_lo = chunks(a_hi[:, 0:2048], KC), chunks(a_lo[:, 0:2048], KC)
        other_hi, other_lo = chunks(a_hi[:, 2048:4096], KC), chunks(a_lo[:, 2048:4096], KC)
        comb_all = chunks(arena[:, 0:4096], EXPERTS)
        gate_f, hid_f = chunks(arena[:, 4096:5120], 4), chunks(arena[:, 5120:6144], 4)
        hid_hi, hid_lo = chunks(a_hi[:, 2048:3072], 4), chunks(a_lo[:, 2048:3072], 4)
        merged, buf_a, buf_b, buf_c = (chunks(arena[:, n * 2048:(n + 1) * 2048], KC) for n in range(4))
        sb_v = chunks(arena[:, 6144:8192], TT)
        mem_x, x_v = chunks(arena[:, 8192:10240], KC), chunks(arena[:, 8192:10240], TT)
        mem_hi, mem_lo = chunks(a_hi[:, 3072:5120], KC), chunks(a_lo[:, 3072:5120], KC)
        xk = c2[:, :, :]
        xq = chunks(arena[:, 10240:12288], KC)
        zm = chunks(full[:, 0:1152], 3)
        spl, lnb, att = (chunks(full[:, n * 768 + 1152:n * 768 + 1920], 2) for n in range(3))
        x_sq = chunks(full[:, 0:2048], KC)
        x_rt = (chunks(full[:, 2048:3072], 4), chunks(full[:, 3072:4096], 4))
        x_p, x_pt = chunks(full[:, 0:1024], 2), chunks(full[:, 1024:2048], 2)

        R = [ctx.enter_context(nc.psum_tensor(f"r{i}", [P, 512], f32)) for i in range(4)]
        Q = [ctx.enter_context(nc.psum_tensor(f"q{i}", [P, 512], f32)) for i in range(4)]

        cols_in, tokens_in, bias_in, mem_in = sem("cols_in"), sem("tokens_in"), sem("bias_in"), sem("mem_in")
        raw_in = [sem(f"raw_in{i}") for i in range(RAW)]
        hi_done = sem("hi_done")
        lo_done = sem("lo_done")
        down_used = sem("down_used")
        r_full = [sem(f"r_full{i}") for i in range(4)]
        r_out = [sem(f"r_out{i}") for i in range(4)]
        q_full = [sem(f"q_full{i}") for i in range(4)]
        q_out = [sem(f"q_out{i}") for i in range(4)]
        mod_filled, mod_copied = sem("mod_filled"), sem("mod_copied")
        cond_step, cond_ready = sem("cond_step"), sem("cond_ready")
        gain_ready = sem("gain_ready")
        squared, scaled = sem("squared"), sem("scaled")
        part_hi, part_lo = sem("part_hi"), sem("part_lo")
        dve_step = sem("dve_step")
        act_step = sem("act_step")
        pool_step = sem("pool_step")
        kr_ready, qr_ready = sem("kr_ready"), sem("qr_ready")
        biased = sem("biased")
        negmax_ready, na_exp, probs_ready = sem("negmax_ready"), sem("na_exp"), sem("probs_ready")
        first_head = sem("first_head")
        o_hi = sem("o_hi")
        exp_in, exp_out = sem("exp_in"), sem("exp_out")
        comb_ready = sem("comb_ready")
        gated = sem("gated")
        hid_hi_s, hid_lo_s = sem("hid_hi_s"), sem("hid_lo_s")
        y_full, y_out = sem("y_full"), sem("y_out")
        conv_done = sem("conv_done")
        cb_hi, cb_lo = sem("cb_hi"), sem("cb_lo")
        merge_done = sem("merge_done")
        z_abs, z_ln, z_sp, z_exp = sem("z_abs"), sem("z_ln"), sem("z_sp"), sem("z_exp")
        head_sq, head_scaled = sem("head_sq"), sem("head_scaled")
        x_negmax, x_probs, xo_hi = sem("x_negmax"), sem("x_probs"), sem("xo_hi")
        gate2_done = sem("gate2_done")
        mg_hi, mg_lo = sem("mg_hi"), sem("mg_lo")
        stored = sem("stored")

        def probs(a):
            return mla_probs[:, a % 2, :] if a < ATT_MLA else na_probs[:, a % 4, :]

        def r_bank(*key):
            return R[R_AT[key] % 4]

        def wait_full(e, *key):
            e.wait_ge(r_full[R_AT[key] % 4], R_AT[key] // 4 + 1)
            return R[R_AT[key] % 4]

        def wait_out(e, *key):
            e.wait_ge(r_out[R_AT[key] % 4], R_AT[key] // 4 + 1)

        def out_sem(*key):
            return r_out[R_AT[key] % 4]

        def wait_qfull(e, *key):
            e.wait_ge(q_full[Q_AT[key] % 4], Q_AT[key] // 4 + 1)
            return Q[Q_AT[key] % 4]

        def wait_qout(e, *key):
            e.wait_ge(q_out[Q_AT[key] % 4], Q_AT[key] // 4 + 1)

        def qout_sem(*key):
            return q_out[Q_AT[key] % 4]

        def norm_io(name):
            if name == "ctx_x":
                return full_k, h_hi, h_lo
            if name == "qa":
                return qa_f, qa_hi, qa_lo
            if name == "kva":
                return kva_f, kva_hi, kva_lo
            if name == "mem":
                return chunks(full[:, 2048:4096], KC), mem_hi, mem_lo
            return chunks(full[:, 0:2048], KC), half_hi, half_lo

        U = FIRST_UNIT
        MOE_B, MLP_B = R_AT[("moe", 0)], R_AT[("mlp", 0)]
        block = ctx.enter_context(nc.Block())

        @block.sync
        def _(sp):
            sp.dma_start(cols[:, :], cols_d).then_inc(cols_in, 16)
            for n in range(RAW):
                sp.dma_start(raw[:, n, :], weights[n]).then_inc(raw_in[n], 16)
                if n == 0:
                    sp.dma_start(consts[:, :], const_d).then_inc(cols_in, 16)
            sp.dma_start(x[:, :, :], xcm_d[0]).then_inc(tokens_in, 16)
            sp.dma_start(c2[:, :, :], xcm_d[1]).then_inc(tokens_in, 16)
            turns = UNITS // RAW - 1
            with sp.Fori(0, turns) as i:
                for j in range(RAW):
                    sp.wait_ge(lo_done, i * RAW + (j + 1))
                    sp.dma_start(raw[:, j, :], weights[i * RAW + (j + RAW)]).then_inc(raw_in[j], 16)
            for n in range(RAW * (turns + 1), UNITS):
                sp.wait_ge(lo_done, n - RAW + 1)
                sp.dma_start(raw[:, n % RAW, :], weights[n]).then_inc(raw_in[n % RAW], 16)
            for k in range(KC):
                sp.wait_ge(y_out, KC + k + 1)
                sp.dma_start(out_d[:, k, :], x[:, k, :]).then_inc(stored, 16)
            sp.wait_ge(stored, 16 * KC)

        @block.gpsimd
        def _(pool):
            step = [0]

            def link(ins):
                step[0] += 1
                ins.then_inc(pool_step, 1)
                pool.wait_ge(pool_step, step[0])

            for qrow in range(2):
                pool.dma_start(na_bias[0][64 * qrow:64 * qrow + 64, :, :], bias_d[qrow]).then_inc(bias_in, 16)
            pool.wait_ge(part_lo, PART0["kva"] + KVC)
            for qrow in range(2):
                pool.dma_start(na_bias[1][64 * qrow:64 * qrow + 64, :, :], bias_d[2 + qrow]).then_inc(bias_in, 16)
            pool.wait_ge(cols_in, 32)
            pool.wait_ge(bias_in, 64)
            win = const("win").unsqueeze(1).to_broadcast([P, NA_HEADS, T])
            neg = const("win_neg").unsqueeze(1).to_broadcast([P, NA_HEADS, T])
            for t in range(2):
                link(nc.gpsimd.tensor_tensor(na_bias[t], na_bias[t], win, ALU.mult))
                nc.gpsimd.tensor_tensor(na_bias[t], na_bias[t], neg, ALU.add).then_inc(biased, 1)
            wait_full(pool, "O", 7)
            pool.dma_start(mem_x, xcm_d[2]).then_inc(mem_in, 16)

            def gates(i, e):
                weight = comb_all[:, i * 2 + e, :]
                for f in range(4):
                    b = MOE_B + 8 * e + f
                    pool.wait_ge(cols_in, 32)
                    pool.wait_ge(r_out[b % 4], i * 4 + (b // 4 + 1))
                    nc.gpsimd.tensor_tensor(gate_f[:, f, :], gate_f[:, f, :], weight, ALU.mult)\
                        .then_inc(gated, 1)

            with pool.Fori(0, EXPERTS // 2) as i:
                gates(i, 0)
                gates(i, 1)

            def merge(branch, gate, gates, first=False):
                for j in range(KC):
                    wait_out(pool, branch, j)
                    wait_out(pool, gate, j)
                    if gate == "gate2" and j >= 4:
                        pool.wait_ge(gate2_done, j - 3)
                    if first:
                        nc.gpsimd.tensor_tensor(merged[:, j, :], buf_a[:, j, :], gates[:, j, :], ALU.mult)\
                            .then_inc(merge_done, 1)
                    else:
                        link(nc.gpsimd.tensor_tensor(buf_a[:, j, :], buf_a[:, j, :], gates[:, j, :], ALU.mult))
                        nc.gpsimd.tensor_tensor(merged[:, j, :], merged[:, j, :], buf_a[:, j, :], ALU.add)\
                            .then_inc(merge_done, 1)

            merge("conv_out", "gate0", buf_b, first=True)
            merge("sb_out", "gate1", buf_b)
            merge("x_out", "gate2", buf_c)

        @block.scalar
        def _(act):
            next_unit = [0]

            def split(n):
                act.wait_ge(raw_in[n % RAW], 16 * (n // RAW + 1))
                if n >= SPLIT and UNIT_END[n - SPLIT] is not None and UNIT_END[n - SPLIT][0] == "mod":
                    act.wait_ge(mod_filled, UNIT_END[n - SPLIT][1] + 1)
                elif n >= SPLIT and UNIT_END[n - SPLIT] in Q_AT:
                    wait_qfull(act, *UNIT_END[n - SPLIT])
                elif n >= SPLIT and UNIT_END[n - SPLIT] is not None:
                    wait_full(act, *UNIT_END[n - SPLIT])
                elif n >= SPLIT:
                    act.wait_ge(down_used, DOWNS_BEFORE[n - SPLIT])
                nc.scalar.activation(w_hi[:, n % SPLIT, :], raw[:, n % RAW, :], ACT.Copy).then_inc(hi_done, 1)

            def ahead(n):
                while next_unit[0] <= min(n + 1, UNITS - 1):
                    split(next_unit[0])
                    next_unit[0] += 1

            def mod_rows_out(u):
                if u >= 2:
                    wait_full(act, "mod", u - 2)
                act.wait_ge(mod_filled, u + 1)
                nc.scalar.activation(mod_rows[:, u % 2, :], r_bank("mod", u)[:, 0:T], ACT.Copy).then_inc(mod_copied, 1)

            def copy_out(dst, *key, w=T, func=ACT.Copy):
                b = wait_full(act, *key)
                nc.scalar.activation(dst, b[:, 0:w], func).then_inc(out_sem(*key), 1)

            def copy_out_q(dst, *key):
                b = wait_qfull(act, *key)
                nc.scalar.activation(dst, b[:, 0:T], ACT.Copy).then_inc(qout_sem(*key), 1)

            def root(name):
                _, w, feats = NORMS[name]
                b = wait_full(act, "ss", name)
                nc.scalar.activation(rt[:, NORM_NAMES.index(name) % 2, 0:w], b[:, 0:w], ACT.Sqrt, bias=const("eps"),
                                     scale=1.0 / feats).then_inc(out_sem("ss", name), 1)

            def upper(name, shift=None):
                f, hi, _ = norm_io(name)
                for k in range(NORMS[name][0]):
                    act.wait_ge(scaled, CHUNK0[name] + k + 1)
                    if shift is None:
                        ins = nc.scalar.activation(hi[:, k, :], f[:, k, :], ACT.Copy)
                    elif name == "ctx_x":
                        for s in range(2):
                            ins = nc.scalar.activation(hi[:, k, T * s:T * s + T], f[:, k, T * s:T * s + T],
                                                       ACT.Identity, bias=mod[:, shift, k, s:s + 1])
                    else:
                        ins = nc.scalar.activation(hi[:, k, :], f[:, k, :], ACT.Identity, bias=mod[:, shift, k, 0:1])
                    ins.then_inc(part_hi, 1)

            def square(name, k, src):
                nc.scalar.activation(norm_io(name)[0][:, k, :], src, ACT.Square).then_inc(squared, 1)

            act.wait_ge(cols_in, 32)
            nc.scalar.activation(cond_s[:, :], col("c"), ACT.Silu).then_inc(cond_step, 1)
            act.wait_ge(cond_step, 1)
            nc.scalar.activation(cond_hi.rearrange("p k (s n) -> p (k s) n", s=2),
                                 cond_s[:, :].unsqueeze(2).to_broadcast([P, 16, 64]), ACT.Copy).then_inc(cond_step, 1)
            nc.scalar.activation(wr_hi[:, :], col("w_r"), ACT.Copy).then_inc(cond_step, 1)
            for u in range(4):
                ahead(U["mod"] + u + 1)
                mod_rows_out(u)
            act.wait_ge(tokens_in, 32)
            for k in range(KC):
                nc.scalar.activation(full_k[:, k, 0:T], x[:, k, :], ACT.Square)
                nc.scalar.activation(full_k[:, k, T:512], c2[:, k, :], ACT.Square).then_inc(squared, 1)
            root("ctx_x")
            for u in range(4, 8):
                ahead(U["mod"] + min(u + 1, 7))
                mod_rows_out(u)
            upper("ctx_x", 0)
            act.wait_ge(part_lo, PART0["ctx_x"] + KC)
            for j in range(5):
                ahead(U["lat"] + j // 2)
                dst, w = (qlat[:, j, :], T) if j < 3 else (kvlat[:, j - 3, :], 512)
                copy_out(dst, "lat", j, w=w)
            ahead(U["lat"] + 3)
            for j in range(5):
                wait_out(act, "lat", j)
                if j < 3:
                    square("qa", j, qlat[:, j, :])
                else:
                    square("kva", j - 3, kvlat[:, j - 3, :])
            for j in range(4):
                ahead(U["naq"] + j // 2)
                copy_out(naq[:, j, :], "naq", j)
            root("qa")
            root("kva")
            for j in range(4):
                ahead(U["nak"] + j // 2)
                copy_out(nak[:, j, :], "nak", j, w=512)
            for u in range(2):
                for t in range(4):
                    ahead(U["nav"] + u)
                    copy_out(nav[:, t, T * u:T * u + T], "nav", u, t)
            upper("qa")
            upper("kva")
            for j in range(4):
                ahead(U["uq"])
                copy_out(qn[:, j, :], "q", j)
            ahead(U["ukv"])
            for j in range(4):
                copy_out(kn[:, j, :], "kn", j, w=512)
            for t in range(4):
                copy_out(vm[:, t, :], "v", t, w=512)

            ahead(U["mod2"] - 1)
            def exp_tile(a):
                act.wait_ge(negmax_ready, a + 1)
                if a < ATT_MLA:
                    if a >= 2:
                        wait_full(act, "PT", a - 2)
                    s = Q[Q_AT[("S", a)] % 4]
                    nc.scalar.activation(probs(a), s[:, :], ACT.Exp, bias=stat[:, 2 + a % 2:3 + a % 2],
                                         scale=(NOPE + ROPE) ** -0.5, accum_out=stat[:, 4 + a % 2:5 + a % 2])\
                        .then_inc(qout_sem("S", a), 1)
                else:
                    nc.scalar.activation(probs(a), probs(a), ACT.Exp,
                                         bias=stat[:, 2 + a % 2:3 + a % 2], accum_out=stat[:, 4 + a % 2:5 + a % 2])\
                        .then_inc(na_exp, 1)

            def turn_tile(a):
                h, t = a // 2, a % 2
                b = wait_full(act, "PT", a)
                if h >= 2 and h % 2 == 0:
                    act.wait_ge(first_head, h // 2)
                elif h >= 2:
                    wait_full(act, "O", (h - 2) // 2)
                nc.scalar.activation(probs_t[h % 2][:, :, P * t:P * t + P], chunks(b[:, :], 4), ACT.Copy)\
                    .then_inc(out_sem("PT", a), 1)

            def o_upper(c):
                b = wait_full(act, "O", c)
                nc.scalar.activation(half_hi[:, c, :], b[:, 0:T], ACT.Copy).then_inc(o_hi, 1)

            for a in range(ATT + 4):
                if a < ATT:
                    exp_tile(a)
                if a % 2 == 0 and 2 <= a <= ATT:
                    mod_rows_out(8 + (a - 2) // 2)
                if a % 4 == 3 and a >= 7:
                    o_upper((a - 7) // 4)
                if 1 <= a <= ATT:
                    turn_tile(a - 1)
                if a % 2 == 1 and a < ATT:
                    ahead(U["mod2"] + a // 2)
            ahead(U["wout"])
            act.wait_ge(mem_in, 16)
            for k in range(KC):
                square("mem", k, mem_x[:, k, :])
            ahead(U["wout"] + 1)
            root("mem")
            ahead(U["wout"] + 2)
            upper("mem")
            ahead(U["wout"] + 3)
            for k in range(KC):
                wait_out(act, "wout", k)
                square("ffn", k, x[:, k, :])
            ahead(U["mk"])
            for j in range(2):
                copy_out(xk[:, j, :], "mk", j)
            root("ffn")
            ahead(U["mk"] + 1)
            upper("ffn", 3)
            for j in range(2, 4):
                copy_out(xk[:, j, :], "mk", j)
            ahead(U["mk"] + 2)
            act.wait_ge(exp_in, 1)
            nc.scalar.activation(route[:, :, 32:40], route[:, :, 24:32], ACT.Exp).then_inc(exp_out, 1)
            for j in range(4, 7):
                copy_out(xk[:, j, :], "mk", j)
            copy_out_q(xk[:, 7, :], "mk", 7)
            ahead(U["moe"])
            for j in range(EXPERTS // 2):
                copy_out(comb_all[:, 2 * j:2 * j + 2, :].rearrange("p e n -> p (e n)"), "comb", j, w=512)

            def split_in_loop(i, units, downs, blocks, n):
                act.wait_ge(raw_in[n % RAW], i * (16 * units // RAW) + 16 * (n // RAW + 1))
                if UNIT_END[n - SPLIT] is None:
                    act.wait_ge(down_used, i * downs + DOWNS_BEFORE[n - SPLIT])
                else:
                    b = R_AT[UNIT_END[n - SPLIT]]
                    act.wait_ge(r_full[b % 4], i * (blocks // 4) + (b // 4 + 1))
                nc.scalar.activation(w_hi[:, n % SPLIT, :], raw[:, n % RAW, :], ACT.Copy).then_inc(hi_done, 1)

            def expert(i, e):
                for u in range(6):
                    for s in range(2):
                        if s == 1:
                            split_in_loop(i, 12, 4, 16, U["moe"] + 6 * e + u + SPLIT)
                        f = 2 * (u % 2) + s
                        b = MOE_B + 8 * e + 2 * u + s
                        if u < 2:
                            act.wait_ge(r_full[b % 4], i * 4 + (b // 4 + 1))
                            nc.scalar.activation(gate_f[:, f, :], R[b % 4][:, 0:T], ACT.Silu).then_inc(r_out[b % 4], 1)
                        elif u < 4:
                            act.wait_ge(r_out[b % 4], i * 4 + (b // 4 + 1))
                            nc.scalar.activation(hid_hi[:, f, :], hid_f[:, f, :], ACT.Copy).then_inc(hid_hi_s, 1)

            with act.Fori(0, EXPERTS // 2) as i:
                expert(i, 0)
                expert(i, 1)
            next_unit[0] = U["moe"] + 6 * EXPERTS + SPLIT
            def values_out(u):
                for t in range(TT):
                    copy_out(x_v[:, t, T * u:T * u + T], "mv", u, t)

            ahead(U["mv"])
            for k in range(KC):
                act.wait_ge(y_out, k + 1)
                square("final", k, x[:, k, :])
            values_out(0)
            ahead(U["mv"] + 1)
            values_out(1)
            root("final")
            ahead(U["mv"] + 2)
            for k in range(KC):
                act.wait_ge(scaled, CHUNK0["final"] + k + 1)
                square("mix", k, x[:, k, :])
            values_out(2)
            ahead(U["mv"] + 3)
            values_out(3)
            root("mix")
            upper("mix")

            def part_out(part, dst, func=ACT.Copy, merged_before=None, blocks=range(KC)):
                for j in blocks:
                    ahead(U[part] + j // 2)
                    if merged_before is not None:
                        act.wait_ge(merge_done, merged_before + j + 1)
                    copy_out(dst[:, j, :], part, j, func=func)

            part_out("c_h", buf_a)
            ahead(U["c_c"] + 3)
            for j in range(KC):
                ahead(U["c_b"] + j // 2)
                wait_out(act, "c_b", j)
                nc.scalar.activation(other_hi[:, j, :], buf_c[:, j, :], ACT.Copy).then_inc(cb_hi, 1)
            part_out("gate0", buf_b, ACT.Sigmoid)
            part_out("conv_out", buf_a)
            part_out("sq", buf_a, merged_before=0)
            part_out("sk", buf_b)
            for u in range(4):
                for t in range(TT):
                    ahead(U["sv"] + u)
                    copy_out(sb_v[:, t, T * u:T * u + T], "sv", u, t)
            ahead(U["xq"])
            act.preload_act_table_set("natural_log_exp_and_others")
            for g in range(SB_HEADS + 3):
                if g < SB_HEADS:
                    h = g
                    act.wait_ge(z_abs, h + 1)
                    nc.scalar.activation(lnb[:, h % 2, :], lnb[:, h % 2, :], ACT.Exp, scale=-1.0).then_inc(act_step, 1)
                    act.wait_ge(act_step, h + 1)
                    nc.scalar.activation(lnb[:, h % 2, :], lnb[:, h % 2, :], ACT.Ln, bias=ones[:, 0:1]).then_inc(z_ln, 1)
                if 2 <= g < SB_HEADS + 2:
                    h = g - 2
                    wait_out(act, "rc", h)
                    nc.scalar.activation(att[:, h % 2, :], att[:, h % 2, :], ACT.Exp).then_inc(z_exp, 1)
                if g - 1 in XQ_AT:
                    j = XQ_AT[g - 1]
                    copy_out_q(xq[:, j, :], "xq", j)
                    if j % 2 == 1:
                        ahead(U["xq"] + j // 2 + 1)
                if g % 2 == 1 and g >= 5:
                    c = (g - 5) // 2
                    b = wait_full(act, "sbo", c)
                    nc.scalar.activation(other_hi[:, c, :], b[:, 0:T], ACT.Copy).then_inc(o_hi, 1)
            b = wait_full(act, "sbo", 7)
            nc.scalar.activation(other_hi[:, 7, :], b[:, 0:T], ACT.Copy).then_inc(o_hi, 1)

            def head_square(src, j):
                nc.scalar.activation(x_sq[:, j, :], src[:, j, :], ACT.Square).then_inc(head_sq, 1)

            def head_root(key, h, which):
                b = wait_full(act, key, h)
                nc.scalar.activation(x_rt[which][:, h, :], b[:, 0:T], ACT.Sqrt, bias=const("eps"),
                                     scale=1.0 / X_DIM).then_inc(out_sem(key, h), 1)

            for j in range(KC):
                head_square(xk, j)
            for j in range(KC):
                ahead(U["sb_out"] + j // 2)
                copy_out(buf_a[:, j, :], "sb_out", j)
                if j >= 4:
                    head_root("ssk", j - 4, 0)
                    wait_qout(act, "xq", 2 * (j - 4) + 1)
                    for c in range(2 * (j - 4), 2 * (j - 4) + 2):
                        head_square(xq, c)
            for j in range(KC):
                ahead(U["gate1"] + j // 2)
                copy_out(buf_b[:, j, :], "gate1", j, func=ACT.Sigmoid)
            ahead(U["gate2"])
            for h in range(X_HEADS):
                head_root("ssq", h, 1)
            part_out("gate2", buf_c, ACT.Sigmoid, blocks=range(4))
            for h in range(X_HEADS):
                act.wait_ge(x_negmax, h + 1)
                s = Q[Q_AT[("XS", h)] % 4]
                for t in range(TT):
                    if h >= 2 and t == 0:
                        wait_full(act, "XP", h - 2)
                    ins = nc.scalar.activation(x_p[:, h % 2, T * t:T * t + T], s[:, T * t:T * t + T], ACT.Exp,
                                               bias=stat[:, 10 + t:11 + t], scale=X_DIM ** -0.5,
                                               accum_out=stat[:, 12 + t:13 + t])
                ins.then_inc(qout_sem("XS", h), 1)
                ahead(U["gate2"] + (4 + h) // 2)
                copy_out(buf_c[:, 4 + h, :], "gate2", 4 + h)
                b = wait_full(act, "XP", h)
                if h >= 2:
                    wait_full(act, "XO", h - 2)
                nc.scalar.activation(x_pt[:, h % 2, :], b[:, :], ACT.Copy).then_inc(out_sem("XP", h), 1)
                if h >= 1:
                    b = wait_full(act, "XO", h - 1)
                    nc.scalar.activation(other_hi[:, 2 * h - 2:2 * h, :], chunks(b[:, :], 2), ACT.Copy).then_inc(xo_hi, 1)
            b = wait_full(act, "XO", 3)
            nc.scalar.activation(other_hi[:, 6:8, :], chunks(b[:, :], 2), ACT.Copy).then_inc(xo_hi, 1)
            for j in range(4, KC):
                wait_out(act, "gate2", j)
                nc.scalar.activation(buf_c[:, j, :], buf_c[:, j, :], ACT.Sigmoid).then_inc(gate2_done, 1)
            part_out("x_out", buf_a, merged_before=KC)
            ahead(U["out"])
            for j in range(KC):
                act.wait_ge(merge_done, 2 * KC + j + 1)
                nc.scalar.activation(half_hi[:, j, :], merged[:, j, :], ACT.Copy).then_inc(mg_hi, 1)
            ahead(U["out"] + 3)
            for k in range(KC):
                wait_out(act, "out", k)
                square("mlp", k, x[:, k, :])
            root("mlp")
            upper("mlp")

            def slab(i, last=False):
                for u in range(4):
                    for s in range(2):
                        if s == 1 and not (last and u >= 2):
                            split_in_loop(i, 4, 2, 4, U["mlp"] + u + SPLIT)
                        f = 2 * u + s
                        if u < 2:
                            b = MLP_B + f
                            act.wait_ge(r_full[b % 4], i + (b // 4 + 1))
                            nc.scalar.activation(gate_f[:, f, :], R[b % 4][:, 0:T], ACT.Relu).then_inc(gated, 1)
                            act.wait_ge(r_out[b % 4], i + (b // 4 + 1))
                            nc.scalar.activation(hid_hi[:, f, :], hid_f[:, f, :], ACT.Copy).then_inc(hid_hi_s, 1)

            ahead(U["mlp"])
            with act.Fori(0, SLABS - 1) as i:
                slab(i)
            slab(SLABS - 1, last=True)

        @block.vector
        def _(dve):
            next_unit, step = [0], [0]

            def link(ins):
                step[0] += 1
                ins.then_inc(dve_step, 1)
                dve.wait_ge(dve_step, step[0])

            def split(n):
                dve.wait_ge(hi_done, n + 1)
                nc.vector.tensor_tensor(w_lo[:, n % SPLIT, :], raw[:, n % RAW, :], w_hi[:, n % SPLIT, :].bitcast(f32),
                                        ALU.subtract).then_inc(lo_done, 1)

            def ahead(n):
                while next_unit[0] <= min(n + 1, UNITS - 1):
                    split(next_unit[0])
                    next_unit[0] += 1

            def lower(dst, src, hi):
                return nc.vector.tensor_tensor(dst, src, hi.bitcast(f32), ALU.subtract)

            def invert_root(name):
                r = rt[:, NORM_NAMES.index(name) % 2, 0:NORMS[name][1]]
                wait_out(dve, "ss", name)
                link(nc.vector.reciprocal(r, r))

            def scale_and_split(name, src, gain_of, shift=None, inverted=False):
                kc, w, _ = NORMS[name]
                f, hi, lo = norm_io(name)
                r = rt[:, NORM_NAMES.index(name) % 2, 0:w]
                if not inverted:
                    invert_root(name)
                for k in range(kc + 1):
                    if k < kc and name == "ctx_x":
                        for s in range(2):
                            ins = nc.vector.scalar_tensor_tensor(
                                out=f[:, k, T * s:T * s + T], in0=(x, c2)[s][:, k, :], scalar=gain[:, 0, k, s:s + 1],
                                in1=r[:, T * s:T * s + T], op0=ALU.mult, op1=ALU.mult)
                        ins.then_inc(scaled, 1)
                    elif k < kc:
                        dst = x[:, k, :] if name == "final" else f[:, k, :]
                        nc.vector.scalar_tensor_tensor(out=dst, in0=src[:, k, :], scalar=gain_of(k), in1=r,
                                                       op0=ALU.mult, op1=ALU.mult).then_inc(scaled, 1)
                    if k >= 1 and name != "final":
                        j = k - 1
                        dve.wait_ge(part_hi, PART0[name] + j + 1)
                        if shift is None:
                            ins = lower(lo[:, j, :], f[:, j, :], hi[:, j, :])
                        elif name == "ctx_x":
                            for s in range(2):
                                c = slice(T * s, T * s + T)
                                ins = nc.vector.scalar_tensor_tensor(
                                    out=lo[:, j, c], in0=f[:, j, c], scalar=mod[:, shift, j, s:s + 1],
                                    in1=hi[:, j, c].bitcast(f32), op0=ALU.add, op1=ALU.subtract)
                        else:
                            ins = nc.vector.scalar_tensor_tensor(
                                out=lo[:, j, :], in0=f[:, j, :], scalar=mod[:, shift, j, 0:1],
                                in1=hi[:, j, :].bitcast(f32), op0=ALU.add, op1=ALU.subtract)
                        ins.then_inc(part_lo, 1)

            def mod_out(u):
                g, k = u // 4, 2 * (u % 4)
                b = wait_full(dve, "mod", u)
                bias = col("b_mod")[:, 2 * u:2 * u + 2].unsqueeze(2).to_broadcast([P, 2, 2])
                nc.vector.tensor_tensor(mod[:, g, k:k + 2, :], chunks(b[:, T:T + 4], 2), bias, ALU.add)\
                    .then_inc(out_sem("mod", u), 1)

            def gains(which, g, name):
                for u in range(4 * g, 4 * g + 4):
                    wait_out(dve, "mod", u)
                gb = col(name).unsqueeze(2).to_broadcast([P, KC, 2])
                link(nc.vector.scalar_tensor_tensor(out=gain[:, which, :, :], in0=mod[:, g, :, :], scalar=1.0, in1=gb,
                                                    op0=ALU.add, op1=ALU.mult))

            dve.wait_ge(cond_step, 2)
            lower(cond_lo.rearrange("p k (s n) -> p (k s) n", s=2),
                  cond_s[:, :].unsqueeze(2).to_broadcast([P, 16, 64]),
                  cond_hi.rearrange("p k (s n) -> p (k s) n", s=2)).then_inc(cond_ready, 1)
            dve.wait_ge(cond_step, 3)
            lower(wr_lo[:, :], col("w_r"), wr_hi[:, :]).then_inc(cond_ready, 1)
            for u in range(8):
                ahead(U["mod"] + min(u + 1, 7))
                mod_out(u)
                if u == 4:
                    invert_root("ctx_x")
            gains(0, 1, "attn_g")
            scale_and_split("ctx_x", None, None, 0, inverted=True)

            ahead(U["lat"] + 3)
            b = wait_full(dve, "lat", 5)
            nc.vector.tensor_tensor(kr, b[:, :], const("cos"), ALU.mult).then_inc(out_sem("lat", 5), 1)
            b = wait_full(dve, "lat", 6)
            nc.vector.tensor_tensor(rot, b[:, :], const("sin"), ALU.mult).then_inc(out_sem("lat", 6), 1)
            wait_out(dve, "lat", 5)
            wait_out(dve, "lat", 6)
            nc.vector.tensor_tensor(kr, kr, rot, ALU.add).then_inc(kr_ready, 1)
            for part in ("naq", "nak", "nav"):
                ahead(U[part] + 1)
                if part == "naq":
                    invert_root("qa")
                if part == "nak":
                    invert_root("kva")
            scale_and_split("qa", qlat, lambda k: col("q_a_g", k), inverted=True)
            scale_and_split("kva", kvlat, lambda k: col("kv_a_g", k), inverted=True)
            ahead(U["uq"] + 1)
            for j in range(2):
                b = wait_full(dve, "q", 4 + j)
                nc.vector.tensor_tensor(qr[:, j, :], b[:, 0:T], const("cos")[:, 0:T], ALU.mult)\
                    .then_inc(out_sem("q", 4 + j), 1)
            for j in range(2):
                b = wait_full(dve, "q", 6 + j)
                nc.vector.tensor_tensor(rot[:, T * j:T * j + T], b[:, 0:T], const("sin")[:, 0:T], ALU.mult)\
                    .then_inc(out_sem("q", 6 + j), 1)
            for j in range(2):
                wait_out(dve, "q", 4 + j)
                wait_out(dve, "q", 6 + j)
                nc.vector.tensor_tensor(qr[:, j, :], qr[:, j, :], rot[:, T * j:T * j + T], ALU.add)\
                    .then_inc(qr_ready, 1)
            ahead(U["ukv"])

            def tile_max(a):
                b = wait_qfull(dve, "S", a)
                mx, nm = stat[:, a % 2:a % 2 + 1], stat[:, 2 + a % 2:3 + a % 2]
                if a < ATT_MLA:
                    link(nc.vector.reduce_max(mx, b[:, :], AX.X))
                    nc.vector.tensor_scalar(nm, mx, -(NOPE + ROPE) ** -0.5, None, ALU.mult).then_inc(negmax_ready, 1)
                else:
                    if a == ATT_MLA:
                        dve.wait_ge(biased, 2)
                    p = probs(a)
                    if a >= ATT_MLA + 4:
                        wait_full(dve, "PT", a - 4)
                    nc.vector.scalar_tensor_tensor(out=p[:, 0:T], in0=b[:, 0:T], scalar=NA_DIM ** -0.5,
                                                   in1=na_bias[a % 2][:, a // 2 - HEADS, :], op0=ALU.mult, op1=ALU.add)
                    nc.vector.tensor_scalar(p[:, T:512], b[:, T:512], NA_DIM ** -0.5, None, ALU.mult)\
                        .then_inc(qout_sem("S", a), 1)
                    wait_qout(dve, "S", a)
                    link(nc.vector.reduce_max(mx, p, AX.X))
                    nc.vector.tensor_scalar(nm, mx, -1.0, None, ALU.mult).then_inc(negmax_ready, 1)

            def tile_scale(a):
                if a < ATT_MLA:
                    wait_qout(dve, "S", a)
                else:
                    dve.wait_ge(na_exp, a - ATT_MLA + 1)
                s, p = stat[:, 4 + a % 2:5 + a % 2], probs(a)
                link(nc.vector.reciprocal(s, s))
                nc.vector.tensor_scalar(p, p, s, None, ALU.mult).then_inc(probs_ready, 1)

            for a in range(ATT + 4):
                if a < ATT:
                    tile_max(a)
                if 1 <= a <= ATT:
                    tile_scale(a - 1)
                if a % 2 == 1 and 3 <= a <= ATT + 1:
                    mod_out(8 + (a - 3) // 2)
                if a % 4 == 3 and a >= 7:
                    c = (a - 7) // 4
                    dve.wait_ge(o_hi, c + 1)
                    b = wait_full(dve, "O", c)
                    lower(half_lo[:, c, :], b[:, 0:T], half_hi[:, c, :]).then_inc(out_sem("O", c), 1)
                if a % 2 == 0 and 2 <= a <= ATT:
                    ahead(U["mod2"] + a // 2 - 1)
            gains(1, 4, "ffn_g")
            for j in range(KC):
                if j == 4:
                    ahead(U["wout"] + 2)
                    scale_and_split("mem", mem_x, lambda k: col("mem_g", k))
                ahead(U["wout"] + j // 2)
                b = wait_full(dve, "wout", j)
                nc.vector.scalar_tensor_tensor(out=x[:, j, :], in0=b[:, 0:T], scalar=mod[:, 2, j, 0:1], in1=x[:, j, :],
                                               op0=ALU.mult, op1=ALU.add).then_inc(out_sem("wout", j), 1)
            for j in range(KC):
                wait_out(dve, "wout", j)
            ahead(U["mk"])
            scale_and_split("ffn", x, lambda k: gain[:, 1, k, 0:1], 3)
            ahead(U["mk"] + 2)

            def rv(lo, w):
                return route[:, :, lo:lo + w]

            def wide(ap, w):
                return ap.to_broadcast([P, TT, w])

            prio = const("prio").unsqueeze(1).to_broadcast([P, TT, 4])

            def largest(val, mx, eq, one):
                link(nc.vector.reduce_max(mx, val, AX.X))
                link(nc.vector.tensor_tensor(eq, val, wide(mx, 4), ALU.is_equal))
                link(nc.vector.tensor_tensor(eq, eq, prio, ALU.mult))
                link(nc.vector.reduce_max(rv(120, 1), eq, AX.X))
                link(nc.vector.tensor_tensor(one, eq, wide(rv(120, 1), 4), ALU.is_equal))

            logits, g_hot, g_max = rv(0, 20), rv(48, 4), rv(121, 1)
            e_sel, e_max, hot1, hot2, top1, top2 = rv(52, 4), rv(122, 1), rv(56, 4), rv(60, 4), rv(123, 1), rv(124, 1)
            scr, comb = rv(64, 16), rv(80, 16)
            b = wait_full(dve, "logits")
            nc.vector.tensor_tensor(logits, chunks(b[:, 0:40], TT), col("b_r").unsqueeze(1).to_broadcast([P, TT, 20]),
                                    ALU.add).then_inc(out_sem("logits"), 1)
            wait_out(dve, "logits")
            largest(rv(0, 4), g_max, rv(100, 4), g_hot)
            for g in range(GROUPS):
                link(nc.vector.tensor_tensor(scr[:, :, 4 * g:4 * g + 4], rv(4 + 4 * g, 4), wide(g_hot[:, :, g:g + 1], 4),
                                             ALU.mult))
            link(nc.vector.reduce_sum(e_sel, scr.rearrange("p t (g e) -> p t e g", g=GROUPS), AX.X))
            link(nc.vector.reduce_max(e_max, e_sel, AX.X))
            link(nc.vector.tensor_tensor(rv(24, 4), rv(0, 4), wide(g_max, 4), ALU.subtract))
            nc.vector.tensor_tensor(rv(28, 4), e_sel, wide(e_max, 4), ALU.subtract).then_inc(exp_in, 1)
            dve.wait_ge(exp_out, 1)
            sums = rv(40, 2)
            link(nc.vector.reduce_sum(sums, rv(32, 8).rearrange("p t (s e) -> p t s e", s=2), AX.X))
            link(nc.vector.reciprocal(sums, sums))
            prob, prob2 = rv(104, 4), rv(108, 4)
            link(nc.vector.tensor_tensor(prob, rv(36, 4), wide(rv(41, 1), 4), ALU.mult))
            largest(prob, top1, rv(100, 4), hot1)
            link(nc.vector.scalar_tensor_tensor(out=prob2, in0=hot1, scalar=-2.0, in1=prob, op0=ALU.mult, op1=ALU.add))
            largest(prob2, top2, rv(100, 4), hot2)
            link(nc.vector.tensor_tensor(hot1, hot1, wide(top1, 4), ALU.mult))
            link(nc.vector.tensor_tensor(hot2, hot2, wide(top2, 4), ALU.mult))
            link(nc.vector.tensor_tensor(hot1, hot1, hot2, ALU.add))
            link(nc.vector.tensor_tensor(top1, top1, top2, ALU.add))
            link(nc.vector.reciprocal(top1, top1))
            link(nc.vector.tensor_tensor(hot1, hot1, wide(top1, 4), ALU.mult))
            link(nc.vector.tensor_tensor(hot1, hot1, wide(rv(40, 1), 4), ALU.mult))
            for g in range(GROUPS):
                ins = nc.vector.tensor_tensor(comb[:, :, 4 * g:4 * g + 4], hot1, wide(g_hot[:, :, g:g + 1], 4), ALU.mult)
            ins.then_inc(comb_ready, 1)
            ahead(U["moe"])

            def split_in_loop(i, units, n):
                dve.wait_ge(hi_done, i * units + (n + 1))
                nc.vector.tensor_tensor(w_lo[:, n % SPLIT, :], raw[:, n % RAW, :], w_hi[:, n % SPLIT, :].bitcast(f32),
                                        ALU.subtract).then_inc(lo_done, 1)

            def expert(i, e):
                for u in range(6):
                    for s in range(2):
                        f = 2 * (u % 2) + s
                        b = MOE_B + 8 * e + 2 * u + s
                        if 2 <= u < 4:
                            dve.wait_ge(gated, i * 8 + (4 * e + f + 1))
                            dve.wait_ge(r_full[b % 4], i * 4 + (b // 4 + 1))
                            nc.vector.tensor_tensor(hid_f[:, f, :], R[b % 4][:, 0:T], gate_f[:, f, :], ALU.mult)\
                                .then_inc(r_out[b % 4], 1)
                        if s == 1:
                            split_in_loop(i, 12, U["moe"] + 6 * e + u + SPLIT)
                        if 2 <= u < 4:
                            dve.wait_ge(hid_hi_s, i * 8 + (4 * e + f + 1))
                            lower(hid_lo[:, f, :], hid_f[:, f, :], hid_hi[:, f, :]).then_inc(hid_lo_s, 1)

            with dve.Fori(0, EXPERTS // 2) as i:
                expert(i, 0)
                expert(i, 1)
            next_unit[0] = U["moe"] + 6 * EXPERTS + SPLIT
            ahead(U["mv"])
            for m in range(KC):
                dve.wait_ge(y_full, m // 2 + 1)
                nc.vector.scalar_tensor_tensor(out=x[:, m, :], in0=Q[m // 2][:, T * (m % 2):T * (m % 2) + T],
                                               scalar=mod[:, 5, m, 0:1], in1=x[:, m, :], op0=ALU.mult, op1=ALU.add)\
                    .then_inc(y_out, 1)
            ahead(U["mv"] + 1)
            scale_and_split("final", x, lambda k: col("final_g", k))
            ahead(U["mv"] + 3)
            scale_and_split("mix", x, lambda k: col("mix_g", k))
            ahead(U["c_h"] + 3)
            for j in range(KC):
                ahead(U["c_c"] + j // 2)
                wait_out(dve, "c_h", j)
                b = wait_full(dve, "c_c", j)
                nc.vector.tensor_tensor(buf_b[:, j, :], b[:, 0:T], buf_a[:, j, :], ALU.mult)\
                    .then_inc(out_sem("c_c", j), 1)
                wait_out(dve, "c_c", j)
                link(nc.vector.tensor_scalar(buf_c[:, j, :], buf_b[:, j, :], col("conv", 16 + j), None, ALU.mult))
                for lag in (1, 2):
                    link(nc.vector.scalar_tensor_tensor(
                        out=buf_c[:, j, lag:T], in0=buf_b[:, j, 0:T - lag], scalar=col("conv", 8 * (2 - lag) + j),
                        in1=buf_c[:, j, lag:T], op0=ALU.mult, op1=ALU.add))
            for j in range(KC):
                ahead(U["c_b"] + j // 2)
                b = wait_full(dve, "c_b", j)
                nc.vector.tensor_tensor(buf_c[:, j, :], b[:, 0:T], buf_c[:, j, :], ALU.mult)\
                    .then_inc(out_sem("c_b", j), 1)
                dve.wait_ge(cb_hi, j + 1)
                lower(other_lo[:, j, :], buf_c[:, j, :], other_hi[:, j, :]).then_inc(cb_lo, 1)
            for part in ("gate0", "conv_out", "sq", "sk", "sv"):
                ahead(U[part] + 3)
            ahead(U["xq"])
            for g in range(SB_HEADS + 3):
                if g < SB_HEADS:
                    h = g
                    if h >= 3:
                        wait_out(dve, "rc", h - 3)
                    b = wait_qfull(dve, "z", h)
                    nc.vector.scalar_tensor_tensor(out=zm[:, h % 3, :], in0=b[:, 0:384], scalar=SB_DIM ** -0.5,
                                                   in1=const("sb_mask"), op0=ALU.mult, op1=ALU.add)\
                        .then_inc(qout_sem("z", h), 1)
                    wait_qout(dve, "z", h)
                    nc.vector.scalar_tensor_tensor(out=lnb[:, h % 2, :], in0=zm[:, h % 3, :], scalar=-1.0,
                                                   in1=zm[:, h % 3, :], op0=ALU.mult, op1=ALU.max).then_inc(z_abs, 1)
                if 1 <= g <= SB_HEADS:
                    h = g - 1
                    dve.wait_ge(z_ln, h + 1)
                    nc.vector.scalar_tensor_tensor(out=spl[:, h % 2, :], in0=zm[:, h % 3, :], scalar=0.0,
                                                   in1=lnb[:, h % 2, :], op0=ALU.max, op1=ALU.add).then_inc(z_sp, 1)
                if 2 <= g < SB_HEADS + 2:
                    h = g - 2
                    b = wait_full(dve, "rc", h)
                    if h >= 2 and h % 2 == 0:
                        dve.wait_ge(first_head, HEADS + h // 2)
                    elif h >= 2:
                        wait_full(dve, "sbo", (h - 2) // 2)
                    nc.vector.tensor_tensor(att[:, h % 2, :], zm[:, h % 3, :], b[:, 0:384], ALU.subtract)\
                        .then_inc(out_sem("rc", h), 1)
                if g % 2 == 1 and g >= 5:
                    c = (g - 5) // 2
                    dve.wait_ge(o_hi, HEADS + c + 1)
                    b = wait_full(dve, "sbo", c)
                    lower(other_lo[:, c, :], b[:, 0:T], other_hi[:, c, :]).then_inc(out_sem("sbo", c), 1)
                if g - 2 in XQ_AT and XQ_AT[g - 2] % 2 == 1:
                    ahead(U["xq"] + XQ_AT[g - 2] // 2 + 1)
            ahead(U["sb_out"])
            dve.wait_ge(o_hi, HEADS + 8)
            b = wait_full(dve, "sbo", 7)
            lower(other_lo[:, 7, :], b[:, 0:T], other_hi[:, 7, :]).then_inc(out_sem("sbo", 7), 1)
            ahead(U["sb_out"] + 3)

            def head_scale(key, dst, which, g, h):
                wait_out(dve, key, h)
                link(nc.vector.reciprocal(x_rt[which][:, h, :], x_rt[which][:, h, :]))
                for c in range(2):
                    nc.vector.scalar_tensor_tensor(out=dst[:, 2 * h + c, :], in0=dst[:, 2 * h + c, :],
                                                   scalar=col(g, c), in1=x_rt[which][:, h, :],
                                                   op0=ALU.mult, op1=ALU.mult).then_inc(head_scaled, 1)

            for h in range(X_HEADS):
                head_scale("ssk", xk, 0, "kn_g", h)
                ahead(U["gate1"] + h)
            ahead(U["gate2"])
            for h in range(X_HEADS):
                head_scale("ssq", xq, 1, "qn_g", h)
                if h == 1:
                    ahead(U["gate2"] + 1)

            def x_scale(h):
                wait_qout(dve, "XS", h)
                link(nc.vector.reciprocal(stat[:, 12:14], stat[:, 12:14]))
                for t in range(TT):
                    p = x_p[:, h % 2, T * t:T * t + T]
                    ins = nc.vector.tensor_scalar(p, p, stat[:, 12 + t:13 + t], None, ALU.mult)
                ins.then_inc(x_probs, 1)

            def x_lower(h):
                dve.wait_ge(xo_hi, h + 1)
                b = wait_full(dve, "XO", h)
                lower(other_lo[:, 2 * h:2 * h + 2, :], chunks(b[:, :], 2), other_hi[:, 2 * h:2 * h + 2, :])\
                    .then_inc(out_sem("XO", h), 1)

            for h in range(X_HEADS):
                b = wait_qfull(dve, "XS", h)
                link(nc.vector.reduce_max(stat[:, 8:10], chunks(b[:, :], 2), AX.X))
                nc.vector.tensor_scalar(stat[:, 10:12], stat[:, 8:10], -X_DIM ** -0.5, None, ALU.mult)\
                    .then_inc(x_negmax, 1)
                x_scale(h)
                ahead(U["gate2"] + (4 + h) // 2)
                if h >= 1:
                    x_lower(h - 1)
            x_lower(X_HEADS - 1)
            ahead(U["x_out"] + 3)
            for j in range(KC):
                dve.wait_ge(mg_hi, j + 1)
                lower(half_lo[:, j, :], merged[:, j, :], half_hi[:, j, :]).then_inc(mg_lo, 1)
            for j in range(KC):
                ahead(U["out"] + j // 2)
                b = wait_full(dve, "out", j)
                nc.vector.tensor_tensor(x[:, j, :], b[:, 0:T], x[:, j, :], ALU.add).then_inc(out_sem("out", j), 1)
            for j in range(KC):
                wait_out(dve, "out", j)
            scale_and_split("mlp", x, lambda k: col("mlp_g", k))

            def slab(i, last=False):
                for u in range(4):
                    for s in range(2):
                        f = 2 * u + s
                        if u < 2:
                            b = MLP_B + f
                            dve.wait_ge(r_full[b % 4], i + (b // 4 + 1))
                            dve.wait_ge(gated, i * 4 + (4 * EXPERTS + f + 1))
                            nc.vector.tensor_tensor(hid_f[:, f, :], R[b % 4][:, 0:T], gate_f[:, f, :], ALU.mult)\
                                .then_inc(r_out[b % 4], 1)
                        if s == 1 and not (last and u >= 2):
                            split_in_loop(i, 4, U["mlp"] + u + SPLIT)
                        if u < 2:
                            dve.wait_ge(hid_hi_s, i * 4 + (4 * EXPERTS + f + 1))
                            lower(hid_lo[:, f, :], hid_f[:, f, :], hid_hi[:, f, :]).then_inc(hid_lo_s, 1)

            ahead(U["mlp"])
            with dve.Fori(0, SLABS - 1) as i:
                slab(i)
            slab(SLABS - 1, last=True)
            for m in range(KC):
                dve.wait_ge(y_full, 4 + m // 2 + 1)
                nc.vector.tensor_tensor(x[:, m, :], Q[m // 2][:, T * (m % 2):T * (m % 2) + T], x[:, m, :], ALU.add)\
                    .then_inc(y_out, 1)

        @block.tensor
        def _(pe):
            mm = nc.tensor.matmul
            filled, q_filled = [0], [0]

            def open_block(*key):
                n = filled[0]
                assert R_AT[key] == n, (key, n)
                filled[0] += 1
                if n >= 4:
                    pe.wait_ge(r_out[n % 4], n // 4)
                return R[n % 4]

            def full_sem(*key):
                return r_full[R_AT[key] % 4]

            def open_q(*key):
                n = q_filled[0]
                assert Q_AT[key] == n, (key, n)
                q_filled[0] += 1
                if n >= 4:
                    pe.wait_ge(q_out[n % 4], n // 4)
                return Q[n % 4]

            def w_part(n, at, w=P):
                return w_hi[:, n % SPLIT, at:at + w], w_lo[:, n % SPLIT, at:at + w]

            def three(out, left, right, start, stop, group=True):
                (lh, ll), (rh, rl) = left, right
                mm(out, lh, rh, start=start, stop=False, skip_group_check=not group)
                mm(out, lh, rl, start=False, stop=False, skip_group_check=not group)
                return mm(out, ll, rh, start=False, stop=stop, skip_group_check=not group)

            def t_block(key, n, at, kc, hi, lo, w=T, ready=None):
                b = open_q(*key) if key in Q_AT else open_block(*key)
                for k in range(kc):
                    if ready is not None:
                        ready(k)
                    ins = three(b[:, 0:w], w_part(n, at + k * P), (hi[:, k, 0:w], lo[:, k, 0:w]), k == 0, k == kc - 1)
                ins.then_inc(q_full[Q_AT[key] % 4] if key in Q_AT else full_sem(*key), 1)

            def after_norm(name):
                return lambda k: pe.wait_ge(part_lo, PART0[name] + k + 1)

            def product(part, hi, lo, w=T, ready=None, blocks=range(KC)):
                for j in blocks:
                    n = U[part] + j // 2
                    if j % 2 == 0:
                        pe.wait_ge(lo_done, n + 1)
                    t_block((part, j), n, (j % 2) * KC * P, KC, hi, lo, w, ready if j == 0 else None)

            def rows(part, hi, lo, units, tiles):
                for u in units:
                    n = U[part] + u
                    pe.wait_ge(lo_done, n + 1)
                    for t in range(tiles):
                        b = open_block(part, u, t)
                        for k in range(KC):
                            c = slice(P * t, P * t + P)
                            ins = three(b[:, 0:T], (hi[:, k, c], lo[:, k, c]), w_part(n, k * T, T), k == 0, k == KC - 1)
                        ins.then_inc(full_sem(part, u, t), 1)

            def sum_squares(name):
                kc, w, _ = NORMS[name]
                b = open_block("ss", name)
                for k in range(kc):
                    pe.wait_ge(squared, CHUNK0[name] + k + 1)
                    ins = mm(b[:, 0:w], ones, norm_io(name)[0][:, k, :], start=(k == 0), stop=(k == kc - 1))
                ins.then_inc(full_sem("ss", name), 1)

            def mod_unit(u):
                n = U["mod"] + u if u < 8 else U["mod2"] + u - 8
                pe.wait_ge(lo_done, n + 1)
                b = open_block("mod", u)
                for k in range(KC):
                    ins = three(b[:, 0:T], (cond_hi[:, k, :], cond_lo[:, k, :]), w_part(n, k * T, T), k == 0, k == KC - 1)
                ins.then_inc(mod_filled, 1)

            def mod_turn(u):
                pe.wait_ge(mod_copied, u + 1)
                b = r_bank("mod", u)
                for m in range(2):
                    ins = mm(b[:, T + 2 * m:T + 2 * m + 2], mod_rows[:, u % 2, P * m:P * m + P], ident[:, 0:P:64],
                             start=True, stop=True)
                ins.then_inc(full_sem("mod", u), 1)

            pe.wait_ge(cond_ready, 2)
            for u in range(9):
                if u == 4:
                    sum_squares("ctx_x")
                if u < 8:
                    mod_unit(u)
                if u >= 1:
                    mod_turn(u - 1)
            for j in range(7):
                n = U["lat"] + j // 2
                if j % 2 == 0:
                    pe.wait_ge(lo_done, n + 1)
                t_block(("lat", j), n, (j % 2) * KC * P, KC, h_hi, h_lo, T if j < 3 else 512,
                        after_norm("ctx_x") if j == 0 else None)
            product("naq", h_hi, h_lo, blocks=range(4))
            sum_squares("qa")
            sum_squares("kva")
            product("nak", h_hi, h_lo, w=512, blocks=range(4))
            rows("nav", h_hi, h_lo, range(2), 4)
            for j in range(8):
                n = U["uq"] + j // 4
                if j % 4 == 0:
                    pe.wait_ge(lo_done, n + 1)
                t_block(("q", j), n, (j % 4) * QC * P, QC, qa_hi, qa_lo, ready=after_norm("qa") if j == 0 else None)
            n = U["ukv"]
            pe.wait_ge(lo_done, n + 1)
            for j in range(4):
                t_block(("kn", j), n, j * KVC * P, KVC, kva_hi, kva_lo, 512, after_norm("kva") if j == 0 else None)
            for t in range(4):
                b = open_block("v", t)
                for k in range(KVC):
                    c = slice(P * t, P * t + P)
                    ins = three(b[:, :], (kva_hi[:, k, c], kva_lo[:, k, c]), w_part(n, 1024 + 512 * k, 512),
                                k == 0, k == KVC - 1)
                ins.then_inc(full_sem("v", t), 1)

            def scores(a):
                h, q = a // 2, slice(P * (a % 2), P * (a % 2) + P)
                b = open_q("S", a)
                if a < ATT_MLA:
                    n_, r_ = slice(64 * (h % 2), 64 * (h % 2) + 64), slice(32 * (h % 4), 32 * (h % 4) + 32)
                    mm(b[:, :], qn[n_, h // 2, q], kn[n_, h // 2, :], start=True, stop=False)
                    ins = mm(b[:, :], qr[r_, h // 4, q], kr[r_, :], start=False, stop=True)
                else:
                    h -= HEADS
                    n_ = slice(64 * (h % 2), 64 * (h % 2) + 64)
                    ins = mm(b[:, :], naq[n_, h // 2, q], nak[n_, h // 2, :], start=True, stop=True)
                ins.then_inc(q_full[Q_AT[("S", a)] % 4], 1)

            def weigh_values(h):
                v = vm if h < HEADS else nav
                b = open_block("O", h // 2) if h % 2 == 0 else r_bank("O", h // 2)
                wait_out(pe, "PT", 2 * h)
                wait_out(pe, "PT", 2 * h + 1)
                hv, ph = (h % HEADS) * VDIM, 64 * (h % 2)
                for kt in range(4):
                    ins = mm(b[ph:ph + 64, 0:T], v[:, kt, hv:hv + VDIM], probs_t[h % 2][:, kt, :],
                             start=(kt == 0), stop=(kt == 3))
                ins.then_inc(first_head if h % 2 == 0 else full_sem("O", h // 2), 1)

            for j in range(4):
                wait_out(pe, "q", j)
                wait_out(pe, "kn", j)
            for t in range(4):
                wait_out(pe, "v", t)
            pe.wait_ge(kr_ready, 1)
            pe.wait_ge(qr_ready, 2)
            for a in range(LEAD):
                scores(a)
            for a in range(ATT + 2):
                if a + LEAD < ATT:
                    scores(a + LEAD)
                if a < ATT:
                    pe.wait_ge(probs_ready, a + 1)
                    b = open_block("PT", a)
                    for kt in range(4):
                        ins = nc.tensor.transpose(b[:, P * kt:P * kt + P], probs(a)[:, P * kt:P * kt + P], ident)
                    ins.then_inc(full_sem("PT", a), 1)
                    if a % 2 == 0:
                        mod_unit(8 + a // 2)
                if a % 2 == 1 and a >= 3:
                    weigh_values((a - 3) // 2)
                if a % 2 == 1 and a < ATT:
                    mod_turn(8 + a // 2)

            def after_heads(k):
                wait_out(pe, "O", k)

            product("wout", half_hi, half_lo, ready=after_heads, blocks=range(4))
            sum_squares("mem")
            product("wout", half_hi, half_lo, blocks=range(4, 8))
            product("mk", mem_hi, mem_lo, ready=after_norm("mem"), blocks=range(2))
            sum_squares("ffn")
            product("mk", mem_hi, mem_lo, blocks=range(2, 4))
            b = open_block("logits")
            for t in range(TT):
                for k in range(KC):
                    if t == 0:
                        after_norm("ffn")(k)
                    c = slice(P * t, P * t + P)
                    ins = three(b[:, 20 * t:20 * t + 20], (half_hi[:, k, c], half_lo[:, k, c]),
                                (wr_hi[:, 20 * k:20 * k + 20], wr_lo[:, 20 * k:20 * k + 20]), k == 0, k == KC - 1)
            ins.then_inc(full_sem("logits"), 1)
            product("mk", mem_hi, mem_lo, blocks=range(4, 8))
            pe.wait_ge(comb_ready, 1)
            for j in range(EXPERTS // 2):
                b = open_block("comb", j)
                for e in range(2):
                    for t in range(TT):
                        weight = route[:, t, 80 + 2 * j + e:81 + 2 * j + e].to_broadcast([P, P])
                        ins = mm(b[:, T * e + P * t:T * e + P * t + P], weight, ident, start=True, stop=True)
                ins.then_inc(full_sem("comb", j), 1)

            def clear_y():
                for m in range(4):
                    mm(Q[m][:, :], ident, zero.to_broadcast([P, 512]), start=True, stop=False, skip_group_check=True)

            def close_y():
                for m in range(4):
                    mm(Q[m][:, :], ident, zero.to_broadcast([P, 512]), start=False, stop=True, skip_group_check=True)\
                        .then_inc(y_full, 1)

            def hidden_unit(n, u, i, units, blocks, b0):
                pe.wait_ge(lo_done, i * units + (n + 1))
                for s in range(2):
                    b = b0 + s
                    pe.wait_ge(r_out[b % 4], i * (blocks // 4) + b // 4)
                    for k in range(KC):
                        ins = three(R[b % 4][:, 0:T], w_part(n, (s * KC + k) * P), (half_hi[:, k, :], half_lo[:, k, :]),
                                    k == 0, k == KC - 1)
                    ins.then_inc(r_full[b % 4], 1)

            def down_unit(n, u, i, units, hid, h0):
                pe.wait_ge(lo_done, i * units + (n + 1))
                for c in range(2):
                    f = 2 * u + c
                    pe.wait_ge(hid_lo_s, i * hid + (h0 + f + 1))
                    for m in range(KC):
                        ins = three(Q[m // 2][:, T * (m % 2):T * (m % 2) + T], w_part(n, (c * KC + m) * P),
                                    (hid_hi[:, f, :], hid_lo[:, f, :]), False, False, group=False)
                ins.then_inc(down_used, 1)

            wait_qout(pe, "mk", 7)
            clear_y()
            with pe.Fori(0, EXPERTS // 2) as i:
                for e in range(2):
                    n = U["moe"] + 6 * e
                    for u in range(4):
                        hidden_unit(n + u, u, i, 12, 16, MOE_B + 8 * e + 2 * u)
                    for u in range(2):
                        down_unit(n + 4 + u, u, i, 12, 8, 4 * e)
            filled[0] += 8 * EXPERTS
            close_y()
            rows("mv", mem_hi, mem_lo, range(2), TT)
            sum_squares("final")
            rows("mv", mem_hi, mem_lo, range(2, 4), TT)
            sum_squares("mix")
            product("c_h", half_hi, half_lo, ready=after_norm("mix"))
            product("c_c", half_hi, half_lo)
            product("c_b", half_hi, half_lo)
            product("gate0", half_hi, half_lo)
            product("conv_out", other_hi, other_lo, ready=lambda k: pe.wait_ge(cb_lo, k + 1))
            for part in ("sq", "sk"):
                product(part, half_hi, half_lo)
            rows("sv", half_hi, half_lo, range(4), TT)

            def z_scores(h):
                ph, c = slice(64 * (h % 2), 64 * (h % 2) + 64), h // 2
                b = open_q("z", h)
                mm(b[:, 0:256], buf_b[ph, c, 0:P], buf_a[ph, c, :], start=True, stop=True)
                mm(b[:, 256:384], buf_b[ph, c, P:T], buf_a[ph, c, P:T], start=True, stop=True)\
                    .then_inc(q_full[Q_AT[("z", h)] % 4], 1)

            def later_keys(h):
                pe.wait_ge(z_sp, h + 1)
                b, s = open_block("rc", h), spl[:, h % 2, :]
                mm(b[:, 0:128], tri, s[:, 0:128], start=True, stop=True)
                mm(b[:, 128:256], tri, s[:, 128:256], start=True, stop=False)
                mm(b[:, 128:256], ones, s[:, 256:384], start=False, stop=True)
                mm(b[:, 256:384], tri, s[:, 256:384], start=True, stop=True)\
                    .then_inc(full_sem("rc", h), 1)

            def sb_values(h):
                pe.wait_ge(z_exp, h + 1)
                b = open_block("sbo", h // 2) if h % 2 == 0 else r_bank("sbo", h // 2)
                ph, hv = slice(64 * (h % 2), 64 * (h % 2) + 64), slice(SB_DIM * h, SB_DIM * h + SB_DIM)
                mm(b[ph, 0:128], sb_v[:, 0, hv], att[:, h % 2, 0:128], start=True, stop=True)
                mm(b[ph, 128:256], sb_v[:, 0, hv], att[:, h % 2, 128:256], start=True, stop=False)
                mm(b[ph, 128:256], sb_v[:, 1, hv], att[:, h % 2, 256:384], start=False, stop=True)\
                    .then_inc(first_head if h % 2 == 0 else full_sem("sbo", h // 2), 1)

            for j in range(KC):
                wait_out(pe, "sq", j)
                wait_out(pe, "sk", j)
                wait_out(pe, "sv", j // 2, j % 2)
            z_scores(0)
            for g in range(SB_HEADS + 3):
                if g + 1 < SB_HEADS:
                    z_scores(g + 1)
                if g in XQ_AT:
                    product("xq", half_hi, half_lo, blocks=[XQ_AT[g]])
                if 1 <= g <= SB_HEADS:
                    later_keys(g - 1)
                if g >= 3:
                    sb_values(g - 3)

            def head_squares(key, before, h):
                pe.wait_ge(head_sq, before + 2 * h + 2)
                b = open_block(key, h)
                for c in range(2):
                    ins = mm(b[:, 0:T], ones, x_sq[:, 2 * h + c, :], start=(c == 0), stop=(c == 1))
                ins.then_inc(full_sem(key, h), 1)

            for j in range(KC):
                product("sb_out", other_hi, other_lo, ready=(lambda k: wait_out(pe, "sbo", k)) if j == 0 else None,
                        blocks=[j])
                if j >= 4:
                    head_squares("ssk", 0, j - 4)
            product("gate1", half_hi, half_lo)
            for h in range(X_HEADS):
                head_squares("ssq", KC, h)
            product("gate2", half_hi, half_lo, blocks=range(4))

            def x_scores(h):
                b = open_q("XS", h)
                for t in range(TT):
                    for c in range(2):
                        ins = mm(b[:, T * t:T * t + T], xq[:, 2 * h + c, P * t:P * t + P], xk[:, 2 * h + c, :],
                                 start=(c == 0), stop=(c == 1))
                ins.then_inc(q_full[Q_AT[("XS", h)] % 4], 1)

            for u in range(4):
                for t in range(TT):
                    wait_out(pe, "mv", u, t)
            pe.wait_ge(head_scaled, 2 * KC)
            x_scores(0)
            x_scores(1)
            for g in range(X_HEADS + 1):
                if g < X_HEADS:
                    product("gate2", half_hi, half_lo, blocks=[4 + g])
                    pe.wait_ge(x_probs, g + 1)
                    b = open_block("XP", g)
                    for kt in range(TT):
                        for t in range(TT):
                            ins = nc.tensor.transpose(b[:, T * kt + P * t:T * kt + P * t + P],
                                                      x_p[:, g % 2, T * t + P * kt:T * t + P * kt + P], ident)
                    ins.then_inc(full_sem("XP", g), 1)
                if g + 2 < X_HEADS:
                    x_scores(g + 2)
                if g >= 1:
                    h = g - 1
                    wait_out(pe, "XP", h)
                    b = open_block("XO", h)
                    for c in range(2):
                        for kt in range(TT):
                            at = X_DIM * h + P * c
                            ins = mm(b[:, T * c:T * c + T], x_v[:, kt, at:at + P], x_pt[:, h % 2, T * kt:T * kt + T],
                                     start=(kt == 0), stop=(kt == 1))
                    ins.then_inc(full_sem("XO", h), 1)
            product("x_out", other_hi, other_lo, ready=lambda k: wait_out(pe, "XO", k // 2))
            product("out", half_hi, half_lo, ready=lambda k: pe.wait_ge(mg_lo, k + 1))
            sum_squares("mlp")
            clear_y()
            for k in range(KC):
                after_norm("mlp")(k)
            with pe.Fori(0, SLABS) as i:
                for u in range(2):
                    hidden_unit(U["mlp"] + u, u, i, 4, 4, MLP_B + 2 * u)
                for u in range(2):
                    down_unit(U["mlp"] + 2 + u, u, i, 4, 4, 4 * EXPERTS)
            close_y()


def constants():
    out = np.zeros((P, N_CONST), np.float32)
    out[:, CONST["ident"]] = np.eye(P, dtype=np.float32)
    out[:, CONST["ones"]] = 1.0
    i = np.arange(P)
    out[:, CONST["tri"]] = i[:, None] >= i[None, :]
    pos = np.arange(T)
    half = ROPE // 2
    inv = (np.float32(10000.0) ** (-np.arange(0, half, 2, dtype=np.float32) / np.float32(half))).astype(np.float32)
    ang = np.concatenate([(pos // GRID_W).astype(np.float32)[:, None] * inv,
                          (pos % GRID_W).astype(np.float32)[:, None] * inv], axis=1)
    at = i % half
    sign = np.where(i % ROPE < half, -1.0, 1.0).astype(np.float32)
    cos, sin = np.ones((P, 512), np.float32), np.zeros((P, 512), np.float32)
    cos[:, 0:T] = np.cos(ang).astype(np.float32).T[at]
    sin[:, 0:T] = sign[:, None] * np.sin(ang).astype(np.float32).T[at]
    out[:, CONST["cos"]], out[:, CONST["sin"]] = cos, sin
    diag = np.where(i[:, None] < i[None, :], 0.0, MASKED)
    out[:, CONST["sb_mask"]] = np.concatenate([diag, np.zeros((P, P)), diag], axis=1)
    c = np.arange(GRID_W)
    start = np.clip(c - NA_WIN_W // 2, 0, GRID_W - NA_WIN_W)
    inside = (c[None, :] >= start[:, None]) & (c[None, :] < start[:, None] + NA_WIN_W)
    inside = np.tile(inside, (2, 4)).astype(np.float32)
    out[:, CONST["win"]] = inside
    out[:, CONST["win_neg"]] = np.where(inside > 0, 0.0, MASKED)
    out[:, CONST["prio"]] = np.arange(4, 0, -1)
    out[:, CONST["eps"]] = EPS
    return out


def in_blocks(w, per_unit=2):
    k, n = w.shape
    b = w.reshape(k // P, P, n // P, P).transpose(2, 1, 0, 3).reshape(n // P, P, k)
    units = -(-len(b) // per_unit)
    out = np.zeros((units, P, UNIT), w.dtype)
    for j in range(len(b)):
        u, s = divmod(j, per_unit)
        out[u, :, s * k:(s + 1) * k] = b[j]
    return out


def in_rows(w):
    k, n = w.shape
    return w.reshape(k // P, P, n // T, T).transpose(2, 1, 0, 3).reshape(n // T, P, UNIT)


def in_down(w):
    k, n = w.shape
    return w.reshape(k // (2 * P), 2, P, n).transpose(0, 2, 1, 3).reshape(k // (2 * P), P, UNIT)


def by_feature(v):
    return v.reshape(-1, P).T


def kernel(**inputs):
    import concourse.bacc as bacc
    from concourse.bass_utils import run_bass_kernel_spmd

    a = {k: np.asarray(v) for k, v in inputs.items()}
    f32 = a["x"].dtype
    w_in, w2, w_uq, w_ukv = a["w_in"][0], a["w_in_2"][0], a["w_uq"][0], a["w_ukv"][0]
    half = ROPE // 2
    swapped = np.concatenate([np.arange(half, ROPE), np.arange(half)])
    q_cols = Q_LORA + NA_HEADS * NA_DIM
    k_rope = w_in[:, q_cols + KV_LORA:q_cols + KV_LORA + ROPE]
    na_k0 = q_cols + KV_LORA + ROPE
    na_w = NA_HEADS * NA_DIM
    uq = w_uq.reshape(Q_LORA, HEADS, NOPE + ROPE)
    ukv = w_ukv.reshape(KV_LORA, HEADS, NOPE + VDIM)
    wm = in_rows(a["w_mod"][0])

    def cut(n):
        return w2[:, n * D:(n + 1) * D]

    kn_v = np.concatenate([
        in_blocks(ukv[:, :, :NOPE].reshape(KV_LORA, -1), 4)[0][:, 0:1024],
        ukv[:, :, NOPE:].reshape(KVC, P, HEADS * VDIM).transpose(1, 0, 2).reshape(P, 1024)], axis=1)[None]
    experts = []
    for e in range(EXPERTS):
        experts += [in_blocks(a["w_gate"][0, e]), in_blocks(a["w_up"][0, e]), in_down(a["w_down"][0, e])]
    slabs = []
    for s in range(SLABS):
        c = slice(s * D_EXPERT, (s + 1) * D_EXPERT)
        slabs += [in_blocks(a["w_up_2"][0][:, c]), in_down(a["w_down_2"][0][c, :])]
    weights = np.concatenate([
        wm[:8],
        in_blocks(np.concatenate([w_in[:, :Q_LORA], w_in[:, q_cols:q_cols + KV_LORA], np.tile(k_rope, (1, 4)),
                                  np.tile(k_rope[:, swapped], (1, 4))], axis=1)),
        in_blocks(w_in[:, Q_LORA:q_cols]), in_blocks(w_in[:, na_k0:na_k0 + na_w]), in_rows(w_in[:, na_k0 + na_w:]),
        in_blocks(np.concatenate([uq[:, :, :NOPE].reshape(Q_LORA, -1), uq[:, :, NOPE:].reshape(Q_LORA, -1),
                                  uq[:, :, NOPE:][:, :, swapped].reshape(Q_LORA, -1)], axis=1), 4),
        kn_v, wm[8:], in_blocks(a["w_out"][0]), in_blocks(a["w_mem_kv_2"][0][:, :D]), *experts,
        in_rows(a["w_mem_kv_2"][0][:, D:]),
        in_blocks(cut(0)), in_blocks(cut(2)), in_blocks(cut(1)), in_blocks(cut(7)), in_blocks(a["w_conv_out_2"][0]),
        in_blocks(cut(3)), in_blocks(cut(4)), in_rows(cut(5)), in_blocks(cut(6)), in_blocks(a["w_sb_out_2"][0]),
        in_blocks(cut(8)), in_blocks(cut(9)), in_blocks(a["w_x_out_2"][0]), in_blocks(a["w_out_2"][0]), *slabs])
    assert weights.shape == (UNITS, P, UNIT)
    tokens = np.stack([v[0].T.reshape(KC, P, T).transpose(1, 0, 2) for v in (a["x"], a["ctx"], a["mem_2"])])
    cond = np.stack([by_feature(a["c"][0]), by_feature(a["c_ctx"])], axis=2).reshape(P, 16)
    router = np.concatenate([a["w_router_group"][0], a["w_router_expert"][0]], axis=1)
    b_router = np.concatenate([a["b_router_group"][0], a["b_router_expert"][0]])
    cols = np.concatenate(
        [by_feature(a[n].reshape(-1)) for n in ("norm_attn_g", "norm_ffn_g", "final_norm_g", "g_mix_2", "g_mem_2",
                                                "g_mlp_2", "q_a_norm_g", "kv_a_norm_g", "q_norm_g_2", "k_norm_g_2")]
        + [by_feature(a["conv_w_2"][0, tap]) for tap in range(3)]
        + [by_feature(a["b_mod"][0]), cond, router.reshape(KC, P, 20).transpose(1, 0, 2).reshape(P, 160),
           np.tile(b_router, (P, 1))], axis=1)
    c = np.arange(GRID_W)
    across = np.clip(c[None, :] - c[:, None] + NA_WIN_W - 1, 0, 2 * NA_WIN_W - 2)
    rows = T // GRID_W
    down = np.arange(rows)[None, :] - np.arange(rows)[:, None] + NA_WIN_H - 1
    bias = a["na_rel_bias"][0][:, down[:, None, :, None], across[None, :, None, :]]
    bias = bias.transpose(1, 2, 0, 3, 4).reshape(rows, GRID_W, NA_HEADS, T)
    arrays = {"weights": weights, "tokens": tokens, "cols": cols, "constants": constants(), "bias": bias}
    arrays = {f"in_{n}": np.ascontiguousarray(v) for n, v in arrays.items()}
    nc = bacc.Bacc("TRN2", target_bir_lowering=False, num_devices=1)
    args = [nc.dram_tensor(n, v.shape, mybir.dt.from_np(v.dtype), kind="ExternalInput").ap() for n, v in arrays.items()]
    out = nc.dram_tensor("out_features", (P, KC, T), mybir.dt.float32, kind="ExternalOutput").ap()
    build_program(nc, *args, out)
    r = run_bass_kernel_spmd(nc, [arrays], core_ids=[0])
    y = r.results[0]["out_features"]
    return y.transpose(1, 0, 2).reshape(D, T).T[None]
```

```python
import numpy as np
import concourse.bass as bass
from concourse import mybir
from contextlib import ExitStack

P = 128
D = 1024
KC = D // P
T = 256
TT = T // P
HEADS, NOPE, ROPE, VDIM = 8, 64, 32, 64
Q_LORA, KV_LORA = 384, 256
QC, KVC = Q_LORA // P, KV_LORA // P
NA_HEADS, NA_DIM = 8, 64
GRID_W, NA_WIN_H, NA_WIN_W = 64, 8, 16
EXPERTS, GROUPS, PER_GROUP, D_EXPERT = 16, 4, 4, 512
SB_HEADS, SB_DIM = 16, 64
X_HEADS, X_DIM = 4, 256
D_FF = 4096
SLABS = D_FF // D_EXPERT
EPS = 1e-6
MASKED = -1e30

UNIT = 2048
UNIT_COUNTS = [
    ("mod", 8),
    ("lat", 4),
    ("naq", 2), ("nak", 2), ("nav", 2),
    ("uq", 2),
    ("ukv", 1),
    ("mod2", 16),
    ("wout", 4), ("mk", 4),
    ("moe", 6 * EXPERTS), ("mv", 4),
    ("c_h", 4), ("c_c", 4), ("c_b", 4), ("gate0", 4), ("conv_out", 4),
    ("sq", 4), ("sk", 4), ("sv", 4), ("xq", 4), ("sb_out", 4), ("gate1", 4),
    ("gate2", 4), ("x_out", 4), ("out", 4),
    ("mlp", 4 * SLABS),
]
FIRST_UNIT, UNITS = {}, 0
for _name, _count in UNIT_COUNTS:
    FIRST_UNIT[_name] = UNITS
    UNITS += _count
RAW, SPLIT = 4, 2

COL = {}
N_COLS = 0
for _name, _count in [("attn_g", 8), ("ffn_g", 8), ("final_g", 8), ("mix_g", 8), ("mem_g", 8), ("mlp_g", 8),
                      ("q_a_g", 3), ("kv_a_g", 2), ("qn_g", 2), ("kn_g", 2), ("conv", 24), ("b_mod", 48),
                      ("c", 16), ("w_r", 160), ("b_r", 20)]:
    COL[_name] = slice(N_COLS, N_COLS + _count)
    N_COLS += _count
CONST = {}
N_CONST = 0
for _name, _count in [("ident", 128), ("ones", 128), ("tri", 128), ("zero", 1), ("cos", 512), ("sin", 512), ("sb_mask", 384),
                      ("win", 256), ("win_neg", 256), ("prio", 4), ("eps", 1)]:
    CONST[_name] = slice(N_CONST, N_CONST + _count)
    N_CONST += _count

ATT = 2 * (HEADS + NA_HEADS)
ATT_MLA = 2 * HEADS
LEAD = 3


XQ_AT = {g: (g - 1) // 2 for g in range(1, 2 * KC, 2)}


def plan_blocks():
    r, q = [], []
    for u in range(9):
        if u == 4:
            r += [("ss", "ctx_x")]
        if u < 8:
            r += [("mod", u)]
    r += [("lat", j) for j in range(7)]
    r += [("naq", j) for j in range(4)] + [("ss", "qa"), ("ss", "kva")] + [("nak", j) for j in range(4)]
    r += [("nav", u, t) for u in range(2) for t in range(4)]
    r += [("q", j) for j in range(8)] + [("kn", j) for j in range(4)] + [("v", t) for t in range(4)]
    q += [("S", a) for a in range(ATT)]
    for a in range(ATT + 2):
        if a < ATT:
            r += [("PT", a)]
            if a % 2 == 0:
                r += [("mod", 8 + a // 2)]
        if a % 4 == 3:
            r += [("O", a // 4)]
    for j in range(8):
        r += [("wout", j)] + ([("ss", "mem")] if j == 3 else [])
    r += [("mk", j) for j in range(2)] + [("ss", "ffn")] + [("mk", j) for j in range(2, 4)] + [("logits",)]
    r += [("mk", j) for j in range(4, 7)] + [("comb", j) for j in range(EXPERTS // 2)]
    q += [("mk", 7)]
    r += [("moe", j) for j in range(8 * EXPERTS)]
    for u in range(4):
        r += [("mv", u, t) for t in range(2)]
        if u in (0, 2):
            r += [("ss", "mix" if u else "final")]
    for part in ("c_h", "c_c", "c_b", "gate0", "conv_out", "sq", "sk"):
        r += [(part, j) for j in range(8)]
    r += [("sv", u, t) for u in range(4) for t in range(2)]
    q += [("z", 0)]
    for g in range(SB_HEADS + 4):
        if g + 1 < SB_HEADS:
            q += [("z", g + 1)]
        if g in XQ_AT:
            q += [("xq", XQ_AT[g])]
        if 2 <= g <= SB_HEADS + 1:
            r += [("rc", g - 2)]
        if g >= 4 and g % 2 == 0:
            r += [("sbo", (g - 4) // 2)]
    for j in range(8):
        r += [("sb_out", j)] + ([("ssk", j - 4)] if j >= 4 else [])
    r += [("gate1", j) for j in range(4)] + [("ssq", h) for h in range(X_HEADS)]
    r += [("gate1", j) for j in range(4, 8)] + [("gate2", j) for j in range(4)]
    q += [("XS", h) for h in range(X_HEADS)]
    for g in range(X_HEADS + 1):
        if g < X_HEADS:
            r += [("gate2", 4 + g), ("XP", g)]
        if g >= 1:
            r += [("XO", g - 1)]
    for part in ("x_out", "out"):
        r += [(part, j) for j in range(8)]
    r += [("ss", "mlp")]
    r += [("mlp", j) for j in range(4 * SLABS)]
    return {k: n for n, k in enumerate(r)}, {k: n for n, k in enumerate(q)}


R_AT, Q_AT = plan_blocks()


def unit_ends():
    out = [("mod", u) for u in range(8)] + [("lat", j) for j in (1, 3, 5, 6)]
    out += [(part, j) for part in ("naq", "nak") for j in (1, 3)] + [("nav", u, 3) for u in range(2)]
    out += [("q", 3), ("q", 7), ("v", 3)] + [("mod", 8 + u) for u in range(16)]
    out += [(part, j) for part in ("wout", "mk") for j in (1, 3, 5, 7)]
    for e in range(EXPERTS):
        out += [("moe", 8 * e + j) for j in (1, 3, 5, 7)] + [None, None]
    for name, count in UNIT_COUNTS[UNIT_COUNTS.index(("mv", 4)):-1]:
        out += [(name, u, 1) if name in ("sv", "mv") else (name, 2 * u + 1) for u in range(count)]
    for s in range(SLABS):
        out += [("mlp", 4 * s + j) for j in (1, 3)] + [None, None]
    assert len(out) == UNITS
    return out


assert R_AT[("moe", 0)] % 4 == 0
UNIT_END = unit_ends()
SPLIT_UNITS = [n for n in range(UNITS) if not any(FIRST_UNIT[m] <= n < FIRST_UNIT[m] + c
                                                  for m, c in UNIT_COUNTS if m in ("mod", "mod2"))]
SPLITS = [sum(m <= n for m in SPLIT_UNITS) for n in range(UNITS)]
MOD_USED = [n + 1 - SPLITS[n] for n in range(UNITS)]
assert all(n % SPLIT == (SPLITS[n] - 1) % SPLIT for n in SPLIT_UNITS)
DOWNS_BEFORE = [sum(k is None for k in UNIT_END[:n + 1]) for n in range(UNITS)]

NORMS = {"ctx_x": (KC, 512, D), "qa": (QC, T, Q_LORA), "kva": (KVC, 512, KV_LORA), "mem": (KC, T, D),
         "ffn": (KC, T, D), "final": (KC, T, D), "mix": (KC, T, D), "mlp": (KC, T, D)}
CHUNK0, PART0 = {}, {}
_c = _s = 0
for _name, (_kc, _, _) in NORMS.items():
    CHUNK0[_name], PART0[_name] = _c, _s
    _c += _kc
    if _name != "final":
        _s += _kc
NORM_NAMES = list(NORMS)


def build_program(nc, weights, xcm_d, cols_d, const_d, bias_d, out_d):
    f32, f32r = mybir.dt.float32, mybir.dt.float32r
    ALU, ACT, AX = mybir.AluOpType, mybir.ActivationFunctionType, mybir.AxisListType
    with ExitStack() as ctx:
        def sb(name, shape, dt=f32):
            return ctx.enter_context(nc.sbuf_tensor(name, shape, dt))

        def sem(name):
            return ctx.enter_context(nc.semaphore(name))

        def chunks(ap, k):
            return ap.rearrange("p (k n) -> p k n", k=k)

        raw = sb("raw", [P, RAW, UNIT])
        w_hi = sb("w_hi", [P, SPLIT, UNIT], f32r)
        w_lo = sb("w_lo", [P, SPLIT, UNIT], f32r)
        consts = sb("consts", [P, N_CONST])
        cols = sb("cols", [P, N_COLS])
        x = sb("x", [P, KC, T])
        c2 = sb("c2", [P, KC, T])
        full = sb("full", [P, 4096])
        a_hi = sb("a_hi", [P, 5120], f32r)
        a_lo = sb("a_lo", [P, 5120], f32r)
        arena = sb("arena", [P, 12288])
        mod = sb("mod", [P, 6, KC, 2])
        gain = sb("gain", [P, 2, KC, 2])
        cond_s = sb("cond_s", [P, 16])
        turn_rows = sb("turn_rows", [20, 2, T])
        mod_rows = turn_rows[0:2, :, :]
        wr_hi, wr_lo = sb("wr_hi", [P, 160], f32r), sb("wr_lo", [P, 160], f32r)
        rt = sb("rt", [P, 2, 512])
        stat = sb("stat", [P, 16])
        route = sb("route", [P, 2, 128])

        def const(name):
            return consts[:, CONST[name]]

        def col(name, k=None):
            s = COL[name]
            return cols[:, s] if k is None else cols[:, s.start + k:s.start + k + 1]

        ident, ones, tri, zero = const("ident"), const("ones"), const("tri"), const("zero")
        h_hi, h_lo = chunks(a_hi[:, 0:4096], KC), chunks(a_lo[:, 0:4096], KC)
        full_k = chunks(full[:, :], KC)
        qlat, kvlat = chunks(full[:, 0:768], QC), chunks(full[:, 768:1792], KVC)
        qa_f, kva_f = chunks(full[:, 1792:2560], QC), chunks(full[:, 2560:3584], KVC)
        qa_hi, qa_lo = chunks(a_hi[:, 0:768], QC), chunks(a_lo[:, 0:768], QC)
        kva_hi, kva_lo = chunks(a_hi[:, 768:1792], KVC), chunks(a_lo[:, 768:1792], KVC)
        naq, nak, nav = chunks(arena[:, 0:1024], 4), chunks(arena[:, 1024:3072], 4), chunks(arena[:, 3072:5120], 4)
        qn, qr, kr = chunks(arena[:, 5120:6144], 4), chunks(arena[:, 6144:6656], 2), arena[:, 6656:7168]
        vm = chunks(arena[:, 7168:9216], 4)
        na_bias = (chunks(arena[:, 9216:11264], NA_HEADS), chunks(full[:, 2048:4096], NA_HEADS))
        rot = arena[:, 11264:11776]
        kn = chunks(c2[:, :, :].rearrange("p k n -> p (k n)"), 4)
        mla_probs = chunks(full[:, 0:1024], 2)
        na_probs = chunks(c2[:, :, :].rearrange("p k n -> p (k n)"), 4)
        probs_t = (chunks(full[:, 1024:2048], 4), chunks(arena[:, 11264:12288], 4))
        half_hi, half_lo = chunks(a_hi[:, 0:2048], KC), chunks(a_lo[:, 0:2048], KC)
        other_hi, other_lo = chunks(a_hi[:, 2048:4096], KC), chunks(a_lo[:, 2048:4096], KC)
        comb_all = chunks(arena[:, 0:4096], EXPERTS)
        gate_f, hid_f = chunks(arena[:, 4096:5120], 4), chunks(arena[:, 5120:6144], 4)
        hid_hi, hid_lo = chunks(a_hi[:, 2048:3072], 4), chunks(a_lo[:, 2048:3072], 4)
        merged, buf_a, buf_b, buf_c = (chunks(arena[:, n * 2048:(n + 1) * 2048], KC) for n in range(4))
        sb_v = chunks(arena[:, 6144:8192], TT)
        mem_x, x_v = chunks(arena[:, 8192:10240], KC), chunks(arena[:, 8192:10240], TT)
        mem_hi, mem_lo = chunks(a_hi[:, 3072:5120], KC), chunks(a_lo[:, 3072:5120], KC)
        mlp_hi, mlp_lo, mlp_f = mem_hi, mem_lo, chunks(full[:, 2048:4096], KC)
        xk = c2[:, :, :]
        xq = chunks(arena[:, 10240:12288], KC)
        zm = chunks(full[:, 0:1536], 4)
        spl, lnb, att = (chunks(full[:, n * 768 + 1536:n * 768 + 2304], 2) for n in range(3))
        x_sq = chunks(full[:, 0:2048], KC)
        x_rt = (chunks(full[:, 2048:3072], 4), chunks(full[:, 3072:4096], 4))
        x_p, x_pt = chunks(full[:, 0:1024], 2), chunks(full[:, 1024:2048], 2)

        R = [ctx.enter_context(nc.psum_tensor(f"r{i}", [P, 512], f32)) for i in range(4)]
        Q = [ctx.enter_context(nc.psum_tensor(f"q{i}", [P, 512], f32)) for i in range(4)]

        cols_in, consts_in, tokens_in = sem("cols_in"), sem("consts_in"), sem("tokens_in")
        bias_in, mem_in = sem("bias_in"), sem("mem_in")
        raw_in = [sem(f"raw_in{i}") for i in range(RAW)]
        hi_done = sem("hi_done")
        lo_done = sem("lo_done")
        down_used = sem("down_used")
        r_full = [sem(f"r_full{i}") for i in range(4)]
        r_out = [sem(f"r_out{i}") for i in range(4)]
        q_full = [sem(f"q_full{i}") for i in range(4)]
        q_out = [sem(f"q_out{i}") for i in range(4)]
        logits_filled, logits_copied = sem("logits_filled"), sem("logits_copied")
        mod_filled, mod_copied = sem("mod_filled"), sem("mod_copied")
        cond_step, router_split = sem("cond_step"), sem("router_split")
        gain_ready = sem("gain_ready")
        squared, scaled = sem("squared"), sem("scaled")
        part_hi, part_lo = sem("part_hi"), sem("part_lo")
        dve_step = sem("dve_step")
        act_step = sem("act_step")
        pool_step = sem("pool_step")
        kr_ready, qr_ready = sem("kr_ready"), sem("qr_ready")
        biased = sem("biased")
        negmax_ready, na_exp, probs_ready = sem("negmax_ready"), sem("na_exp"), sem("probs_ready")
        first_head = sem("first_head")
        o_hi = sem("o_hi")
        exp_in, exp_out = sem("exp_in"), sem("exp_out")
        comb_ready = sem("comb_ready")
        gated = sem("gated")
        hid_hi_s, hid_lo_s = sem("hid_hi_s"), sem("hid_lo_s")
        y_full, y_out = sem("y_full"), sem("y_out")
        conv_done = sem("conv_done")
        cb_hi, cb_lo = sem("cb_hi"), sem("cb_lo")
        merge_done = sem("merge_done")
        z_abs, z_ln, z_sp, z_exp = sem("z_abs"), sem("z_ln"), sem("z_sp"), sem("z_exp")
        head_sq, head_scaled = sem("head_sq"), sem("head_scaled")
        x_negmax, x_probs, xo_hi = sem("x_negmax"), sem("x_probs"), sem("xo_hi")
        gate2_done = sem("gate2_done")
        x_merged = sem("x_merged")
        mg_hi, mg_lo = sem("mg_hi"), sem("mg_lo")
        stored = sem("stored")

        def probs(a):
            return mla_probs[:, a % 2, :] if a < ATT_MLA else na_probs[:, a % 4, :]

        def r_bank(*key):
            return R[R_AT[key] % 4]

        def wait_full(e, *key):
            e.wait_ge(r_full[R_AT[key] % 4], R_AT[key] // 4 + 1)
            return R[R_AT[key] % 4]

        def wait_out(e, *key):
            e.wait_ge(r_out[R_AT[key] % 4], R_AT[key] // 4 + 1)

        def out_sem(*key):
            return r_out[R_AT[key] % 4]

        def wait_qfull(e, *key):
            e.wait_ge(q_full[Q_AT[key] % 4], Q_AT[key] // 4 + 1)
            return Q[Q_AT[key] % 4]

        def wait_qout(e, *key):
            e.wait_ge(q_out[Q_AT[key] % 4], Q_AT[key] // 4 + 1)

        def qout_sem(*key):
            return q_out[Q_AT[key] % 4]

        def norm_io(name):
            if name == "ctx_x":
                return full_k, h_hi, h_lo
            if name == "qa":
                return qa_f, qa_hi, qa_lo
            if name == "kva":
                return kva_f, kva_hi, kva_lo
            if name == "mem":
                return chunks(full[:, 2048:4096], KC), mem_hi, mem_lo
            if name == "mlp":
                return chunks(full[:, 0:2048], KC), mlp_hi, mlp_lo
            return chunks(full[:, 0:2048], KC), half_hi, half_lo

        U = FIRST_UNIT
        MOE_B, MLP_B = R_AT[("moe", 0)], R_AT[("mlp", 0)]
        block = ctx.enter_context(nc.Block())

        @block.sync
        def _(sp):
            sp.dma_start(cols[:, :], cols_d).then_inc(cols_in, 16)
            for n in range(RAW):
                sp.dma_start(raw[:, n, :], weights[n]).then_inc(raw_in[n], 16)
                if n == 1:
                    sp.dma_start(consts[:, :], const_d).then_inc(consts_in, 16)
            sp.dma_start(x[:, :, :], xcm_d[0]).then_inc(tokens_in, 16)
            sp.dma_start(c2[:, :, :], xcm_d[1]).then_inc(tokens_in, 16)

            def next_raw(n):
                if n - RAW in SPLIT_UNITS:
                    sp.wait_ge(lo_done, SPLITS[n - RAW])
                else:
                    sp.wait_ge(mod_filled, MOD_USED[n - RAW])
                sp.dma_start(raw[:, n % RAW, :], weights[n]).then_inc(raw_in[n % RAW], 16)

            mods = MOD_USED[-1]
            first = (U["wout"] // RAW + 2) * RAW
            turns = (UNITS - first) // RAW
            for n in range(RAW, first):
                next_raw(n)
            with sp.Fori(0, turns) as i:
                for j in range(RAW):
                    sp.wait_ge(lo_done, i * RAW + (first + j - RAW + 1 - mods))
                    sp.dma_start(raw[:, j, :], weights[i * RAW + (first + j)]).then_inc(raw_in[j], 16)
            for n in range(first + turns * RAW, UNITS):
                next_raw(n)
            for k in range(KC):
                sp.wait_ge(y_out, KC + k + 1)
                sp.dma_start(out_d[:, k, :], x[:, k, :]).then_inc(stored, 16)
            sp.wait_ge(stored, 16 * KC)

        @block.gpsimd
        def _(pool):
            step = [0]

            def link(ins):
                step[0] += 1
                ins.then_inc(pool_step, 1)
                pool.wait_ge(pool_step, step[0])

            for qrow in range(2):
                pool.dma_start(na_bias[0][64 * qrow:64 * qrow + 64, :, :], bias_d[qrow]).then_inc(bias_in, 16)
            pool.wait_ge(part_lo, PART0["kva"] + KVC)
            for qrow in range(2):
                pool.dma_start(na_bias[1][64 * qrow:64 * qrow + 64, :, :], bias_d[2 + qrow]).then_inc(bias_in, 16)
            pool.wait_ge(consts_in, 16)
            pool.wait_ge(bias_in, 64)
            win = const("win").unsqueeze(1).to_broadcast([P, NA_HEADS, T])
            neg = const("win_neg").unsqueeze(1).to_broadcast([P, NA_HEADS, T])
            for t in range(2):
                link(nc.gpsimd.tensor_tensor(na_bias[t], na_bias[t], win, ALU.mult))
                nc.gpsimd.tensor_tensor(na_bias[t], na_bias[t], neg, ALU.add).then_inc(biased, 1)
            wait_full(pool, "O", 7)
            pool.dma_start(mem_x, xcm_d[2]).then_inc(mem_in, 16)

            def gates(i, e):
                weight = comb_all[:, i * 2 + e, :]
                for f in range(4):
                    b = MOE_B + 8 * e + f
                    pool.wait_ge(consts_in, 16)
                    pool.wait_ge(r_out[b % 4], i * 4 + (b // 4 + 1))
                    nc.gpsimd.tensor_tensor(gate_f[:, f, :], gate_f[:, f, :], weight, ALU.mult)\
                        .then_inc(gated, 1)

            with pool.Fori(0, EXPERTS // 2) as i:
                gates(i, 0)
                gates(i, 1)

            def merge(branch, gate, gates, first=False):
                for j in range(KC):
                    wait_out(pool, branch, j)
                    wait_out(pool, gate, j)
                    if first:
                        nc.gpsimd.tensor_tensor(merged[:, j, :], buf_a[:, j, :], gates[:, j, :], ALU.mult)\
                            .then_inc(merge_done, 1)
                    else:
                        link(nc.gpsimd.tensor_tensor(buf_a[:, j, :], buf_a[:, j, :], gates[:, j, :], ALU.mult))
                        nc.gpsimd.tensor_tensor(merged[:, j, :], merged[:, j, :], buf_a[:, j, :], ALU.add)\
                            .then_inc(merge_done, 1)

            merge("conv_out", "gate0", buf_b, first=True)
            merge("sb_out", "gate1", buf_b)

        @block.scalar
        def _(act):
            next_unit = [0]

            def split(n):
                act.wait_ge(raw_in[n % RAW], 16 * (n // RAW + 1))
                if SPLITS[n] > SPLIT:
                    last = SPLIT_UNITS[SPLITS[n] - 1 - SPLIT]
                    if UNIT_END[last] is None:
                        act.wait_ge(down_used, DOWNS_BEFORE[last])
                    elif UNIT_END[last] in Q_AT:
                        wait_qfull(act, *UNIT_END[last])
                    else:
                        wait_full(act, *UNIT_END[last])
                nc.scalar.activation(w_hi[:, n % SPLIT, :], raw[:, n % RAW, :], ACT.Copy).then_inc(hi_done, 1)

            def ahead(n):
                while next_unit[0] <= min(n + 1, UNITS - 1):
                    if next_unit[0] in SPLIT_UNITS:
                        split(next_unit[0])
                    next_unit[0] += 1

            def mod_rows_out(u):
                if u >= 2:
                    wait_full(act, "mod", u - 2)
                act.wait_ge(mod_filled, u + 1)
                nc.scalar.activation(mod_rows[:, u % 2, :], r_bank("mod", u)[0:2, 0:T], ACT.Copy).then_inc(mod_copied, 1)

            def copy_out(dst, *key, w=T, func=ACT.Copy):
                b = wait_full(act, *key)
                nc.scalar.activation(dst, b[:, 0:w], func).then_inc(out_sem(*key), 1)

            def copy_out_q(dst, *key):
                b = wait_qfull(act, *key)
                nc.scalar.activation(dst, b[:, 0:T], ACT.Copy).then_inc(qout_sem(*key), 1)

            def root(name):
                _, w, feats = NORMS[name]
                b = wait_full(act, "ss", name)
                nc.scalar.activation(rt[:, NORM_NAMES.index(name) % 2, 0:w], b[:, 0:w], ACT.Sqrt, bias=const("eps"),
                                     scale=1.0 / feats).then_inc(out_sem("ss", name), 1)

            def upper(name, shift=None):
                f, hi, _ = norm_io(name)
                for k in range(NORMS[name][0]):
                    act.wait_ge(scaled, CHUNK0[name] + k + 1)
                    if shift is None:
                        ins = nc.scalar.activation(hi[:, k, :], f[:, k, :], ACT.Copy)
                    else:
                        ins = nc.scalar.activation(hi[:, k, :], f[:, k, :], ACT.Identity, bias=mod[:, shift, k, 0:1])
                    ins.then_inc(part_hi, 1)

            def square(name, k, src):
                nc.scalar.activation(norm_io(name)[0][:, k, :], src, ACT.Square).then_inc(squared, 1)

            def ctx_x_upper(first, end):
                for k in range(first, end):
                    act.wait_ge(scaled, k + 1)
                    wait_out(act, "mod", 4 + k // 2)
                    for s in range(2):
                        ins = nc.scalar.activation(h_hi[:, k, T * s:T * s + T], full_k[:, k, T * s:T * s + T],
                                                   ACT.Identity, bias=mod[:, 0, k, s:s + 1])
                    ins.then_inc(part_hi, 1)

            act.wait_ge(cols_in, 16)
            nc.scalar.activation(cond_s[:, :], col("c"), ACT.Silu).then_inc(cond_step, 1)
            nc.scalar.activation(wr_hi[:, :], col("w_r"), ACT.Copy).then_inc(cond_step, 1)
            for u in range(8):
                mod_rows_out(u)
                if u == 2:
                    act.wait_ge(consts_in, 16)
                    act.preload_act_table_set("sqrt_and_others")
                    act.wait_ge(tokens_in, 32)
                    for k in range(KC):
                        nc.scalar.activation(full_k[:, k, 0:T], x[:, k, :], ACT.Square)
                        nc.scalar.activation(full_k[:, k, T:512], c2[:, k, :], ACT.Square).then_inc(squared, 1)
                if u == 3:
                    root("ctx_x")
                if u >= 5:
                    ctx_x_upper(2 * u - 10, 2 * u - 8)
                if u == 5:
                    ahead(U["lat"] - 1)
            ctx_x_upper(6, 8)
            act.wait_ge(part_lo, PART0["ctx_x"] + KC)
            for j in range(5):
                ahead(U["lat"] + j // 2)
                dst, w = (qlat[:, j, :], T) if j < 3 else (kvlat[:, j - 3, :], 512)
                copy_out(dst, "lat", j, w=w)
            ahead(U["lat"] + 3)
            for j in range(5):
                wait_out(act, "lat", j)
                if j < 3:
                    square("qa", j, qlat[:, j, :])
                else:
                    square("kva", j - 3, kvlat[:, j - 3, :])
            for j in range(4):
                ahead(U["naq"] + j // 2)
                copy_out(naq[:, j, :], "naq", j)
            root("qa")
            root("kva")
            for j in range(4):
                ahead(U["nak"] + j // 2)
                copy_out(nak[:, j, :], "nak", j, w=512)
            for u in range(2):
                for t in range(4):
                    ahead(U["nav"] + u)
                    copy_out(nav[:, t, T * u:T * u + T], "nav", u, t)
            upper("qa")
            upper("kva")
            for j in range(4):
                ahead(U["uq"])
                copy_out(qn[:, j, :], "q", j)
            ahead(U["ukv"])
            for j in range(4):
                copy_out(kn[:, j, :], "kn", j, w=512)
            for t in range(4):
                copy_out(vm[:, t, :], "v", t, w=512)

            def exp_tile(a):
                act.wait_ge(negmax_ready, a + 1)
                if a < ATT_MLA:
                    if a >= 2:
                        wait_full(act, "PT", a - 2)
                    s = Q[Q_AT[("S", a)] % 4]
                    nc.scalar.activation(probs(a), s[:, :], ACT.Exp, bias=stat[:, 2 + a % 2:3 + a % 2],
                                         scale=(NOPE + ROPE) ** -0.5, accum_out=stat[:, 4 + a % 2:5 + a % 2])\
                        .then_inc(qout_sem("S", a), 1)
                else:
                    nc.scalar.activation(probs(a), probs(a), ACT.Exp,
                                         bias=stat[:, 2 + a % 2:3 + a % 2], accum_out=stat[:, 4 + a % 2:5 + a % 2])\
                        .then_inc(na_exp, 1)

            def turn_tile(a):
                h, t = a // 2, a % 2
                b = wait_full(act, "PT", a)
                if h >= 2 and h % 2 == 0:
                    act.wait_ge(first_head, h // 2)
                elif h >= 2:
                    wait_full(act, "O", (h - 2) // 2)
                nc.scalar.activation(probs_t[h % 2][:, :, P * t:P * t + P], chunks(b[:, :], 4), ACT.Copy)\
                    .then_inc(out_sem("PT", a), 1)

            def o_upper(c):
                b = wait_full(act, "O", c)
                nc.scalar.activation(half_hi[:, c, :], b[:, 0:T], ACT.Copy).then_inc(o_hi, 1)

            for a in range(ATT + 4):
                if a < ATT:
                    exp_tile(a)
                if a % 2 == 0 and 2 <= a <= ATT:
                    mod_rows_out(8 + (a - 2) // 2)
                if a % 4 == 3 and a >= 7:
                    o_upper((a - 7) // 4)
                if 1 <= a <= ATT:
                    turn_tile(a - 1)
                if a == ATT:
                    ahead(U["wout"])
            ahead(U["wout"])
            act.preload_act_table_set("sqrt_and_others")
            act.wait_ge(mem_in, 16)
            for k in range(KC):
                square("mem", k, mem_x[:, k, :])
            ahead(U["wout"] + 1)
            root("mem")
            ahead(U["wout"] + 3)
            upper("mem")
            for k in range(KC):
                wait_out(act, "wout", k)
                square("ffn", k, x[:, k, :])
            ahead(U["mk"])
            for j in range(2):
                copy_out(xk[:, j, :], "mk", j)
            root("ffn")
            ahead(U["mk"] + 1)
            upper("ffn", 3)
            for j in range(2, 4):
                copy_out(xk[:, j, :], "mk", j)
            act.wait_ge(logits_filled, 1)
            nc.scalar.activation(turn_rows[:, 0, :], r_bank("logits")[0:20, 0:T], ACT.Copy).then_inc(logits_copied, 1)
            ahead(U["mk"] + 2)
            act.wait_ge(exp_in, 1)
            nc.scalar.activation(route[:, :, 32:40], route[:, :, 24:32], ACT.Exp).then_inc(exp_out, 1)
            for j in range(4, 7):
                copy_out(xk[:, j, :], "mk", j)
            copy_out_q(xk[:, 7, :], "mk", 7)
            ahead(U["moe"])
            for j in range(EXPERTS // 2):
                copy_out(comb_all[:, 2 * j:2 * j + 2, :].rearrange("p e n -> p (e n)"), "comb", j, w=512)

            def split_in_loop(i, units, downs, blocks, n):
                act.wait_ge(raw_in[n % RAW], i * (16 * units // RAW) + 16 * (n // RAW + 1))
                if UNIT_END[n - SPLIT] is None:
                    act.wait_ge(down_used, i * downs + DOWNS_BEFORE[n - SPLIT])
                else:
                    b = R_AT[UNIT_END[n - SPLIT]]
                    act.wait_ge(r_full[b % 4], i * (blocks // 4) + (b // 4 + 1))
                nc.scalar.activation(w_hi[:, n % SPLIT, :], raw[:, n % RAW, :], ACT.Copy).then_inc(hi_done, 1)

            def expert(i, e):
                for u in range(6):
                    for s in range(2):
                        if s == 1:
                            split_in_loop(i, 12, 4, 16, U["moe"] + 6 * e + u + SPLIT)
                        f = 2 * (u % 2) + s
                        b = MOE_B + 8 * e + 2 * u + s
                        if u < 2:
                            act.wait_ge(r_full[b % 4], i * 4 + (b // 4 + 1))
                            nc.scalar.activation(gate_f[:, f, :], R[b % 4][:, 0:T], ACT.Silu).then_inc(r_out[b % 4], 1)
                        elif u < 4:
                            act.wait_ge(r_out[b % 4], i * 4 + (b // 4 + 1))
                            nc.scalar.activation(hid_hi[:, f, :], hid_f[:, f, :], ACT.Copy).then_inc(hid_hi_s, 1)

            with act.Fori(0, EXPERTS // 2) as i:
                expert(i, 0)
                expert(i, 1)
            next_unit[0] = U["moe"] + 6 * EXPERTS + SPLIT
            def values_out(u):
                for t in range(TT):
                    copy_out(x_v[:, t, T * u:T * u + T], "mv", u, t)

            ahead(U["mv"])
            act.preload_act_table_set("sqrt_and_others")
            for k in range(KC):
                act.wait_ge(y_out, k + 1)
                square("final", k, x[:, k, :])
            values_out(0)
            root("final")
            ahead(U["mv"] + 1)
            values_out(1)
            for k in range(KC):
                act.wait_ge(scaled, CHUNK0["final"] + k + 1)
                square("mix", k, x[:, k, :])
            ahead(U["mv"] + 2)
            values_out(2)
            root("mix")
            ahead(U["mv"] + 3)
            upper("mix")
            values_out(3)

            def part_out(part, dst, func=ACT.Copy, merged_before=None, blocks=range(KC)):
                for j in blocks:
                    ahead(U[part] + j // 2)
                    if merged_before is not None:
                        act.wait_ge(merge_done, merged_before + j + 1)
                    copy_out(dst[:, j, :], part, j, func=func)

            part_out("c_h", buf_a)
            ahead(U["c_c"] + 3)
            for j in range(KC):
                ahead(U["c_b"] + j // 2)
                wait_out(act, "c_b", j)
                nc.scalar.activation(other_hi[:, j, :], buf_c[:, j, :], ACT.Copy).then_inc(cb_hi, 1)
            part_out("gate0", buf_b, ACT.Sigmoid)
            part_out("conv_out", buf_a)
            part_out("sq", buf_a, merged_before=0)
            part_out("sk", buf_b)
            for u in range(4):
                for t in range(TT):
                    ahead(U["sv"] + u)
                    copy_out(sb_v[:, t, T * u:T * u + T], "sv", u, t)
            ahead(U["xq"])
            act.preload_act_table_set("natural_log_exp_and_others")
            for g in range(SB_HEADS + 4):
                if g < SB_HEADS:
                    h = g
                    act.wait_ge(z_abs, h + 1)
                    nc.scalar.activation(lnb[:, h % 2, :], lnb[:, h % 2, :], ACT.Exp, scale=-1.0).then_inc(act_step, 1)
                    act.wait_ge(act_step, h + 1)
                    nc.scalar.activation(lnb[:, h % 2, :], lnb[:, h % 2, :], ACT.Ln, bias=ones[:, 0:1]).then_inc(z_ln, 1)
                if 3 <= g < SB_HEADS + 3:
                    h = g - 3
                    wait_out(act, "rc", h)
                    nc.scalar.activation(att[:, h % 2, :], att[:, h % 2, :], ACT.Exp).then_inc(z_exp, 1)
                if g - 1 in XQ_AT:
                    j = XQ_AT[g - 1]
                    copy_out_q(xq[:, j, :], "xq", j)
                    if j % 2 == 1:
                        ahead(U["xq"] + j // 2 + 1)
                if g % 2 == 0 and g >= 6:
                    c = (g - 6) // 2
                    b = wait_full(act, "sbo", c)
                    nc.scalar.activation(other_hi[:, c, :], b[:, 0:T], ACT.Copy).then_inc(o_hi, 1)
            b = wait_full(act, "sbo", 7)
            nc.scalar.activation(other_hi[:, 7, :], b[:, 0:T], ACT.Copy).then_inc(o_hi, 1)

            def head_square(src, j):
                nc.scalar.activation(x_sq[:, j, :], src[:, j, :], ACT.Square).then_inc(head_sq, 1)

            def head_root(key, h, which):
                b = wait_full(act, key, h)
                nc.scalar.activation(x_rt[which][:, h, :], b[:, 0:T], ACT.Sqrt, bias=const("eps"),
                                     scale=1.0 / X_DIM).then_inc(out_sem(key, h), 1)

            for j in range(KC):
                head_square(xk, j)
            for j in range(KC):
                ahead(U["sb_out"] + j // 2)
                copy_out(buf_a[:, j, :], "sb_out", j)
                if j >= 4:
                    head_root("ssk", j - 4, 0)
                    wait_qout(act, "xq", 2 * (j - 4) + 1)
                    for c in range(2 * (j - 4), 2 * (j - 4) + 2):
                        head_square(xq, c)
            for j in range(KC):
                ahead(U["gate1"] + j // 2)
                copy_out(buf_b[:, j, :], "gate1", j, func=ACT.Sigmoid)
                if j == 3:
                    ahead(U["gate1"] + 2)
                    for h in range(X_HEADS):
                        head_root("ssq", h, 1)
            part_out("gate2", buf_c, ACT.Sigmoid, blocks=range(4))
            def x_exp(h):
                act.wait_ge(x_negmax, h + 1)
                s, st = Q[Q_AT[("XS", h)] % 4], 8 * (h % 2)
                if h >= 2:
                    wait_full(act, "XP", h - 2)
                for t in range(TT):
                    ins = nc.scalar.activation(x_p[:, h % 2, T * t:T * t + T], s[:, T * t:T * t + T], ACT.Exp,
                                               bias=stat[:, st + 2 + t:st + 3 + t], scale=X_DIM ** -0.5,
                                               accum_out=stat[:, st + 4 + t:st + 5 + t])
                ins.then_inc(qout_sem("XS", h), 1)

            x_exp(0)
            for h in range(X_HEADS):
                if h + 1 < X_HEADS:
                    x_exp(h + 1)
                ahead(U["gate2"] + (4 + h) // 2)
                copy_out(buf_c[:, 4 + h, :], "gate2", 4 + h)
                b = wait_full(act, "XP", h)
                if h >= 2:
                    wait_full(act, "XO", h - 2)
                nc.scalar.activation(x_pt[:, h % 2, :], b[:, :], ACT.Copy).then_inc(out_sem("XP", h), 1)
                if h >= 1:
                    b = wait_full(act, "XO", h - 1)
                    nc.scalar.activation(other_hi[:, 2 * h - 2:2 * h, :], chunks(b[:, :], 2), ACT.Copy).then_inc(xo_hi, 1)
            b = wait_full(act, "XO", 3)
            nc.scalar.activation(other_hi[:, 6:8, :], chunks(b[:, :], 2), ACT.Copy).then_inc(xo_hi, 1)
            for j in range(4, KC):
                wait_out(act, "gate2", j)
                nc.scalar.activation(buf_c[:, j, :], buf_c[:, j, :], ACT.Sigmoid).then_inc(gate2_done, 1)
            for j in range(KC):
                ahead(U["x_out"] + j // 2)
                act.wait_ge(x_merged, j + 1)
                nc.scalar.activation(half_hi[:, j, :], merged[:, j, :], ACT.Copy).then_inc(mg_hi, 1)
            for k in range(KC):
                ahead(U["out"] + k // 2)
                wait_out(act, "out", k)
                square("mlp", k, x[:, k, :])
                act.wait_ge(scaled, CHUNK0["mlp"] + k + 1)
                nc.scalar.activation(mlp_hi[:, k, :], mlp_f[:, k, :], ACT.Copy).then_inc(part_hi, 1)
            b = wait_full(act, "ss", "mlp")
            nc.scalar.activation(rt[:, 1, 0:T], b[:, 0:T], ACT.Identity, bias=const("eps"), scale=1.0 / D)\
                .then_inc(out_sem("ss", "mlp"), 1)

            def slab(i, last=False):
                for u in range(4):
                    for s in range(2):
                        if s == 1 and not (last and u >= 2):
                            split_in_loop(i, 4, 2, 4, U["mlp"] + u + SPLIT)
                        f = 2 * u + s
                        if u < 2:
                            b = MLP_B + f
                            act.wait_ge(r_out[b % 4], i + (b // 4 + 1))
                            nc.scalar.activation(hid_hi[:, f, :], hid_f[:, f, :], ACT.Copy).then_inc(hid_hi_s, 1)

            ahead(U["mlp"])
            with act.Fori(0, SLABS - 1) as i:
                slab(i)
            slab(SLABS - 1, last=True)

        @block.vector
        def _(dve):
            next_unit, step = [0], [0]

            def link(ins):
                step[0] += 1
                ins.then_inc(dve_step, 1)
                dve.wait_ge(dve_step, step[0])

            def split(n):
                dve.wait_ge(hi_done, SPLITS[n])
                nc.vector.tensor_tensor(w_lo[:, n % SPLIT, :], raw[:, n % RAW, :], w_hi[:, n % SPLIT, :].bitcast(f32),
                                        ALU.subtract).then_inc(lo_done, 1)

            def ahead(n):
                while next_unit[0] <= min(n + 1, UNITS - 1):
                    if next_unit[0] in SPLIT_UNITS:
                        split(next_unit[0])
                    next_unit[0] += 1

            def lower(dst, src, hi):
                return nc.vector.tensor_tensor(dst, src, hi.bitcast(f32), ALU.subtract)

            def invert_root(name):
                r = rt[:, NORM_NAMES.index(name) % 2, 0:NORMS[name][1]]
                wait_out(dve, "ss", name)
                link(nc.vector.reciprocal(r, r))

            def scale_and_split(name, src, gain_of, shift=None, inverted=False):
                kc, w, _ = NORMS[name]
                f, hi, lo = norm_io(name)
                r = rt[:, NORM_NAMES.index(name) % 2, 0:w]
                if not inverted:
                    invert_root(name)
                for k in range(kc + 1):
                    if k < kc:
                        dst = x[:, k, :] if name == "final" else f[:, k, :]
                        nc.vector.scalar_tensor_tensor(out=dst, in0=src[:, k, :], scalar=gain_of(k), in1=r,
                                                       op0=ALU.mult, op1=ALU.mult).then_inc(scaled, 1)
                    if k >= 1 and name != "final":
                        j = k - 1
                        dve.wait_ge(part_hi, PART0[name] + j + 1)
                        if shift is None:
                            ins = lower(lo[:, j, :], f[:, j, :], hi[:, j, :])
                        else:
                            ins = nc.vector.scalar_tensor_tensor(
                                out=lo[:, j, :], in0=f[:, j, :], scalar=mod[:, shift, j, 0:1],
                                in1=hi[:, j, :].bitcast(f32), op0=ALU.add, op1=ALU.subtract)
                        ins.then_inc(part_lo, 1)

            def ctx_x_scale(k):
                for s in range(2):
                    c = slice(T * s, T * s + T)
                    ins = nc.vector.scalar_tensor_tensor(
                        out=full_k[:, k, c], in0=(x, c2)[s][:, k, :], scalar=gain[:, 0, k, s:s + 1],
                        in1=rt[:, 0, c], op0=ALU.mult, op1=ALU.mult)
                ins.then_inc(scaled, 1)

            def ctx_x_lower(k):
                dve.wait_ge(part_hi, k + 1)
                for s in range(2):
                    c = slice(T * s, T * s + T)
                    ins = nc.vector.scalar_tensor_tensor(
                        out=h_lo[:, k, c], in0=full_k[:, k, c], scalar=mod[:, 0, k, s:s + 1],
                        in1=h_hi[:, k, c].bitcast(f32), op0=ALU.add, op1=ALU.subtract)
                ins.then_inc(part_lo, 1)

            def mod_out(u):
                v = (u + 4) % 8 if u < 8 else u
                g, k = v // 4, 2 * (v % 4)
                b = wait_full(dve, "mod", u)
                bias = col("b_mod")[:, 2 * v:2 * v + 2].unsqueeze(2).to_broadcast([P, 2, 2])
                nc.vector.tensor_tensor(mod[:, g, k:k + 2, :], chunks(b[:, T:T + 4], 2), bias, ALU.add)\
                    .then_inc(out_sem("mod", u), 1)

            def gains(which, g, name):
                for u in range(0, 4) if g == 1 else range(4 * g, 4 * g + 4):
                    wait_out(dve, "mod", u)
                gb = col(name).unsqueeze(2).to_broadcast([P, KC, 2])
                link(nc.vector.scalar_tensor_tensor(out=gain[:, which, :, :], in0=mod[:, g, :, :], scalar=1.0, in1=gb,
                                                    op0=ALU.add, op1=ALU.mult))

            dve.wait_ge(cond_step, 2)
            lower(wr_lo[:, :], col("w_r"), wr_hi[:, :]).then_inc(router_split, 1)
            for u in range(8):
                if u == 3:
                    invert_root("ctx_x")
                mod_out(u)
                if u == 3:
                    gains(0, 1, "attn_g")
                    for k in range(KC):
                        ctx_x_scale(k)
                if u >= 4:
                    for k in range(2 * u - 8, 2 * u - 6):
                        ctx_x_lower(k)
                if u == 5:
                    ahead(U["lat"] - 1)

            ahead(U["lat"] + 3)
            b = wait_full(dve, "lat", 5)
            nc.vector.tensor_tensor(kr, b[:, :], const("cos"), ALU.mult).then_inc(out_sem("lat", 5), 1)
            b = wait_full(dve, "lat", 6)
            nc.vector.tensor_tensor(rot, b[:, :], const("sin"), ALU.mult).then_inc(out_sem("lat", 6), 1)
            wait_out(dve, "lat", 5)
            wait_out(dve, "lat", 6)
            nc.vector.tensor_tensor(kr, kr, rot, ALU.add).then_inc(kr_ready, 1)
            for part in ("naq", "nak", "nav"):
                ahead(U[part] + 1)
                if part == "naq":
                    invert_root("qa")
                if part == "nak":
                    invert_root("kva")
            scale_and_split("qa", qlat, lambda k: col("q_a_g", k), inverted=True)
            scale_and_split("kva", kvlat, lambda k: col("kv_a_g", k), inverted=True)
            ahead(U["uq"] + 1)
            for j in range(2):
                b = wait_full(dve, "q", 4 + j)
                nc.vector.tensor_tensor(qr[:, j, :], b[:, 0:T], const("cos")[:, 0:T], ALU.mult)\
                    .then_inc(out_sem("q", 4 + j), 1)
            for j in range(2):
                b = wait_full(dve, "q", 6 + j)
                nc.vector.tensor_tensor(rot[:, T * j:T * j + T], b[:, 0:T], const("sin")[:, 0:T], ALU.mult)\
                    .then_inc(out_sem("q", 6 + j), 1)
            for j in range(2):
                wait_out(dve, "q", 4 + j)
                wait_out(dve, "q", 6 + j)
                nc.vector.tensor_tensor(qr[:, j, :], qr[:, j, :], rot[:, T * j:T * j + T], ALU.add)\
                    .then_inc(qr_ready, 1)
            ahead(U["ukv"])

            def tile_max(a):
                b = wait_qfull(dve, "S", a)
                mx, nm = stat[:, a % 2:a % 2 + 1], stat[:, 2 + a % 2:3 + a % 2]
                if a < ATT_MLA:
                    link(nc.vector.reduce_max(mx, b[:, :], AX.X))
                    nc.vector.tensor_scalar(nm, mx, -(NOPE + ROPE) ** -0.5, None, ALU.mult).then_inc(negmax_ready, 1)
                else:
                    if a == ATT_MLA:
                        dve.wait_ge(biased, 2)
                    p = probs(a)
                    if a >= ATT_MLA + 4:
                        wait_full(dve, "PT", a - 4)
                    nc.vector.scalar_tensor_tensor(out=p[:, 0:T], in0=b[:, 0:T], scalar=NA_DIM ** -0.5,
                                                   in1=na_bias[a % 2][:, a // 2 - HEADS, :], op0=ALU.mult, op1=ALU.add)
                    nc.vector.tensor_scalar(p[:, T:512], b[:, T:512], NA_DIM ** -0.5, None, ALU.mult)\
                        .then_inc(qout_sem("S", a), 1)
                    wait_qout(dve, "S", a)
                    link(nc.vector.reduce_max(mx, p, AX.X))
                    nc.vector.tensor_scalar(nm, mx, -1.0, None, ALU.mult).then_inc(negmax_ready, 1)

            def tile_scale(a):
                if a < ATT_MLA:
                    wait_qout(dve, "S", a)
                else:
                    dve.wait_ge(na_exp, a - ATT_MLA + 1)
                s, p = stat[:, 4 + a % 2:5 + a % 2], probs(a)
                link(nc.vector.reciprocal(s, s))
                nc.vector.tensor_scalar(p, p, s, None, ALU.mult).then_inc(probs_ready, 1)

            for a in range(ATT + 4):
                if a < ATT:
                    tile_max(a)
                if 1 <= a <= ATT:
                    tile_scale(a - 1)
                if a % 2 == 1 and 3 <= a <= ATT + 1:
                    mod_out(8 + (a - 3) // 2)
                if a % 4 == 3 and a >= 7:
                    c = (a - 7) // 4
                    dve.wait_ge(o_hi, c + 1)
                    b = wait_full(dve, "O", c)
                    lower(half_lo[:, c, :], b[:, 0:T], half_hi[:, c, :]).then_inc(out_sem("O", c), 1)
                if a == ATT:
                    ahead(U["wout"])
            gains(1, 4, "ffn_g")
            for j in range(KC):
                if j == 6:
                    ahead(U["wout"] + 3)
                    scale_and_split("mem", mem_x, lambda k: col("mem_g", k))
                ahead(U["wout"] + j // 2)
                b = wait_full(dve, "wout", j)
                nc.vector.scalar_tensor_tensor(out=x[:, j, :], in0=b[:, 0:T], scalar=mod[:, 2, j, 0:1], in1=x[:, j, :],
                                               op0=ALU.mult, op1=ALU.add).then_inc(out_sem("wout", j), 1)
            for j in range(KC):
                wait_out(dve, "wout", j)
            ahead(U["mk"])
            scale_and_split("ffn", x, lambda k: gain[:, 1, k, 0:1], 3)
            ahead(U["mk"] + 2)

            def rv(lo, w):
                return route[:, :, lo:lo + w]

            def wide(ap, w):
                return ap.to_broadcast([P, TT, w])

            prio = const("prio").unsqueeze(1).to_broadcast([P, TT, 4])

            def largest(val, mx, eq, one):
                link(nc.vector.reduce_max(mx, val, AX.X))
                link(nc.vector.tensor_tensor(eq, val, wide(mx, 4), ALU.is_equal))
                link(nc.vector.tensor_tensor(eq, eq, prio, ALU.mult))
                link(nc.vector.reduce_max(rv(120, 1), eq, AX.X))
                link(nc.vector.tensor_tensor(one, eq, wide(rv(120, 1), 4), ALU.is_equal))

            logits, g_hot, g_max = rv(0, 20), rv(48, 4), rv(121, 1)
            e_sel, e_max, hot1, hot2, top1, top2 = rv(52, 4), rv(122, 1), rv(56, 4), rv(60, 4), rv(123, 1), rv(124, 1)
            scr, comb = rv(64, 16), rv(80, 16)
            b = wait_full(dve, "logits")
            nc.vector.tensor_tensor(logits, chunks(b[:, T:T + 40], TT), col("b_r").unsqueeze(1).to_broadcast([P, TT, 20]),
                                    ALU.add).then_inc(out_sem("logits"), 1)
            wait_out(dve, "logits")
            largest(rv(0, 4), g_max, rv(100, 4), g_hot)
            for g in range(GROUPS):
                link(nc.vector.tensor_tensor(scr[:, :, 4 * g:4 * g + 4], rv(4 + 4 * g, 4), wide(g_hot[:, :, g:g + 1], 4),
                                             ALU.mult))
            link(nc.vector.reduce_sum(e_sel, scr.rearrange("p t (g e) -> p t e g", g=GROUPS), AX.X))
            link(nc.vector.reduce_max(e_max, e_sel, AX.X))
            link(nc.vector.tensor_tensor(rv(24, 4), rv(0, 4), wide(g_max, 4), ALU.subtract))
            nc.vector.tensor_tensor(rv(28, 4), e_sel, wide(e_max, 4), ALU.subtract).then_inc(exp_in, 1)
            dve.wait_ge(exp_out, 1)
            sums = rv(40, 2)
            link(nc.vector.reduce_sum(sums, rv(32, 8).rearrange("p t (s e) -> p t s e", s=2), AX.X))
            link(nc.vector.reciprocal(sums, sums))
            prob, prob2 = rv(104, 4), rv(108, 4)
            link(nc.vector.tensor_tensor(prob, rv(36, 4), wide(rv(41, 1), 4), ALU.mult))
            largest(prob, top1, rv(100, 4), hot1)
            link(nc.vector.scalar_tensor_tensor(out=prob2, in0=hot1, scalar=-2.0, in1=prob, op0=ALU.mult, op1=ALU.add))
            largest(prob2, top2, rv(100, 4), hot2)
            link(nc.vector.tensor_tensor(hot1, hot1, wide(top1, 4), ALU.mult))
            link(nc.vector.tensor_tensor(hot2, hot2, wide(top2, 4), ALU.mult))
            link(nc.vector.tensor_tensor(hot1, hot1, hot2, ALU.add))
            link(nc.vector.tensor_tensor(top1, top1, top2, ALU.add))
            link(nc.vector.reciprocal(top1, top1))
            link(nc.vector.tensor_tensor(hot1, hot1, wide(top1, 4), ALU.mult))
            link(nc.vector.tensor_tensor(hot1, hot1, wide(rv(40, 1), 4), ALU.mult))
            for g in range(GROUPS):
                ins = nc.vector.tensor_tensor(comb[:, :, 4 * g:4 * g + 4], hot1, wide(g_hot[:, :, g:g + 1], 4), ALU.mult)
            ins.then_inc(comb_ready, 1)
            ahead(U["moe"])

            def split_in_loop(i, units, n):
                dve.wait_ge(hi_done, i * units + SPLITS[n])
                nc.vector.tensor_tensor(w_lo[:, n % SPLIT, :], raw[:, n % RAW, :], w_hi[:, n % SPLIT, :].bitcast(f32),
                                        ALU.subtract).then_inc(lo_done, 1)

            def expert(i, e):
                for u in range(6):
                    for s in range(2):
                        f = 2 * (u % 2) + s
                        b = MOE_B + 8 * e + 2 * u + s
                        if 2 <= u < 4:
                            dve.wait_ge(gated, i * 8 + (4 * e + f + 1))
                            dve.wait_ge(r_full[b % 4], i * 4 + (b // 4 + 1))
                            nc.vector.tensor_tensor(hid_f[:, f, :], R[b % 4][:, 0:T], gate_f[:, f, :], ALU.mult)\
                                .then_inc(r_out[b % 4], 1)
                        if s == 1:
                            split_in_loop(i, 12, U["moe"] + 6 * e + u + SPLIT)
                        if 2 <= u < 4:
                            dve.wait_ge(hid_hi_s, i * 8 + (4 * e + f + 1))
                            lower(hid_lo[:, f, :], hid_f[:, f, :], hid_hi[:, f, :]).then_inc(hid_lo_s, 1)

            with dve.Fori(0, EXPERTS // 2) as i:
                expert(i, 0)
                expert(i, 1)
            next_unit[0] = U["moe"] + 6 * EXPERTS + SPLIT
            ahead(U["mv"])
            for m in range(KC):
                dve.wait_ge(y_full, m // 2 + 1)
                nc.vector.scalar_tensor_tensor(out=x[:, m, :], in0=Q[m // 2][:, T * (m % 2):T * (m % 2) + T],
                                               scalar=mod[:, 5, m, 0:1], in1=x[:, m, :], op0=ALU.mult, op1=ALU.add)\
                    .then_inc(y_out, 1)
            ahead(U["mv"] + 1)
            scale_and_split("final", x, lambda k: col("final_g", k))
            ahead(U["mv"] + 3)
            scale_and_split("mix", x, lambda k: col("mix_g", k))
            ahead(U["c_h"] + 3)
            for j in range(KC):
                ahead(U["c_c"] + j // 2)
                wait_out(dve, "c_h", j)
                b = wait_full(dve, "c_c", j)
                nc.vector.tensor_tensor(buf_b[:, j, :], b[:, 0:T], buf_a[:, j, :], ALU.mult)\
                    .then_inc(out_sem("c_c", j), 1)
                wait_out(dve, "c_c", j)
                link(nc.vector.tensor_scalar(buf_c[:, j, :], buf_b[:, j, :], col("conv", 16 + j), None, ALU.mult))
                for lag in (1, 2):
                    link(nc.vector.scalar_tensor_tensor(
                        out=buf_c[:, j, lag:T], in0=buf_b[:, j, 0:T - lag], scalar=col("conv", 8 * (2 - lag) + j),
                        in1=buf_c[:, j, lag:T], op0=ALU.mult, op1=ALU.add))
            for j in range(KC):
                ahead(U["c_b"] + j // 2)
                b = wait_full(dve, "c_b", j)
                nc.vector.tensor_tensor(buf_c[:, j, :], b[:, 0:T], buf_c[:, j, :], ALU.mult)\
                    .then_inc(out_sem("c_b", j), 1)
                dve.wait_ge(cb_hi, j + 1)
                lower(other_lo[:, j, :], buf_c[:, j, :], other_hi[:, j, :]).then_inc(cb_lo, 1)
            for part in ("gate0", "conv_out", "sq", "sk", "sv"):
                ahead(U[part] + 3)
            ahead(U["xq"])
            for g in range(SB_HEADS + 4):
                if g < SB_HEADS:
                    h = g
                    if h >= 4:
                        wait_out(dve, "rc", h - 4)
                    b = wait_qfull(dve, "z", h)
                    nc.vector.scalar_tensor_tensor(out=zm[:, h % 4, :], in0=b[:, 0:384], scalar=SB_DIM ** -0.5,
                                                   in1=const("sb_mask"), op0=ALU.mult, op1=ALU.add)\
                        .then_inc(qout_sem("z", h), 1)
                    wait_qout(dve, "z", h)
                    nc.vector.scalar_tensor_tensor(out=lnb[:, h % 2, :], in0=zm[:, h % 4, :], scalar=-1.0,
                                                   in1=zm[:, h % 4, :], op0=ALU.mult, op1=ALU.max).then_inc(z_abs, 1)
                if 1 <= g <= SB_HEADS:
                    h = g - 1
                    dve.wait_ge(z_ln, h + 1)
                    if h >= 2:
                        wait_full(dve, "rc", h - 2)
                    nc.vector.scalar_tensor_tensor(out=spl[:, h % 2, :], in0=zm[:, h % 4, :], scalar=0.0,
                                                   in1=lnb[:, h % 2, :], op0=ALU.max, op1=ALU.add).then_inc(z_sp, 1)
                if 3 <= g < SB_HEADS + 3:
                    h = g - 3
                    b = wait_full(dve, "rc", h)
                    if h >= 2 and h % 2 == 0:
                        dve.wait_ge(first_head, HEADS + h // 2)
                    elif h >= 2:
                        wait_full(dve, "sbo", (h - 2) // 2)
                    nc.vector.tensor_tensor(att[:, h % 2, :], zm[:, h % 4, :], b[:, 0:384], ALU.subtract)\
                        .then_inc(out_sem("rc", h), 1)
                if g % 2 == 0 and g >= 6:
                    c = (g - 6) // 2
                    dve.wait_ge(o_hi, HEADS + c + 1)
                    b = wait_full(dve, "sbo", c)
                    lower(other_lo[:, c, :], b[:, 0:T], other_hi[:, c, :]).then_inc(out_sem("sbo", c), 1)
                if g - 2 in XQ_AT and XQ_AT[g - 2] % 2 == 1:
                    ahead(U["xq"] + XQ_AT[g - 2] // 2 + 1)
            ahead(U["sb_out"])
            dve.wait_ge(o_hi, HEADS + 8)
            b = wait_full(dve, "sbo", 7)
            lower(other_lo[:, 7, :], b[:, 0:T], other_hi[:, 7, :]).then_inc(out_sem("sbo", 7), 1)
            ahead(U["sb_out"] + 3)

            def head_scale(key, dst, which, g, h):
                wait_out(dve, key, h)
                link(nc.vector.reciprocal(x_rt[which][:, h, :], x_rt[which][:, h, :]))
                for c in range(2):
                    nc.vector.scalar_tensor_tensor(out=dst[:, 2 * h + c, :], in0=dst[:, 2 * h + c, :],
                                                   scalar=col(g, c), in1=x_rt[which][:, h, :],
                                                   op0=ALU.mult, op1=ALU.mult).then_inc(head_scaled, 1)

            for h in range(X_HEADS):
                head_scale("ssk", xk, 0, "kn_g", h)
                if h % 2 == 0:
                    ahead(U["gate1"] + h // 2)
            ahead(U["gate1"] + 2)
            for h in range(X_HEADS):
                head_scale("ssq", xq, 1, "qn_g", h)
                if h >= 1:
                    ahead(U["gate1"] + 2 + h)
            ahead(U["gate2"] + 1)

            def x_scale(h):
                wait_qout(dve, "XS", h)
                st = 8 * (h % 2) + 4
                link(nc.vector.reciprocal(stat[:, st:st + 2], stat[:, st:st + 2]))
                for t in range(TT):
                    p = x_p[:, h % 2, T * t:T * t + T]
                    ins = nc.vector.tensor_scalar(p, p, stat[:, st + t:st + t + 1], None, ALU.mult)
                ins.then_inc(x_probs, 1)

            def x_lower(h):
                dve.wait_ge(xo_hi, h + 1)
                b = wait_full(dve, "XO", h)
                lower(other_lo[:, 2 * h:2 * h + 2, :], chunks(b[:, :], 2), other_hi[:, 2 * h:2 * h + 2, :])\
                    .then_inc(out_sem("XO", h), 1)

            for g in range(X_HEADS + 2):
                if g < X_HEADS:
                    b, st = wait_qfull(dve, "XS", g), 8 * (g % 2)
                    link(nc.vector.reduce_max(stat[:, st:st + 2], chunks(b[:, :], 2), AX.X))
                    nc.vector.tensor_scalar(stat[:, st + 2:st + 4], stat[:, st:st + 2], -X_DIM ** -0.5, None, ALU.mult)\
                        .then_inc(x_negmax, 1)
                if 1 <= g <= X_HEADS:
                    x_scale(g - 1)
                    ahead(U["gate2"] + (3 + g) // 2)
                if g >= 2:
                    x_lower(g - 2)
            for j in range(KC + 1):
                if j < KC:
                    ahead(U["x_out"] + j // 2)
                    dve.wait_ge(merge_done, KC + j + 1)
                    if j >= 4:
                        dve.wait_ge(gate2_done, j - 3)
                    else:
                        wait_out(dve, "gate2", j)
                    b = wait_full(dve, "x_out", j)
                    nc.vector.tensor_tensor(buf_a[:, j, :], b[:, 0:T], buf_c[:, j, :], ALU.mult)\
                        .then_inc(out_sem("x_out", j), 1)
                    wait_out(dve, "x_out", j)
                    nc.vector.tensor_tensor(merged[:, j, :], merged[:, j, :], buf_a[:, j, :], ALU.add)\
                        .then_inc(x_merged, 1)
                if j >= 1:
                    dve.wait_ge(mg_hi, j)
                    lower(half_lo[:, j - 1, :], merged[:, j - 1, :], half_hi[:, j - 1, :]).then_inc(mg_lo, 1)
            for j in range(KC + 1):
                if j < KC:
                    ahead(U["out"] + j // 2)
                    b = wait_full(dve, "out", j)
                    nc.vector.tensor_tensor(x[:, j, :], b[:, 0:T], x[:, j, :], ALU.add).then_inc(out_sem("out", j), 1)
                    wait_out(dve, "out", j)
                    nc.vector.tensor_scalar(mlp_f[:, j, :], x[:, j, :], col("mlp_g", j), None, ALU.mult)\
                        .then_inc(scaled, 1)
                if j >= 1:
                    dve.wait_ge(part_hi, PART0["mlp"] + j)
                    lower(mlp_lo[:, j - 1, :], mlp_f[:, j - 1, :], mlp_hi[:, j - 1, :]).then_inc(part_lo, 1)
            wait_out(dve, "ss", "mlp")
            link(nc.vector.reciprocal(rt[:, 1, 0:T], rt[:, 1, 0:T]))

            def slab(i, last=False):
                for u in range(4):
                    for s in range(2):
                        f = 2 * u + s
                        if u < 2:
                            b = MLP_B + f
                            dve.wait_ge(r_full[b % 4], i + (b // 4 + 1))
                            nc.vector.scalar_tensor_tensor(out=gate_f[:, f, :], in0=R[b % 4][:, 0:T], scalar=0.0,
                                                           in1=rt[:, 1, 0:T], op0=ALU.max, op1=ALU.mult)\
                                .then_inc(gated, 1)
                            dve.wait_ge(gated, i * 4 + (4 * EXPERTS + f + 1))
                            nc.vector.scalar_tensor_tensor(out=hid_f[:, f, :], in0=R[b % 4][:, 0:T], scalar=0.0,
                                                           in1=gate_f[:, f, :], op0=ALU.max, op1=ALU.mult)\
                                .then_inc(r_out[b % 4], 1)
                        if s == 1 and not (last and u >= 2):
                            split_in_loop(i, 4, U["mlp"] + u + SPLIT)
                        if u < 2:
                            dve.wait_ge(hid_hi_s, i * 4 + (4 * EXPERTS + f + 1))
                            lower(hid_lo[:, f, :], hid_f[:, f, :], hid_hi[:, f, :]).then_inc(hid_lo_s, 1)

            ahead(U["mlp"])
            with dve.Fori(0, SLABS - 1) as i:
                slab(i)
            slab(SLABS - 1, last=True)
            for m in range(KC):
                dve.wait_ge(y_full, 4 + m // 2 + 1)
                nc.vector.tensor_tensor(x[:, m, :], Q[m // 2][:, T * (m % 2):T * (m % 2) + T], x[:, m, :], ALU.add)\
                    .then_inc(y_out, 1)

        @block.tensor
        def _(pe):
            mm = nc.tensor.matmul
            filled, q_filled = [0], [0]

            def open_block(*key):
                n = filled[0]
                assert R_AT[key] == n, (key, n)
                filled[0] += 1
                if n >= 4:
                    pe.wait_ge(r_out[n % 4], n // 4)
                return R[n % 4]

            def full_sem(*key):
                return r_full[R_AT[key] % 4]

            def open_q(*key):
                n = q_filled[0]
                assert Q_AT[key] == n, (key, n)
                q_filled[0] += 1
                if n >= 4:
                    pe.wait_ge(q_out[n % 4], n // 4)
                return Q[n % 4]

            def w_part(n, at, w=P):
                return w_hi[:, n % SPLIT, at:at + w], w_lo[:, n % SPLIT, at:at + w]

            def three(out, left, right, start, stop, group=True):
                (lh, ll), (rh, rl) = left, right
                mm(out, lh, rh, start=start, stop=False, skip_group_check=not group)
                mm(out, lh, rl, start=False, stop=False, skip_group_check=not group)
                return mm(out, ll, rh, start=False, stop=stop, skip_group_check=not group)

            def t_block(key, n, at, kc, hi, lo, w=T, ready=None):
                b = open_q(*key) if key in Q_AT else open_block(*key)
                for k in range(kc):
                    if ready is not None:
                        ready(k)
                    ins = three(b[:, 0:w], w_part(n, at + k * P), (hi[:, k, 0:w], lo[:, k, 0:w]), k == 0, k == kc - 1)
                ins.then_inc(q_full[Q_AT[key] % 4] if key in Q_AT else full_sem(*key), 1)

            def after_norm(name):
                return lambda k: pe.wait_ge(part_lo, PART0[name] + k + 1)

            def product(part, hi, lo, w=T, ready=None, blocks=range(KC)):
                for j in blocks:
                    n = U[part] + j // 2
                    if j % 2 == 0:
                        pe.wait_ge(lo_done, SPLITS[n])
                    t_block((part, j), n, (j % 2) * KC * P, KC, hi, lo, w, ready if j == 0 else None)

            def rows(part, hi, lo, units, tiles):
                for u in units:
                    n = U[part] + u
                    pe.wait_ge(lo_done, SPLITS[n])
                    for t in range(tiles):
                        b = open_block(part, u, t)
                        for k in range(KC):
                            c = slice(P * t, P * t + P)
                            ins = three(b[:, 0:T], (hi[:, k, c], lo[:, k, c]), w_part(n, k * T, T), k == 0, k == KC - 1)
                        ins.then_inc(full_sem(part, u, t), 1)

            def sum_squares(name):
                kc, w, _ = NORMS[name]
                b = open_block("ss", name)
                for k in range(kc):
                    pe.wait_ge(squared, CHUNK0[name] + k + 1)
                    ins = mm(b[:, 0:w], ones, norm_io(name)[0][:, k, :], start=(k == 0), stop=(k == kc - 1))
                ins.then_inc(full_sem("ss", name), 1)

            def mod_unit(u):
                n = U["mod"] + u if u < 8 else U["mod2"] + u - 8
                pe.wait_ge(raw_in[n % RAW], 16 * (n // RAW + 1))
                b = open_block("mod", u)
                for k in range(KC):
                    ins = mm(b[0:2, 0:T], cond_s[:, 2 * k:2 * k + 2], raw[:, n % RAW, k * T:k * T + T],
                             start=(k == 0), stop=(k == KC - 1))
                ins.then_inc(mod_filled, 1)

            def mod_turn(u):
                pe.wait_ge(mod_copied, u + 1)
                pe.wait_ge(consts_in, 16)
                b = r_bank("mod", u)
                for m in range(2):
                    ins = mm(b[:, T + 2 * m:T + 2 * m + 2], mod_rows[:, u % 2, P * m:P * m + P], ident[0:2, 0:2],
                             start=True, stop=True)
                ins.then_inc(full_sem("mod", u), 1)

            pe.wait_ge(cond_step, 1)
            for u in range(9):
                if u == 4:
                    sum_squares("ctx_x")
                if u < 8:
                    mod_unit(u)
                if u >= 1:
                    mod_turn(u - 1)
            for j in range(7):
                n = U["lat"] + j // 2
                if j % 2 == 0:
                    pe.wait_ge(lo_done, SPLITS[n])
                t_block(("lat", j), n, (j % 2) * KC * P, KC, h_hi, h_lo, T if j < 3 else 512,
                        after_norm("ctx_x") if j == 0 else None)
            product("naq", h_hi, h_lo, blocks=range(4))
            sum_squares("qa")
            sum_squares("kva")
            product("nak", h_hi, h_lo, w=512, blocks=range(4))
            rows("nav", h_hi, h_lo, range(2), 4)
            for j in range(8):
                n = U["uq"] + j // 4
                if j % 4 == 0:
                    pe.wait_ge(lo_done, SPLITS[n])
                t_block(("q", j), n, (j % 4) * QC * P, QC, qa_hi, qa_lo, ready=after_norm("qa") if j == 0 else None)
            n = U["ukv"]
            pe.wait_ge(lo_done, SPLITS[n])
            for j in range(4):
                t_block(("kn", j), n, j * KVC * P, KVC, kva_hi, kva_lo, 512, after_norm("kva") if j == 0 else None)
            for t in range(4):
                b = open_block("v", t)
                for k in range(KVC):
                    c = slice(P * t, P * t + P)
                    ins = three(b[:, :], (kva_hi[:, k, c], kva_lo[:, k, c]), w_part(n, 1024 + 512 * k, 512),
                                k == 0, k == KVC - 1)
                ins.then_inc(full_sem("v", t), 1)

            def scores(a):
                h, q = a // 2, slice(P * (a % 2), P * (a % 2) + P)
                b = open_q("S", a)
                if a < ATT_MLA:
                    n_, r_ = slice(64 * (h % 2), 64 * (h % 2) + 64), slice(32 * (h % 4), 32 * (h % 4) + 32)
                    mm(b[:, :], qn[n_, h // 2, q], kn[n_, h // 2, :], start=True, stop=False)
                    ins = mm(b[:, :], qr[r_, h // 4, q], kr[r_, :], start=False, stop=True)
                else:
                    h -= HEADS
                    n_ = slice(64 * (h % 2), 64 * (h % 2) + 64)
                    ins = mm(b[:, :], naq[n_, h // 2, q], nak[n_, h // 2, :], start=True, stop=True)
                ins.then_inc(q_full[Q_AT[("S", a)] % 4], 1)

            def weigh_values(h):
                v = vm if h < HEADS else nav
                b = open_block("O", h // 2) if h % 2 == 0 else r_bank("O", h // 2)
                wait_out(pe, "PT", 2 * h)
                wait_out(pe, "PT", 2 * h + 1)
                hv, ph = (h % HEADS) * VDIM, 64 * (h % 2)
                for kt in range(4):
                    ins = mm(b[ph:ph + 64, 0:T], v[:, kt, hv:hv + VDIM], probs_t[h % 2][:, kt, :],
                             start=(kt == 0), stop=(kt == 3))
                ins.then_inc(first_head if h % 2 == 0 else full_sem("O", h // 2), 1)

            for j in range(4):
                wait_out(pe, "q", j)
                wait_out(pe, "kn", j)
            for t in range(4):
                wait_out(pe, "v", t)
            pe.wait_ge(kr_ready, 1)
            pe.wait_ge(qr_ready, 2)
            for a in range(LEAD):
                scores(a)
            for a in range(ATT + 2):
                if a + LEAD < ATT:
                    scores(a + LEAD)
                if a < ATT:
                    pe.wait_ge(probs_ready, a + 1)
                    b = open_block("PT", a)
                    for kt in range(4):
                        ins = nc.tensor.transpose(b[:, P * kt:P * kt + P], probs(a)[:, P * kt:P * kt + P], ident)
                    ins.then_inc(full_sem("PT", a), 1)
                    if a % 2 == 0:
                        mod_unit(8 + a // 2)
                if a % 2 == 1 and a >= 3:
                    weigh_values((a - 3) // 2)
                if a % 2 == 1 and a < ATT:
                    mod_turn(8 + a // 2)

            def after_heads(k):
                wait_out(pe, "O", k)

            product("wout", half_hi, half_lo, ready=after_heads, blocks=range(4))
            sum_squares("mem")
            product("wout", half_hi, half_lo, blocks=range(4, 8))
            product("mk", mem_hi, mem_lo, ready=after_norm("mem"), blocks=range(2))
            sum_squares("ffn")
            product("mk", mem_hi, mem_lo, blocks=range(2, 4))
            pe.wait_ge(router_split, 1)
            b = open_block("logits")
            for k in range(KC):
                after_norm("ffn")(k)
                ins = three(b[0:20, 0:T], (wr_hi[:, 20 * k:20 * k + 20], wr_lo[:, 20 * k:20 * k + 20]),
                            (half_hi[:, k, :], half_lo[:, k, :]), k == 0, k == KC - 1)
            ins.then_inc(logits_filled, 1)
            product("mk", mem_hi, mem_lo, blocks=range(4, 5))
            pe.wait_ge(logits_copied, 1)
            for t in range(TT):
                ins = mm(b[:, T + 20 * t:T + 20 * t + 20], turn_rows[:, 0, P * t:P * t + P], ident[0:20, 0:20],
                         start=True, stop=True)
            ins.then_inc(full_sem("logits"), 1)
            product("mk", mem_hi, mem_lo, blocks=range(5, 8))
            pe.wait_ge(comb_ready, 1)
            for j in range(EXPERTS // 2):
                b = open_block("comb", j)
                for e in range(2):
                    for t in range(TT):
                        weight = route[:, t, 80 + 2 * j + e:81 + 2 * j + e].to_broadcast([P, P])
                        ins = mm(b[:, T * e + P * t:T * e + P * t + P], weight, ident, start=True, stop=True)
                ins.then_inc(full_sem("comb", j), 1)

            def clear_y():
                for m in range(4):
                    mm(Q[m][:, :], ident, zero.to_broadcast([P, 512]), start=True, stop=False, skip_group_check=True)

            def close_y():
                for m in range(4):
                    mm(Q[m][:, :], ident, zero.to_broadcast([P, 512]), start=False, stop=True, skip_group_check=True)\
                        .then_inc(y_full, 1)

            def hidden_unit(n, u, i, units, blocks, b0, hi, lo):
                pe.wait_ge(lo_done, i * units + SPLITS[n])
                for s in range(2):
                    b = b0 + s
                    pe.wait_ge(r_out[b % 4], i * (blocks // 4) + b // 4)
                    for k in range(KC):
                        ins = three(R[b % 4][:, 0:T], w_part(n, (s * KC + k) * P), (hi[:, k, :], lo[:, k, :]),
                                    k == 0, k == KC - 1)
                    ins.then_inc(r_full[b % 4], 1)

            def down_unit(n, u, i, units, hid, h0):
                pe.wait_ge(lo_done, i * units + SPLITS[n])
                for c in range(2):
                    f = 2 * u + c
                    pe.wait_ge(hid_lo_s, i * hid + (h0 + f + 1))
                    for m in range(KC):
                        ins = three(Q[m // 2][:, T * (m % 2):T * (m % 2) + T], w_part(n, (c * KC + m) * P),
                                    (hid_hi[:, f, :], hid_lo[:, f, :]), False, False, group=False)
                ins.then_inc(down_used, 1)

            wait_qout(pe, "mk", 7)
            clear_y()
            with pe.Fori(0, EXPERTS // 2) as i:
                for e in range(2):
                    n = U["moe"] + 6 * e
                    for u in range(4):
                        hidden_unit(n + u, u, i, 12, 16, MOE_B + 8 * e + 2 * u, half_hi, half_lo)
                    for u in range(2):
                        down_unit(n + 4 + u, u, i, 12, 8, 4 * e)
            filled[0] += 8 * EXPERTS
            close_y()
            rows("mv", mem_hi, mem_lo, [0], TT)
            sum_squares("final")
            rows("mv", mem_hi, mem_lo, [1, 2], TT)
            sum_squares("mix")
            rows("mv", mem_hi, mem_lo, [3], TT)
            product("c_h", half_hi, half_lo, ready=after_norm("mix"))
            product("c_c", half_hi, half_lo)
            product("c_b", half_hi, half_lo)
            product("gate0", half_hi, half_lo)
            product("conv_out", other_hi, other_lo, ready=lambda k: pe.wait_ge(cb_lo, k + 1))
            for part in ("sq", "sk"):
                product(part, half_hi, half_lo)
            rows("sv", half_hi, half_lo, range(4), TT)

            def z_scores(h):
                ph, c = slice(64 * (h % 2), 64 * (h % 2) + 64), h // 2
                b = open_q("z", h)
                mm(b[:, 0:256], buf_b[ph, c, 0:P], buf_a[ph, c, :], start=True, stop=True)
                mm(b[:, 256:384], buf_b[ph, c, P:T], buf_a[ph, c, P:T], start=True, stop=True)\
                    .then_inc(q_full[Q_AT[("z", h)] % 4], 1)

            def later_keys(h):
                pe.wait_ge(z_sp, h + 1)
                b, s = open_block("rc", h), spl[:, h % 2, :]
                mm(b[:, 0:128], tri, s[:, 0:128], start=True, stop=True)
                mm(b[:, 128:256], tri, s[:, 128:256], start=True, stop=False)
                mm(b[:, 128:256], ones, s[:, 256:384], start=False, stop=True)
                mm(b[:, 256:384], tri, s[:, 256:384], start=True, stop=True)\
                    .then_inc(full_sem("rc", h), 1)

            def sb_values(h):
                pe.wait_ge(z_exp, h + 1)
                b = open_block("sbo", h // 2) if h % 2 == 0 else r_bank("sbo", h // 2)
                ph, hv = slice(64 * (h % 2), 64 * (h % 2) + 64), slice(SB_DIM * h, SB_DIM * h + SB_DIM)
                mm(b[ph, 0:128], sb_v[:, 0, hv], att[:, h % 2, 0:128], start=True, stop=True)
                mm(b[ph, 128:256], sb_v[:, 0, hv], att[:, h % 2, 128:256], start=True, stop=False)
                mm(b[ph, 128:256], sb_v[:, 1, hv], att[:, h % 2, 256:384], start=False, stop=True)\
                    .then_inc(first_head if h % 2 == 0 else full_sem("sbo", h // 2), 1)

            for j in range(KC):
                wait_out(pe, "sq", j)
                wait_out(pe, "sk", j)
                wait_out(pe, "sv", j // 2, j % 2)
            z_scores(0)
            for g in range(SB_HEADS + 4):
                if g + 1 < SB_HEADS:
                    z_scores(g + 1)
                if g in XQ_AT:
                    product("xq", half_hi, half_lo, blocks=[XQ_AT[g]])
                if 2 <= g <= SB_HEADS + 1:
                    later_keys(g - 2)
                if g >= 4:
                    sb_values(g - 4)

            def head_squares(key, before, h):
                pe.wait_ge(head_sq, before + 2 * h + 2)
                b = open_block(key, h)
                for c in range(2):
                    ins = mm(b[:, 0:T], ones, x_sq[:, 2 * h + c, :], start=(c == 0), stop=(c == 1))
                ins.then_inc(full_sem(key, h), 1)

            for j in range(KC):
                product("sb_out", other_hi, other_lo, ready=(lambda k: wait_out(pe, "sbo", k)) if j == 0 else None,
                        blocks=[j])
                if j >= 4:
                    head_squares("ssk", 0, j - 4)
            product("gate1", half_hi, half_lo, blocks=range(4))
            for h in range(X_HEADS):
                head_squares("ssq", KC, h)
            product("gate1", half_hi, half_lo, blocks=range(4, 8))
            product("gate2", half_hi, half_lo, blocks=range(4))

            def x_scores(h):
                b = open_q("XS", h)
                for t in range(TT):
                    for c in range(2):
                        ins = mm(b[:, T * t:T * t + T], xq[:, 2 * h + c, P * t:P * t + P], xk[:, 2 * h + c, :],
                                 start=(c == 0), stop=(c == 1))
                ins.then_inc(q_full[Q_AT[("XS", h)] % 4], 1)

            for u in range(4):
                for t in range(TT):
                    wait_out(pe, "mv", u, t)
            pe.wait_ge(head_scaled, 2 * KC)
            x_scores(0)
            x_scores(1)
            for g in range(X_HEADS + 1):
                if g < X_HEADS:
                    product("gate2", half_hi, half_lo, blocks=[4 + g])
                    pe.wait_ge(x_probs, g + 1)
                    b = open_block("XP", g)
                    for kt in range(TT):
                        for t in range(TT):
                            ins = nc.tensor.transpose(b[:, T * kt + P * t:T * kt + P * t + P],
                                                      x_p[:, g % 2, T * t + P * kt:T * t + P * kt + P], ident)
                    ins.then_inc(full_sem("XP", g), 1)
                if g + 2 < X_HEADS:
                    x_scores(g + 2)
                if g >= 1:
                    h = g - 1
                    wait_out(pe, "XP", h)
                    b = open_block("XO", h)
                    for c in range(2):
                        for kt in range(TT):
                            at = X_DIM * h + P * c
                            ins = mm(b[:, T * c:T * c + T], x_v[:, kt, at:at + P], x_pt[:, h % 2, T * kt:T * kt + T],
                                     start=(kt == 0), stop=(kt == 1))
                    ins.then_inc(full_sem("XO", h), 1)
            product("x_out", other_hi, other_lo, ready=lambda k: wait_out(pe, "XO", k // 2))
            product("out", half_hi, half_lo, ready=lambda k: pe.wait_ge(mg_lo, k + 1))
            sum_squares("mlp")
            clear_y()
            for k in range(KC):
                after_norm("mlp")(k)
            with pe.Fori(0, SLABS) as i:
                for u in range(2):
                    hidden_unit(U["mlp"] + u, u, i, 4, 4, MLP_B + 2 * u, mlp_hi, mlp_lo)
                for u in range(2):
                    down_unit(U["mlp"] + 2 + u, u, i, 4, 4, 4 * EXPERTS)
            close_y()


def constants():
    out = np.zeros((P, N_CONST), np.float32)
    out[:, CONST["ident"]] = np.eye(P, dtype=np.float32)
    out[:, CONST["ones"]] = 1.0
    i = np.arange(P)
    out[:, CONST["tri"]] = i[:, None] >= i[None, :]
    pos = np.arange(T)
    half = ROPE // 2
    inv = (np.float32(10000.0) ** (-np.arange(0, half, 2, dtype=np.float32) / np.float32(half))).astype(np.float32)
    ang = np.concatenate([(pos // GRID_W).astype(np.float32)[:, None] * inv,
                          (pos % GRID_W).astype(np.float32)[:, None] * inv], axis=1)
    at = i % half
    sign = np.where(i % ROPE < half, -1.0, 1.0).astype(np.float32)
    cos, sin = np.ones((P, 512), np.float32), np.zeros((P, 512), np.float32)
    cos[:, 0:T] = np.cos(ang).astype(np.float32).T[at]
    sin[:, 0:T] = sign[:, None] * np.sin(ang).astype(np.float32).T[at]
    out[:, CONST["cos"]], out[:, CONST["sin"]] = cos, sin
    diag = np.where(i[:, None] < i[None, :], 0.0, MASKED)
    out[:, CONST["sb_mask"]] = np.concatenate([diag, np.zeros((P, P)), diag], axis=1)
    c = np.arange(GRID_W)
    start = np.clip(c - NA_WIN_W // 2, 0, GRID_W - NA_WIN_W)
    inside = (c[None, :] >= start[:, None]) & (c[None, :] < start[:, None] + NA_WIN_W)
    inside = np.tile(inside, (2, 4)).astype(np.float32)
    out[:, CONST["win"]] = inside
    out[:, CONST["win_neg"]] = np.where(inside > 0, 0.0, MASKED)
    out[:, CONST["prio"]] = np.arange(4, 0, -1)
    out[:, CONST["eps"]] = EPS
    return out


def in_blocks(w, per_unit=2):
    k, n = w.shape
    b = w.reshape(k // P, P, n // P, P).transpose(2, 1, 0, 3).reshape(n // P, P, k)
    units = -(-len(b) // per_unit)
    out = np.zeros((units, P, UNIT), w.dtype)
    for j in range(len(b)):
        u, s = divmod(j, per_unit)
        out[u, :, s * k:(s + 1) * k] = b[j]
    return out


def in_rows(w):
    k, n = w.shape
    return w.reshape(k // P, P, n // T, T).transpose(2, 1, 0, 3).reshape(n // T, P, UNIT)


def in_down(w):
    k, n = w.shape
    return w.reshape(k // (2 * P), 2, P, n).transpose(0, 2, 1, 3).reshape(k // (2 * P), P, UNIT)


def by_feature(v):
    return v.reshape(-1, P).T


def kernel(**inputs):
    import concourse.bacc as bacc
    from concourse.bass_utils import run_bass_kernel_spmd

    a = {k: np.asarray(v) for k, v in inputs.items()}
    f32 = a["x"].dtype
    w_in, w2, w_uq, w_ukv = a["w_in"][0], a["w_in_2"][0], a["w_uq"][0], a["w_ukv"][0]
    half = ROPE // 2
    swapped = np.concatenate([np.arange(half, ROPE), np.arange(half)])
    q_cols = Q_LORA + NA_HEADS * NA_DIM
    k_rope = w_in[:, q_cols + KV_LORA:q_cols + KV_LORA + ROPE]
    na_k0 = q_cols + KV_LORA + ROPE
    na_w = NA_HEADS * NA_DIM
    uq = w_uq.reshape(Q_LORA, HEADS, NOPE + ROPE)
    ukv = w_ukv.reshape(KV_LORA, HEADS, NOPE + VDIM)
    wm = in_rows(a["w_mod"][0])

    def cut(n):
        return w2[:, n * D:(n + 1) * D]

    kn_v = np.concatenate([
        in_blocks(ukv[:, :, :NOPE].reshape(KV_LORA, -1), 4)[0][:, 0:1024],
        ukv[:, :, NOPE:].reshape(KVC, P, HEADS * VDIM).transpose(1, 0, 2).reshape(P, 1024)], axis=1)[None]
    experts = []
    for e in range(EXPERTS):
        experts += [in_blocks(a["w_gate"][0, e]), in_blocks(a["w_up"][0, e]), in_down(a["w_down"][0, e])]
    slabs = []
    for s in range(SLABS):
        c = slice(s * D_EXPERT, (s + 1) * D_EXPERT)
        slabs += [in_blocks(a["w_up_2"][0][:, c]), in_down(a["w_down_2"][0][c, :])]
    weights = np.concatenate([
        wm[4:8], wm[:4],
        in_blocks(np.concatenate([w_in[:, :Q_LORA], w_in[:, q_cols:q_cols + KV_LORA], np.tile(k_rope, (1, 4)),
                                  np.tile(k_rope[:, swapped], (1, 4))], axis=1)),
        in_blocks(w_in[:, Q_LORA:q_cols]), in_blocks(w_in[:, na_k0:na_k0 + na_w]), in_rows(w_in[:, na_k0 + na_w:]),
        in_blocks(np.concatenate([uq[:, :, :NOPE].reshape(Q_LORA, -1), uq[:, :, NOPE:].reshape(Q_LORA, -1),
                                  uq[:, :, NOPE:][:, :, swapped].reshape(Q_LORA, -1)], axis=1), 4),
        kn_v, wm[8:], in_blocks(a["w_out"][0]), in_blocks(a["w_mem_kv_2"][0][:, :D]), *experts,
        in_rows(a["w_mem_kv_2"][0][:, D:]),
        in_blocks(cut(0)), in_blocks(cut(2)), in_blocks(cut(1)), in_blocks(cut(7)), in_blocks(a["w_conv_out_2"][0]),
        in_blocks(cut(3)), in_blocks(cut(4)), in_rows(cut(5)), in_blocks(cut(6)), in_blocks(a["w_sb_out_2"][0]),
        in_blocks(cut(8)), in_blocks(cut(9)), in_blocks(a["w_x_out_2"][0]), in_blocks(a["w_out_2"][0]), *slabs])
    assert weights.shape == (UNITS, P, UNIT)
    tokens = np.stack([v[0].T.reshape(KC, P, T).transpose(1, 0, 2) for v in (a["x"], a["ctx"], a["mem_2"])])
    cond = np.stack([by_feature(a["c"][0]), by_feature(a["c_ctx"])], axis=2).reshape(P, 16)
    router = np.concatenate([a["w_router_group"][0], a["w_router_expert"][0]], axis=1)
    b_router = np.concatenate([a["b_router_group"][0], a["b_router_expert"][0]])
    cols = np.concatenate(
        [by_feature(a[n].reshape(-1)) for n in ("norm_attn_g", "norm_ffn_g", "final_norm_g", "g_mix_2", "g_mem_2",
                                                "g_mlp_2", "q_a_norm_g", "kv_a_norm_g", "q_norm_g_2", "k_norm_g_2")]
        + [by_feature(a["conv_w_2"][0, tap]) for tap in range(3)]
        + [by_feature(a["b_mod"][0]), cond, router.reshape(KC, P, 20).transpose(1, 0, 2).reshape(P, 160),
           np.tile(b_router, (P, 1))], axis=1)
    c = np.arange(GRID_W)
    across = np.clip(c[None, :] - c[:, None] + NA_WIN_W - 1, 0, 2 * NA_WIN_W - 2)
    rows = T // GRID_W
    down = np.arange(rows)[None, :] - np.arange(rows)[:, None] + NA_WIN_H - 1
    bias = a["na_rel_bias"][0][:, down[:, None, :, None], across[None, :, None, :]]
    bias = bias.transpose(1, 2, 0, 3, 4).reshape(rows, GRID_W, NA_HEADS, T)
    arrays = {"weights": weights, "tokens": tokens, "cols": cols, "constants": constants(), "bias": bias}
    arrays = {f"in_{n}": np.ascontiguousarray(v) for n, v in arrays.items()}
    nc = bacc.Bacc("TRN2", target_bir_lowering=False, num_devices=1)
    args = [nc.dram_tensor(n, v.shape, mybir.dt.from_np(v.dtype), kind="ExternalInput").ap() for n, v in arrays.items()]
    out = nc.dram_tensor("out_features", (P, KC, T), mybir.dt.float32, kind="ExternalOutput").ap()
    build_program(nc, *args, out)
    r = run_bass_kernel_spmd(nc, [arrays], core_ids=[0])
    y = r.results[0]["out_features"]
    return y.transpose(1, 0, 2).reshape(D, T).T[None]
```
